# Optimizing a Trainium2 kernel written in Bass

```python
import math
import jax, jax.numpy as jnp
from jax import lax
import numpy as np

D_MODEL = 1024
BATCH = 1
SEQ = 512
DEPTH = 2

HEAD_DIM = 64
ROPE_THETA = 10000.0
EPS = 1e-6
N_MIXERS = 2
DIL_GROUPS = ((128, 1), (512, 4), (2048, 16))
N_DIL_GROUPS = len(DIL_GROUPS)
DIL_HEADS = D_MODEL // HEAD_DIM
DIL_WIDTH = DIL_HEADS * HEAD_DIM
DIL_IN = 3 * N_DIL_GROUPS * DIL_WIDTH + DIL_WIDTH
DIFF_HEADS = D_MODEL // HEAD_DIM // 2
DIFF_QK_DIM = HEAD_DIM
DIFF_V_DIM = 2 * HEAD_DIM
DIFF_WIDTH = DIFF_HEADS * DIFF_V_DIM
DIFF_QK_WIDTH = 2 * DIFF_HEADS * DIFF_QK_DIM
DIFF_IN = 2 * DIFF_QK_WIDTH + 2 * DIFF_WIDTH
Q_BLOCK = 128
N_DIL_LAYERS = (DEPTH + 1) // 2
N_DIFF_LAYERS = DEPTH // 2


def rmsnorm(x, g):
    x32 = x.astype(jnp.float32)
    y = x32 * lax.rsqrt(jnp.mean(x32 * x32, axis=-1, keepdims=True) + EPS)
    return y.astype(x.dtype) * g

def rope(x, pos):
    dh = x.shape[-1]
    freqs = ROPE_THETA ** (-jnp.arange(0, dh, 2, dtype=jnp.float32) / dh)
    ang = pos.astype(jnp.float32)[:, None] * freqs[None, :]
    cos = jnp.cos(ang)[None, :, None, :].astype(x.dtype)
    sin = jnp.sin(ang)[None, :, None, :].astype(x.dtype)
    x1, x2 = x[..., : dh // 2], x[..., dh // 2:]
    return jnp.concatenate([x1 * cos - x2 * sin, x2 * cos + x1 * sin], axis=-1)

def dilated_window_attention(q, k, v, window, dilation):
    B, S, H, Dh = q.shape
    w = window // dilation
    L = S // dilation
    nb = -(-L // w)
    Lp = nb * w

    def to_sub(t):
        t = t.reshape(B, L, dilation, H, Dh).transpose(0, 2, 1, 3, 4)
        t = jnp.pad(t, ((0, 0), (0, 0), (0, Lp - L), (0, 0), (0, 0)))
        return t.reshape(B, dilation, nb, w, H, Dh)

    qs, ks, vs = to_sub(q), to_sub(k), to_sub(v)

    def with_prev(t):
        prev = jnp.pad(t, ((0, 0), (0, 0), (1, 0), (0, 0), (0, 0), (0, 0)))[:, :, :-1]
        return jnp.concatenate([prev, t], axis=3)

    kb, vb = with_prev(ks), with_prev(vs)
    scores = jnp.einsum('brnqhd,brnkhd->brnhqk', qs, kb).astype(jnp.float32) * (Dh ** -0.5)
    qi = jnp.arange(w)[:, None]
    kj = jnp.arange(2 * w)[None, :]
    dist = w + qi - kj
    kpos = jnp.arange(nb)[:, None, None] * w + kj[None] - w
    mask = (dist >= 0)[None] & (dist <= w)[None] & (kpos >= 0)
    scores = jnp.where(mask[None, None, :, None], scores, -jnp.inf)
    m = jnp.max(scores, axis=-1, keepdims=True)
    p = jnp.exp(scores - m)
    den = jnp.sum(p, axis=-1)
    out = jnp.einsum('brnhqk,brnkhd->brnhqd', p.astype(v.dtype), vb).astype(jnp.float32)
    out = out / den[..., None]
    lse = m[..., 0] + jnp.log(den)
    out = out.transpose(0, 1, 2, 4, 3, 5).reshape(B, dilation, Lp, H, Dh)[:, :, :L]
    out = out.transpose(0, 2, 1, 3, 4).reshape(B, S, H, Dh)
    lse = lse.transpose(0, 1, 2, 4, 3).reshape(B, dilation, Lp, H)[:, :, :L]
    lse = lse.transpose(0, 2, 1, 3).reshape(B, S, H)
    return out, lse

def dilated_mixer(h, w_in, w_out):
    B, S, _ = h.shape
    pos = jnp.arange(S)
    proj = h @ w_in
    n_qkv = 3 * N_DIL_GROUPS * DIL_WIDTH
    qkv = proj[..., :n_qkv].reshape(B, S, 3, N_DIL_GROUPS * DIL_HEADS, HEAD_DIM)
    gate = proj[..., n_qkv:]
    q = rope(qkv[:, :, 0], pos)
    k = rope(qkv[:, :, 1], pos)
    v = qkv[:, :, 2]
    outs, lses = [], []
    for g, (window, dil) in enumerate(DIL_GROUPS):
        sl = slice(g * DIL_HEADS, (g + 1) * DIL_HEADS)
        o, lse = dilated_window_attention(q[:, :, sl], k[:, :, sl], v[:, :, sl], window, dil)
        outs.append(o)
        lses.append(lse)
    alpha = jax.nn.softmax(jnp.stack(lses, axis=0), axis=0)
    o = jnp.sum(alpha[..., None] * jnp.stack(outs, axis=0), axis=0)
    y = o.reshape(B, S, DIL_WIDTH).astype(h.dtype) * jax.nn.silu(gate)
    return y @ w_out

def diff_mixer(h, w_in, lq1, lk1, lq2, lk2, subln, w_out, lambda_init):
    B, S, _ = h.shape
    pos = jnp.arange(S)
    proj = h @ w_in
    q = proj[..., :DIFF_QK_WIDTH].reshape(B, S, 2 * DIFF_HEADS, DIFF_QK_DIM)
    k = proj[..., DIFF_QK_WIDTH:2 * DIFF_QK_WIDTH].reshape(B, S, 2 * DIFF_HEADS, DIFF_QK_DIM)
    v = proj[..., 2 * DIFF_QK_WIDTH:2 * DIFF_QK_WIDTH + DIFF_WIDTH].reshape(B, S, DIFF_HEADS, DIFF_V_DIM)
    gate = proj[..., 2 * DIFF_QK_WIDTH + DIFF_WIDTH:]
    q = rope(q, pos).reshape(B, S, DIFF_HEADS, 2, DIFF_QK_DIM)
    k = rope(k, pos).reshape(B, S, DIFF_HEADS, 2, DIFF_QK_DIM)
    lam = (jnp.exp(jnp.sum(lq1.astype(jnp.float32) * lk1.astype(jnp.float32)))
           - jnp.exp(jnp.sum(lq2.astype(jnp.float32) * lk2.astype(jnp.float32))) + lambda_init)
    n_qb = S // Q_BLOCK
    qb = q.reshape(B, n_qb, Q_BLOCK, DIFF_HEADS, 2, DIFF_QK_DIM).transpose(1, 0, 2, 3, 4, 5)
    scale = DIFF_QK_DIM ** -0.5
    kpos = jnp.arange(S)

    def block(args):
        qblk, bi = args
        s = jnp.einsum('bqhcd,bkhcd->bchqk', qblk, k).astype(jnp.float32) * scale
        qpos = bi * Q_BLOCK + jnp.arange(Q_BLOCK)
        s = jnp.where(kpos[None, :] <= qpos[:, None], s, -jnp.inf)
        p = jax.nn.softmax(s, axis=-1)
        a = p[:, 0] - lam * p[:, 1]
        return jnp.einsum('bhqk,bkhd->bqhd', a.astype(v.dtype), v)

    o = lax.map(block, (qb, jnp.arange(n_qb)))
    o = o.transpose(1, 0, 2, 3, 4).reshape(B, S, DIFF_HEADS, DIFF_V_DIM)
    o = rmsnorm(o, subln) * (1.0 - lambda_init)
    y = o.reshape(B, S, DIFF_WIDTH) * jax.nn.silu(gate)
    return y @ w_out

def first_inputs(seed: int = 0) -> dict:
    key = jax.random.key(seed)
    ks = jax.random.split(key, 12)
    f32 = jnp.float32
    x = jax.random.normal(ks[0], (BATCH, SEQ, D_MODEL), f32)
    norm_pre = 1.0 + 0.05 * jax.random.normal(ks[1], (DEPTH, D_MODEL), f32)
    norm_post = 1.0 + 0.05 * jax.random.normal(ks[2], (DEPTH, D_MODEL), f32)
    dil_w_in = jax.random.normal(ks[3], (N_DIL_LAYERS, D_MODEL, DIL_IN), f32) * D_MODEL ** -0.5
    dil_w_out = jax.random.normal(ks[4], (N_DIL_LAYERS, DIL_WIDTH, D_MODEL), f32) * DIL_WIDTH ** -0.5
    diff_w_in = jax.random.normal(ks[5], (N_DIFF_LAYERS, D_MODEL, DIFF_IN), f32) * D_MODEL ** -0.5
    diff_w_out = jax.random.normal(ks[6], (N_DIFF_LAYERS, DIFF_WIDTH, D_MODEL), f32) * DIFF_WIDTH ** -0.5
    diff_lambda_q1 = 0.1 * jax.random.normal(ks[7], (N_DIFF_LAYERS, DIFF_QK_DIM), f32)
    diff_lambda_k1 = 0.1 * jax.random.normal(ks[8], (N_DIFF_LAYERS, DIFF_QK_DIM), f32)
    diff_lambda_q2 = 0.1 * jax.random.normal(ks[9], (N_DIFF_LAYERS, DIFF_QK_DIM), f32)
    diff_lambda_k2 = 0.1 * jax.random.normal(ks[10], (N_DIFF_LAYERS, DIFF_QK_DIM), f32)
    diff_subln = 1.0 + 0.05 * jax.random.normal(ks[11], (N_DIFF_LAYERS, DIFF_V_DIM), f32)
    return {"x": x, "norm_pre": norm_pre, "norm_post": norm_post,
            "dil_w_in": dil_w_in, "dil_w_out": dil_w_out,
            "diff_w_in": diff_w_in, "diff_w_out": diff_w_out,
            "diff_lambda_q1": diff_lambda_q1, "diff_lambda_k1": diff_lambda_k1,
            "diff_lambda_q2": diff_lambda_q2, "diff_lambda_k2": diff_lambda_k2,
            "diff_subln": diff_subln}

def first_block(x, norm_pre, norm_post, dil_w_in, dil_w_out, diff_w_in, diff_w_out,
              diff_lambda_q1, diff_lambda_k1, diff_lambda_q2, diff_lambda_k2, diff_subln):
    h = x
    for i in range(DEPTH):
        u = rmsnorm(h, norm_pre[i])
        j = i // N_MIXERS
        if i % N_MIXERS == 0:
            y = dilated_mixer(u, dil_w_in[j], dil_w_out[j])
        else:
            lambda_init = 0.8 - 0.6 * math.exp(-0.3 * i)
            y = diff_mixer(u, diff_w_in[j], diff_lambda_q1[j], diff_lambda_k1[j],
                           diff_lambda_q2[j], diff_lambda_k2[j], diff_subln[j],
                           diff_w_out[j], lambda_init)
        h = h + rmsnorm(y, norm_post[i])
    return h


DEPTH_2 = 1

CHUNK = 64
A_HEADS = 8
A_HEAD_DIM = 64
A_WIDTH = A_HEADS * A_HEAD_DIM
IDX_HEADS = 4
IDX_DIM = 64
TOPK_MAX = 256
REL_BUCKETS = 32
REL_MAX_DIST = 128
SSM_GROUPS = 16
SSM_GROUP_CH = 16
SSM_WIDTH = SSM_GROUPS * SSM_GROUP_CH
SSM_STATE = 64
DT_MIN = 0.001
DT_MAX = 0.1
MEM_TOKENS = 256
MEM_HEADS = 4
MEM_HEAD_DIM = 64
MEM_WIDTH = MEM_HEADS * MEM_HEAD_DIM
N_BRANCHES = 3
FFN_DIM = 2816
NORM_EPS = 1e-6
IN_SPLITS = (A_WIDTH, A_HEAD_DIM, A_HEAD_DIM, IDX_HEADS * IDX_DIM, IDX_DIM, IDX_HEADS,
             SSM_WIDTH, MEM_WIDTH, N_BRANCHES * D_MODEL)
W_IN_COLS = (A_WIDTH + 2 * A_HEAD_DIM + IDX_HEADS * IDX_DIM + IDX_DIM + IDX_HEADS
             + SSM_WIDTH + MEM_WIDTH + N_BRANCHES * D_MODEL)


def rms_norm(x, g):
    xf = x.astype(jnp.float32)
    y = xf * lax.rsqrt(jnp.mean(xf * xf, axis=-1, keepdims=True) + NORM_EPS)
    return (y * g.astype(jnp.float32)).astype(x.dtype)

def swiglu_ffn(h, w_in, w_out):
    gate, up = jnp.split(h @ w_in, 2, axis=-1)
    return (jax.nn.silu(gate) * up) @ w_out

def t5_bucket(rel):
    half = REL_BUCKETS // 2
    max_exact = half // 2
    n = jnp.abs(rel)
    nf = jnp.maximum(n, 1).astype(jnp.float32)
    large = max_exact + (jnp.log(nf / max_exact) / math.log(REL_MAX_DIST / max_exact)
                         * (half - max_exact)).astype(jnp.int32)
    large = jnp.minimum(large, half - 1)
    return jnp.where(rel > 0, half, 0) + jnp.where(n < max_exact, n, large)

def indexed_sparse_attention(q, k, v, q_idx, k_idx, w_idx, rel_bias):
    b_, s_ = q.shape[0], q.shape[1]
    topk = min(TOPK_MAX, s_ // 4)
    nblk = s_ // Q_BLOCK
    key_pos = jnp.arange(s_, dtype=jnp.int32)
    scale = A_HEAD_DIM ** -0.5
    idx_scale = IDX_DIM ** -0.5
    head_w_scale = IDX_HEADS ** -0.5

    def to_blocks(a):
        return a.reshape((b_, nblk, Q_BLOCK) + a.shape[2:]).swapaxes(0, 1)

    def block(args):
        qb, qib, wb, start = args
        t = start + jnp.arange(Q_BLOCK, dtype=jnp.int32)
        limit = (t // CHUNK + 1) * CHUNK
        rel = jax.nn.relu(jnp.einsum('bqhd,bsd->bqhs', qib, k_idx).astype(jnp.float32) * idx_scale)
        score = jnp.einsum('bqhs,bqh->bqs', rel, wb.astype(jnp.float32) * head_w_scale)
        score = jnp.where(key_pos[None, None, :] < limit[None, :, None], score, -jnp.inf)
        _, sel = lax.top_k(score, topk)
        valid = sel < limit[None, :, None]
        flat = sel.reshape(b_, Q_BLOCK * topk, 1)
        k_sel = jnp.take_along_axis(k, flat, axis=1).reshape(b_, Q_BLOCK, topk, A_HEAD_DIM)
        v_sel = jnp.take_along_axis(v, flat, axis=1).reshape(b_, Q_BLOCK, topk, A_HEAD_DIM)
        bias = rel_bias[t5_bucket(sel - t[None, :, None])]
        logits = (jnp.einsum('bqhd,bqkd->bqhk', qb, k_sel).astype(jnp.float32) * scale
                  + jnp.transpose(bias, (0, 1, 3, 2)).astype(jnp.float32))
        logits = jnp.where(valid[:, :, None, :], logits, -jnp.inf)
        p = jax.nn.softmax(logits, axis=-1).astype(v_sel.dtype)
        return jnp.einsum('bqhk,bqkd->bqhd', p, v_sel)

    starts = jnp.arange(nblk, dtype=jnp.int32) * Q_BLOCK
    out = lax.map(block, (to_blocks(q), to_blocks(q_idx), to_blocks(w_idx), starts))
    return out.swapaxes(0, 1).reshape(b_, s_, A_WIDTH)

def _complex_affine_combine(e1, e2):
    a1r, a1i, b1r, b1i = e1
    a2r, a2i, b2r, b2i = e2
    return (a2r * a1r - a2i * a1i,
            a2r * a1i + a2i * a1r,
            a2r * b1r - a2i * b1i + b2r,
            a2r * b1i + a2i * b1r + b2i)

def s5_layer(u, lam_re, lam_im, log_dt, b_re, b_im, c_re, c_im, d):
    b_, s_ = u.shape[0], u.shape[1]
    f32 = jnp.float32
    uf = u.astype(f32).reshape(b_, s_, SSM_GROUPS, SSM_GROUP_CH)
    lr, li = lam_re.astype(f32), lam_im.astype(f32)
    dt = jnp.exp(log_dt.astype(f32))[:, None]
    mag = jnp.exp(lr * dt)
    ar, ai = mag * jnp.cos(li * dt), mag * jnp.sin(li * dt)
    den = lr * lr + li * li
    fr = ((ar - 1.0) * lr + ai * li) / den
    fi = (ai * lr - (ar - 1.0) * li) / den
    br, bi = b_re.astype(f32), b_im.astype(f32)
    bbr = fr[..., None] * br - fi[..., None] * bi
    bbi = fr[..., None] * bi + fi[..., None] * br
    bur = jnp.einsum('bsgc,gpc->bsgp', uf, bbr)
    bui = jnp.einsum('bsgc,gpc->bsgp', uf, bbi)
    elems = (jnp.broadcast_to(ar, bur.shape), jnp.broadcast_to(ai, bur.shape), bur, bui)
    _, _, xr, xi = lax.associative_scan(_complex_affine_combine, elems, axis=1)
    y = (jnp.einsum('bsgp,gcp->bsgc', xr, c_re.astype(f32))
         - jnp.einsum('bsgp,gcp->bsgc', xi, c_im.astype(f32))
         + d.astype(f32).reshape(SSM_GROUPS, SSM_GROUP_CH) * uf)
    return y.reshape(b_, s_, SSM_WIDTH).astype(u.dtype)

def memory_attention(q, k, v):
    logits = jnp.einsum('bshd,bmhd->bhsm', q, k).astype(jnp.float32) * (MEM_HEAD_DIM ** -0.5)
    p = jax.nn.softmax(logits, axis=-1).astype(v.dtype)
    out = jnp.einsum('bhsm,bmhd->bshd', p, v)
    return out.reshape(q.shape[0], q.shape[1], MEM_WIDTH)

def second_inputs(seed: int = 0) -> dict:
    key = jax.random.key(seed)
    ks = jax.random.split(key, 32)
    f32 = jnp.float32
    L = DEPTH_2

    def nrm(k, shape, scale):
        return jax.random.normal(k, shape, f32) * scale

    def gain(k, shape):
        return 1.0 + 0.02 * jax.random.normal(k, shape, f32)

    n = jnp.arange(SSM_STATE, dtype=f32)
    return {
        'x': nrm(ks[0], (BATCH, SEQ, D_MODEL), 1.0),
        'mem': nrm(ks[1], (BATCH, MEM_TOKENS, D_MODEL), 1.0),
        'ffn1_norm': gain(ks[2], (L, D_MODEL)),
        'ffn1_w_in': nrm(ks[3], (L, D_MODEL, 2 * FFN_DIM), D_MODEL ** -0.5),
        'ffn1_w_out': nrm(ks[4], (L, FFN_DIM, D_MODEL), FFN_DIM ** -0.5),
        'mix_norm': gain(ks[5], (L, D_MODEL)),
        'w_in': nrm(ks[6], (L, D_MODEL, W_IN_COLS), D_MODEL ** -0.5),
        'a_q_gain': gain(ks[7], (L, A_HEAD_DIM)),
        'a_k_gain': gain(ks[8], (L, A_HEAD_DIM)),
        'rel_bias': nrm(ks[9], (REL_BUCKETS, A_HEADS), 0.5),
        'w_o_a': nrm(ks[10], (L, A_WIDTH, D_MODEL), A_WIDTH ** -0.5),
        'ssm_lambda_re': -0.5 + nrm(ks[11], (L, SSM_GROUPS, SSM_STATE), 0.01),
        'ssm_lambda_im': math.pi * n + nrm(ks[12], (L, SSM_GROUPS, SSM_STATE), 0.01),
        'ssm_log_dt': jax.random.uniform(ks[13], (L, SSM_GROUPS), f32,
                                         minval=math.log(DT_MIN), maxval=math.log(DT_MAX)),
        'ssm_b_re': nrm(ks[14], (L, SSM_GROUPS, SSM_STATE, SSM_GROUP_CH), (2 * SSM_GROUP_CH) ** -0.5),
        'ssm_b_im': nrm(ks[15], (L, SSM_GROUPS, SSM_STATE, SSM_GROUP_CH), (2 * SSM_GROUP_CH) ** -0.5),
        'ssm_c_re': nrm(ks[16], (L, SSM_GROUPS, SSM_GROUP_CH, SSM_STATE), SSM_STATE ** -0.5),
        'ssm_c_im': nrm(ks[17], (L, SSM_GROUPS, SSM_GROUP_CH, SSM_STATE), SSM_STATE ** -0.5),
        'ssm_d': nrm(ks[18], (L, SSM_WIDTH), 1.0),
        'w_glu': nrm(ks[19], (L, SSM_WIDTH, 2 * D_MODEL), SSM_WIDTH ** -0.5),
        'mem_norm': gain(ks[20], (L, D_MODEL)),
        'w_mem_kv': nrm(ks[21], (L, D_MODEL, 2 * MEM_WIDTH), D_MODEL ** -0.5),
        'm_q_gain': gain(ks[22], (L, MEM_HEAD_DIM)),
        'm_k_gain': gain(ks[23], (L, MEM_HEAD_DIM)),
        'w_o_m': nrm(ks[24], (L, MEM_WIDTH, D_MODEL), MEM_WIDTH ** -0.5),
        'w_out': nrm(ks[25], (L, D_MODEL, D_MODEL), D_MODEL ** -0.5),
        'ffn2_norm': gain(ks[26], (L, D_MODEL)),
        'ffn2_w_in': nrm(ks[27], (L, D_MODEL, 2 * FFN_DIM), D_MODEL ** -0.5),
        'ffn2_w_out': nrm(ks[28], (L, FFN_DIM, D_MODEL), FFN_DIM ** -0.5),
        'final_norm': gain(ks[29], (L, D_MODEL)),
    }

def second_block(x, mem, ffn1_norm, ffn1_w_in, ffn1_w_out, mix_norm, w_in, a_q_gain, a_k_gain,
              rel_bias, w_o_a, ssm_lambda_re, ssm_lambda_im, ssm_log_dt, ssm_b_re, ssm_b_im,
              ssm_c_re, ssm_c_im, ssm_d, w_glu, mem_norm, w_mem_kv, m_q_gain, m_k_gain, w_o_m,
              w_out, ffn2_norm, ffn2_w_in, ffn2_w_out, final_norm):
    b_, s_ = x.shape[0], x.shape[1]
    offsets = [sum(IN_SPLITS[:i + 1]) for i in range(len(IN_SPLITS) - 1)]
    for l in range(DEPTH_2):
        x = x + 0.5 * swiglu_ffn(rms_norm(x, ffn1_norm[l]), ffn1_w_in[l], ffn1_w_out[l])
        h = rms_norm(x, mix_norm[l])
        q_a, k_a, v_a, q_i, k_i, w_i, u_s, q_m, gates = jnp.split(h @ w_in[l], offsets, axis=-1)
        q_a = rms_norm(q_a.reshape(b_, s_, A_HEADS, A_HEAD_DIM), a_q_gain[l])
        k_a = rms_norm(k_a, a_k_gain[l])
        o_a = indexed_sparse_attention(q_a, k_a, v_a, q_i.reshape(b_, s_, IDX_HEADS, IDX_DIM),
                                       k_i, w_i, rel_bias) @ w_o_a[l]
        y_s = jax.nn.gelu(s5_layer(u_s, ssm_lambda_re[l], ssm_lambda_im[l], ssm_log_dt[l],
                                   ssm_b_re[l], ssm_b_im[l], ssm_c_re[l], ssm_c_im[l], ssm_d[l]))
        glu_a, glu_b = jnp.split(y_s @ w_glu[l], 2, axis=-1)
        o_b = glu_a * jax.nn.sigmoid(glu_b)
        mem_kv = rms_norm(mem, mem_norm[l]) @ w_mem_kv[l]
        m_k, m_v = jnp.split(mem_kv, 2, axis=-1)
        m_k = rms_norm(m_k.reshape(b_, MEM_TOKENS, MEM_HEADS, MEM_HEAD_DIM), m_k_gain[l])
        m_v = m_v.reshape(b_, MEM_TOKENS, MEM_HEADS, MEM_HEAD_DIM)
        q_m = rms_norm(q_m.reshape(b_, s_, MEM_HEADS, MEM_HEAD_DIM), m_q_gain[l])
        o_m = memory_attention(q_m, m_k, m_v) @ w_o_m[l]
        g = jax.nn.sigmoid(gates.reshape(b_, s_, N_BRANCHES, D_MODEL))
        merged = g[:, :, 0] * o_a + g[:, :, 1] * o_b + g[:, :, 2] * o_m
        x = x + merged @ w_out[l]
        x = x + 0.5 * swiglu_ffn(rms_norm(x, ffn2_norm[l]), ffn2_w_in[l], ffn2_w_out[l])
        x = rms_norm(x, final_norm[l])
    return x


def setup_inputs(seed=0):
    out = dict(first_inputs(seed))
    for name, value in second_inputs(seed + 1).items():
        if name != "x":
            out[name + "_2"] = value
    return out


def reference(
    x, norm_pre, norm_post, dil_w_in, dil_w_out, diff_w_in, diff_w_out, diff_lambda_q1,
    diff_lambda_k1, diff_lambda_q2, diff_lambda_k2, diff_subln, mem_2, ffn1_norm_2, ffn1_w_in_2,
    ffn1_w_out_2, mix_norm_2, w_in_2, a_q_gain_2, a_k_gain_2, rel_bias_2, w_o_a_2,
    ssm_lambda_re_2, ssm_lambda_im_2, ssm_log_dt_2, ssm_b_re_2, ssm_b_im_2, ssm_c_re_2,
    ssm_c_im_2, ssm_d_2, w_glu_2, mem_norm_2, w_mem_kv_2, m_q_gain_2, m_k_gain_2, w_o_m_2,
    w_out_2, ffn2_norm_2, ffn2_w_in_2, ffn2_w_out_2, final_norm_2,
):
    x = first_block(
        x, norm_pre, norm_post, dil_w_in, dil_w_out, diff_w_in, diff_w_out, diff_lambda_q1,
        diff_lambda_k1, diff_lambda_q2, diff_lambda_k2, diff_subln,
    )
    return second_block(
        x, mem_2, ffn1_norm_2, ffn1_w_in_2, ffn1_w_out_2, mix_norm_2, w_in_2, a_q_gain_2,
        a_k_gain_2, rel_bias_2, w_o_a_2, ssm_lambda_re_2, ssm_lambda_im_2, ssm_log_dt_2,
        ssm_b_re_2, ssm_b_im_2, ssm_c_re_2, ssm_c_im_2, ssm_d_2, w_glu_2, mem_norm_2,
        w_mem_kv_2, m_q_gain_2, m_k_gain_2, w_o_m_2, w_out_2, ffn2_norm_2, ffn2_w_in_2,
        ffn2_w_out_2, final_norm_2,
    )


_drawn_inputs = setup_inputs


def setup_inputs(seed=0):
    import zlib

    import numpy as np

    out = dict(_drawn_inputs(seed))
    spreads = {}
    factors = {'diff_lambda_q2': 5.868,
     'diff_lambda_k2': 8.0,
     'ffn1_norm_2': 8.0,
     'mix_norm_2': 8.0,
     'a_q_gain_2': 8.0,
     'a_k_gain_2': 8.0,
     'rel_bias_2': 3.227,
     'ssm_lambda_re_2': 64.0,
     'ssm_lambda_im_2': 44.008,
     'ssm_log_dt_2': 48.264,
     'ssm_b_re_2': 62.32,
     'ssm_b_im_2': 62.656,
     'ssm_c_re_2': 63.424,
     'ssm_c_im_2': 62.68,
     'mem_norm_2': 8.0,
     'm_q_gain_2': 8.0,
     'm_k_gain_2': 8.0,
     'ffn2_norm_2': 22.655,
     'final_norm_2': 7.751,
     'diff_lambda_q1': 6.932,
     'diff_lambda_k1': 8.0}
    for name, (base, spread) in spreads.items():
        noise = np.random.default_rng([zlib.crc32(name.encode()), seed]).standard_normal(out[name].shape)
        drawn = base * np.exp(spread * noise) if base else spread * noise
        out[name] = __import__('jax').numpy.asarray(drawn.astype(out[name].dtype))
    for name, factor in factors.items():
        out[name] = (out[name] * factor).astype(out[name].dtype)
    return out
```

```python
import math
from contextlib import ExitStack

import numpy as np

import concourse.bass as bass
from concourse import mybir

P = 128
D = 1024
S = 512
NT = S // P
KC = D // P
KQ = 4
PIECE = KQ * 512
RING = 5
HD = 64
EPS = 1e-6
NEG = -1.0e30
TAKEN = -3.0e38
LAMBDA_INIT = 0.8 - 0.6 * math.exp(-0.3 * 1)

DIL = (1, 4, 16)
DIL_HEADS = 16
ROW = HD + 2

FFN = 2816
FC = FFN // P
MEM = 256
W_IN = 4548
TOPK = min(256, S // 4)
BUCKETS = 32

F32 = mybir.dt.float32
ALU = mybir.AluOpType
ACT = mybir.ActivationFunctionType
AX = mybir.AxisListType

CONSTS = {}
_at = 0
for _name, _n in (("ident", P), ("exchange", P), ("cos", S), ("sin", S), ("mask_first", 384), ("mask_band", 512),
                  ("mask_causal", 512), ("mask_16", P), ("mask_limit", P), ("onehot", 640)):
    CONSTS[_name] = (_at, _at + _n)
    _at += _n
N_CONSTS = _at

PARAMS = {}
_at = 0
for _name, _n in (("norm_pre0", KC), ("norm_pre1", KC), ("ffn1_norm", KC), ("mix_norm", KC), ("ffn2_norm", KC),
                  ("mem_norm", KC), ("a_q_gain", 1), ("a_k_gain", 1), ("m_q_gain", 1), ("m_k_gain", 1),
                  ("lam_re", 8), ("lam_im", 8), ("log_dt", 8), ("ssm_d", 2), ("rel_bias", 8),
                  ("b_re", P), ("b_im", P), ("c_re", P), ("c_im", P)):
    PARAMS[_name] = (_at, _at + _n)
    _at += _n
N_PARAMS = _at

ROWS = {}
_at = 0
for _name, _n in (("post0", D), ("post1", D), ("final", D), ("subln", P), ("lq1", HD), ("lk1", HD), ("lq2", HD), ("lk2", HD)):
    ROWS[_name] = (_at, _at + _n)
    _at += _n
N_ROWS = _at


class Queue:

    def __init__(self, sem):
        self.sem, self.count, self.items, self.waited = sem, 0, [], {}

    def wait(self, *tokens):
        for token in tokens:
            if token is None:
                continue
            if isinstance(token, list):
                self.wait(*token)
                continue
            sem, value = token
            if self.waited.get(sem.name, 0) < value:
                self.waited[sem.name] = value
                self.items.append((None, sem, value, None))

    def __call__(self, method, *args, after=(), signal=True, **kwargs):
        self.wait(*after)
        self.items.append((method, args, kwargs, (self.sem, 1) if signal else None))
        if signal:
            self.count += 1
        return self.sem, self.count

    def dma(self, method, out, in_, counter, after=()):
        self.wait(*after)
        counter[1] += 16
        self.items.append((method, (out, in_), {}, (counter[0], 16)))
        return counter[0], counter[1]

    def run(self, eng):
        for method, a, b, inc in self.items:
            if method is None:
                eng.wait_ge(a, b)
            else:
                ins = method(*a, **b)
                if inc:
                    ins.then_inc(*inc)


def interleave(main, side, ratio=1.0):
    owed = 0.0
    for _ in main:
        owed += ratio
        while owed >= 1.0:
            owed -= 1.0
            next(side, None)
    for _ in side:
        pass


def chain(*streams):
    for stream in streams:
        yield from stream


def program(nc, I, out, stop_after):
    T, V, A, G, SP = nc.tensor, nc.vector, nc.scalar, nc.gpsimd, nc.sync
    ctx = ExitStack()
    with ctx:
        def sb(name, shape):
            return ctx.enter_context(nc.sbuf_tensor(name, shape, F32))

        def sem(name):
            return ctx.enter_context(nc.semaphore(name))

        consts = sb("consts", [P, N_CONSTS])
        params = sb("params", [P, N_PARAMS])
        ring = sb("ring", [P, RING, PIECE])
        x = sb("x", [P, NT, D])
        xT = sb("xT", [P, KC, S])
        small = sb("small", [P, 640])
        minus_half = sb("minus_half", [P, 36])
        ARENA = 29900
        arena = sb("arena", [P, ARENA])
        bank = [ctx.enter_context(nc.psum_tensor(f"bank{i}", [P, 512], F32)) for i in range(8)]
        scratch = nc.dram_tensor("scratch_heads", (3, S, DIL_HEADS * ROW), F32, kind="Internal").ap()
        scratch_bias = nc.dram_tensor("scratch_bias", (8, 640), F32, kind="Internal").ap()

        def const(name, rows=P):
            a, b = CONSTS[name]
            return consts[0:rows, a:b]

        def param(name, i=None):
            a, b = PARAMS[name]
            return params[:, a:b] if i is None else params[:, a + i:a + i + 1]

        ident = const("ident")

        pe, dve, act, pool = Queue(sem("pe_done")), Queue(sem("dve_done")), Queue(sem("act_done")), Queue(sem("pool_done"))
        sp = Queue(sem("sp_done"))
        piece_landed = [[sem(f"piece_landed{i}"), 0] for i in range(RING)]
        counters = {}

        def counter(name):
            if name not in counters:
                counters[name] = [sem(name), 0]
            return counters[name]

        piece_read = [None] * RING
        bank_read = [None] * 8
        n_pieces = [0]

        def barrier():
            done = [(q.sem, q.count) for q in (pe, dve, act, pool) if q.count] + [tuple(c) for c in counters.values() if c[1]]
            for q in (pe, dve, act, pool):
                q.wait(*done)
            carved[0] = 0

        carved = [0]

        def carve(*shape):
            n = int(np.prod(shape))
            a = arena[:, carved[0]:carved[0] + n]
            carved[0] += n
            assert carved[0] <= ARENA, carved[0]
            if len(shape) == 1:
                return a
            if len(shape) == 2:
                return a.rearrange("p (a b) -> p a b", a=shape[0])
            if len(shape) == 3:
                return a.rearrange("p (a b c) -> p a b c", a=shape[0], b=shape[1])
            return a.rearrange("p (a b c d) -> p a b c d", a=shape[0], b=shape[1], c=shape[2])

        def load_piece(view, kq, n):
            slot = n_pieces[0] % RING
            n_pieces[0] += 1
            dst = ring[:, slot, 0:kq * n].rearrange("p (k n) -> p k n", k=kq)
            if isinstance(view, tuple):
                for i, part in enumerate(view):
                    w = n // len(view)
                    landed = sp.dma(SP.dma_start, dst[:, :, i * w:(i + 1) * w], part, piece_landed[slot], after=[piece_read[slot]])
            else:
                landed = sp.dma(SP.dma_start, dst, view, piece_landed[slot], after=[piece_read[slot]])
            return dst, landed, slot

        def weight(w, k0, kq, c0, n):
            return w[k0 * P:(k0 + kq) * P, c0:c0 + n].rearrange("(k p) n -> p k n", p=P)

        def project(pieces, terms, outs, consume, out_rows=P, out_cols=S):
            k0 = 0
            total = sum(kq for _, kq, _ in pieces)
            for view, kq, n in pieces:
                piece, landed, slot = load_piece(view, kq, n)
                for b, o in enumerate(outs):
                    for kk in range(kq):
                        k = k0 + kk
                        lhsT, rhs = terms(piece, k, kk, o)
                        done = pe(T.matmul, bank[b][0:out_rows, 0:out_cols], lhsT, rhs, start=(k == 0), stop=(k == total - 1),
                                  after=[landed, bank_read[b]] if k == 0 else [landed], signal=(kk == kq - 1))
                    if k0 + kq == total:
                        bank_read[b] = consume(o, bank[b][0:out_rows, 0:out_cols], done)
                    yield
                piece_read[slot] = done
                k0 += kq

        def token_major(w, c0, n, tokens, consume, src=None, K=KC):
            src = xT if src is None else src
            return project([(weight(w, k, min(KQ, K - k), c0, n), min(KQ, K - k), n) for k in range(0, K, KQ)],
                           lambda piece, k, kk, i: (tokens(src[:, k, :], i), piece[:, kk, :]),
                           range(NT), consume, out_cols=n)

        def feature_major(w, c0, consume, src=None, K=KC):
            src = xT if src is None else src
            return project([(weight(w, k, min(KQ, K - k), c0, 512), min(KQ, K - k), 512) for k in range(0, K, KQ)],
                           lambda piece, k, kk, j: (piece[:, kk, j * P:(j + 1) * P], src[:, k, :]),
                           range(4), consume)

        def tile(a, i):
            return a[:, i * P:(i + 1) * P]

        def rstd_of(sums, n, dst, after):
            width = sums.shape[-1]
            t = dve(V.tensor_scalar, dst, sums, 1.0 / n, EPS, ALU.mult, ALU.add, after=after)
            return pool(G.tensor_tensor, dst, dst, minus_half[:, 0:width], ALU.pow, after=[t])

        norm_ss = small[:, 0:8]
        norm_rstd = small[:, 8:16]

        def norm_to_feature_major(src, gain, dst, tmp, after, tiles=NT, consumed=None):
            ready = []
            for n in range(tiles):
                t = act(A.activation, tmp[:, n, :], src[:, n, :], ACT.Square, accum_out=norm_ss[:, n:n + 1], after=after)
                t = rstd_of(norm_ss[:, n:n + 1], D, norm_rstd[:, n:n + 1], [t])
                ready.append(dve(V.tensor_scalar, tmp[:, n, :], src[:, n, :], norm_rstd[:, n:n + 1], None, ALU.mult, after=[t]))
            done = []
            for k in range(KC):
                b = k % 8
                for n in range(tiles):
                    t = pe(T.transpose, tile(bank[b], n), tile(tmp[:, n, :], k), ident,
                           after=[ready[n], bank_read[b]], signal=(n == tiles - 1))
                if k % 2 == 0:
                    t = act(A.activation, dst[:, k, 0:tiles * P], bank[b][:, 0:tiles * P], ACT.Copy, scale=param(gain, k), after=[t, consumed])
                else:
                    t = dve(V.tensor_scalar, dst[:, k, 0:tiles * P], bank[b][:, 0:tiles * P], param(gain, k), None, ALU.mult, after=[t, consumed])
                bank_read[b] = t
                done.append(t)
            return done


        def tanh_half(psum, dst, after):
            return act(A.activation, dst, psum, ACT.Tanh, scale=0.5, after=after)

        def twice_silu(psum, dst, after):
            t = tanh_half(psum, dst, after)
            return dve(V.scalar_tensor_tensor, dst, dst, 1.0, psum, ALU.add, ALU.mult, after=[t])

        def add_normed(Y, Yready, row, tmp):
            squares = [None] * NT
            for n in range(NT):
                t = act(A.activation, tmp[:, n % 2, :], Y[:, n, :], ACT.Square, accum_out=norm_ss[:, n:n + 1],
                        after=[Yready[n], squares[n - 2] if n > 1 else None])
                squares[n] = t
                t = rstd_of(norm_ss[:, n:n + 1], D, norm_rstd[:, n:n + 1], [t])
                t = dve(V.scalar_tensor_tensor, Y[:, n, :], Y[:, n, :], norm_rstd[:, n:n + 1], row, ALU.mult, ALU.mult, after=[t])
                t = dve(V.tensor_tensor, x[:, n, :], x[:, n, :], Y[:, n, :], ALU.add, after=[t])
            return t

        first = counter("consts_landed")
        consts_in = sp.dma(SP.dma_start, consts[:, :], I["consts"], first)
        consts_in = sp.dma(SP.dma_start, params[:, :], I["params"], first)
        x_in = [act.dma(A.dma_start, x[:, n, :], I["x"][n * P:(n + 1) * P, :], counter("x_landed")) for n in range(NT)][-1]
        minus_half_set = pool(G.memset, minus_half[:, :], -0.5)
        pool.wait(minus_half_set)
        for q in (pe, dve, act, pool):
            q.wait(consts_in, x_in)

        def load_row(name, dst, after=()):
            a, b = ROWS[name]
            src = I["rows"][0, a:b].partition_broadcast(P)
            return pool.dma(G.dma_start, dst, src, counter("rows_landed"), after=after)

        gate = arena[:, ARENA - NT * D:ARENA].rearrange("p (a b) -> p a b", a=NT)

        def dilated_layer():
            QT, KT, VV = carve(2, 4, S), carve(2, 4, S), carve(2, NT, 512)
            rope_a, rope_b = carve(2, S), carve(2, S)
            scores_sb, PT = carve(2, 896), carve(2, 7, P)
            stage = carve(2, NT, 8, ROW)
            normed = gate
            w_in = I["dil_w_in"]
            norm_to_feature_major(x, "norm_pre0", xT, normed, [])
            xT_ready = [(act.sem, act.count), (dve.sem, dve.count)]
            pe.wait(*xT_ready)
            xT16, xT16_ready, xT_turned = arena[:, ARENA - KC * S:ARENA].rearrange("p (a b) -> p a b", a=KC), [], [pe.count]

            rope_read = [None, None]
            rope_n = [0]

            def rope(dst, psum, token, g, free):
                b = rope_n[0] % 2
                rope_n[0] += 1
                t1 = dve(V.tensor_tensor, rope_a[:, b, :], psum, const("cos"), ALU.mult, after=[token, rope_read[b]])
                for quad in range(4):
                    t = act(A.copy, rope_b[32 * quad:32 * quad + 32, b, :], psum[32 * (quad ^ 1):32 * (quad ^ 1) + 32, :],
                            after=[t1, rope_read[b]], signal=(quad == 3))
                read = t
                t = dve(V.tensor_tensor, rope_b[:, b, :], rope_b[:, b, :], const("sin"), ALU.mult, after=[t])
                r = DIL[g]
                if r == 1:
                    o, a, c = dst, rope_a[:, b, :], rope_b[:, b, :]
                else:
                    o = dst.rearrange("p (r l) -> p l r", r=r)
                    a = rope_a[:, b, :].rearrange("p (l r) -> p l r", r=r)
                    c = rope_b[:, b, :].rearrange("p (l r) -> p l r", r=r)
                t = dve(V.tensor_tensor, o, a, c, ALU.add, after=[t, free])
                rope_read[b] = t
                return read, t

            def group_tokens(g):
                def pick(a, i):
                    if DIL[g] == 1:
                        return tile(a, i)
                    if DIL[g] == 4:
                        return a.rearrange("p (l r) -> p r l", r=4)[:, i, :]
                    return tile(a, i)
                return pick

            heads_read = [None, None]
            ready = {}

            def projections(u):
                g, hf, buf = u // 2, u % 2, u % 2
                ready[u] = []

                def rotate(dst):
                    def consume(j, psum, token):
                        read, t = rope(dst[:, buf, j, :], psum, token, g, heads_read[buf])
                        ready[u].append(t)
                        return read
                    return consume

                def keep_v(i, psum, token):
                    t = act(A.copy, VV[:, buf, i, :], psum, after=[token, heads_read[buf]])
                    ready[u].append(t)
                    return t

                c = g * D + hf * 512
                yield from feature_major(w_in, c, rotate(QT))
                yield from feature_major(w_in, 3 * D + c, rotate(KT))
                if u == 2:
                    for k in range(KC):
                        xT16_ready.append(pool(G.tensor_copy, xT16[:, k, :].rearrange("p (r l) -> p r l", r=16),
                                               xT[:, k, :].rearrange("p (l r) -> p r l", r=16), after=xT_ready + [(pe.sem, xT_turned[0])]))
                if u == 4:
                    pe.wait(*xT16_ready)
                yield from token_major(w_in, 6 * D + c, 512, group_tokens(g), keep_v, src=xT16 if g == 2 else xT)

            stage_read = [None, None]
            sc_read, pt_read = [None, None], [None, None]
            heads_n = [0]

            def attention(u):
                g, hf, buf = u // 2, u % 2, u % 2
                st = stage[:, buf]
                if g == 0:
                    blocks = [[(0, 0)], [(1, 0), (2, 1)], [(3, 1), (4, 2)], [(5, 2), (6, 3)]]
                    spans = [(0, 128), (128, 256), (384, 256), (640, 256)]
                else:
                    blocks = [[(i, i)] for i in range(NT)]
                    spans = [(128 * i, 128) for i in range(NT)]
                nb = 7 if g == 0 else 4
                exp_done, first_b = {}, {}

                def score(hh):
                    j, off = hh // 2, 64 * (hh % 2)
                    q, k = QT[off:off + 64, buf, j, :], KT[off:off + 64, buf, j, :]
                    s = heads_n[0] % 2
                    heads_n[0] += 1
                    first_b[hh] = s
                    sc = scores_sb[:, s, :]
                    if g == 0:
                        for b, tiles_ in ((4, (0, 1)), (5, (2, 3))):
                            base = spans[tiles_[0]][0]
                            for i in tiles_:
                                a, n = spans[i]
                                k0 = max(0, i - 1) * P
                                t = pe(T.matmul, bank[b][:, a - base:a - base + n], tile(q, i), k[:, k0:k0 + n], start=True, stop=True,
                                       after=[bank_read[b], ready[u]], signal=(i == tiles_[1]))
                            n = 384 if b == 4 else 512
                            t = dve(V.scalar_tensor_tensor, sc[:, base:base + n], bank[b][:, 0:n], HD ** -0.5,
                                    const("mask_first" if b == 4 else "mask_band"), ALU.mult, ALU.add, after=[t, sc_read[s]])
                            bank_read[b] = t
                        dve(V.tensor_reduce, st[:, 0:1, hh, ROW - 1], sc[:, 0:P], AX.X, ALU.max, negate=True,
                            after=[t, stage_read[buf]], signal=False)
                        t = dve(V.tensor_reduce, st[:, 1:4, hh, ROW - 1], sc[:, P:896].rearrange("p (a b) -> p a b", a=3),
                                AX.X, ALU.max, negate=True)
                    else:
                        b = 4 + s
                        for i in range(NT):
                            t = pe(T.matmul, tile(bank[b], i), tile(q, i), tile(k, i), start=True, stop=True,
                                   after=[bank_read[b], ready[u]], signal=(i == NT - 1))
                        m = const("mask_causal")[:, 384:512] if g == 1 else const("mask_16")
                        t = dve(V.scalar_tensor_tensor, sc[:, 0:512].rearrange("p (a b) -> p a b", a=NT),
                                bank[b][:, :].rearrange("p (a b) -> p a b", a=NT), HD ** -0.5,
                                m.unsqueeze(1).to_broadcast([P, NT, P]), ALU.mult, ALU.add, after=[t, sc_read[s]])
                        bank_read[b] = t
                        t = dve(V.tensor_reduce, st[:, :, hh, ROW - 1], sc[:, 0:512].rearrange("p (a b) -> p a b", a=NT),
                                AX.X, ALU.max, negate=True, after=[t, stage_read[buf]])
                    for i in range(NT):
                        a, n = spans[i]
                        t2 = act(A.activation, sc[:, a:a + n], sc[:, a:a + n], ACT.Exp, bias=st[:, i, hh, ROW - 1:ROW],
                                 accum_out=st[:, i, hh, ROW - 2:ROW - 1], after=[t])
                    exp_done[hh] = t2

                pt_done = {}

                def turn(hh):
                    s = first_b[hh]
                    for r, lo in enumerate(range(0, nb, 4)):
                        hi = min(nb, lo + 4)
                        for blk in range(lo, hi):
                            t = pe(T.transpose, tile(bank[6], blk - lo), tile(scores_sb[:, s, :], blk), ident,
                                   after=[exp_done[hh], bank_read[6]], signal=(blk == hi - 1))
                        n = (hi - lo) * P
                        dst = PT[:, s, lo:hi, :].rearrange("p a b -> p (a b)")
                        if r == 0:
                            t3 = dve(V.tensor_copy, dst, bank[6][:, 0:n], after=[t, pt_read[s]])
                        else:
                            t3 = act(A.copy, dst, bank[6][:, 0:n], after=[t, pt_read[s]])
                        bank_read[6] = t3
                        pt_done[hh, r] = t3
                    sc_read[s] = t

                def values(hh):
                    s = first_b[hh]
                    for i in range(NT):
                        for m, (blk, kt) in enumerate(blocks[i]):
                            t = pe(T.matmul, bank[7][:, i * HD:(i + 1) * HD], PT[:, s, blk, :], VV[:, buf, kt, hh * HD:(hh + 1) * HD],
                                   start=(m == 0), stop=(m == len(blocks[i]) - 1),
                                   after=[pt_done[hh, 0], pt_done.get((hh, 1)), bank_read[7]], signal=(i == NT - 1 and m == len(blocks[i]) - 1))
                    pt_read[s] = t
                    bank_read[7] = dve(V.tensor_copy, st[:, :, hh, 0:HD], bank[7][:, 0:NT * HD].rearrange("p (a b) -> p a b", a=NT),
                                       after=[t])
                    return t

                for step in range(8 + 1):
                    if step < 8:
                        score(step)
                    yield
                    if step >= 1:
                        turn(step - 1)
                        yield
                        t = values(step - 1)
                    yield
                heads_read[buf] = t
                done = [bank_read[7], exp_done[7], (act.sem, act.count)]
                for i in range(NT):
                    rows = scratch[g].rearrange("(l r) c -> r l c", r=DIL[g])
                    if DIL[g] == 16:
                        for rr in range(4):
                            stage_read[buf] = pool.dma(G.dma_start, rows[4 * i + rr, :, hf * 8 * ROW:(hf + 1) * 8 * ROW],
                                                       st[32 * rr:32 * rr + 32, i].rearrange("p a b -> p (a b)"), counter(f"stage_stored{buf}"), after=done)
                    else:
                        dst = rows[i] if DIL[g] == 4 else rows[0, i * P:(i + 1) * P]
                        stage_read[buf] = pool.dma(G.dma_start, dst[:, hf * 8 * ROW:(hf + 1) * 8 * ROW],
                                                   st[:, i].rearrange("p a b -> p (a b)"), counter(f"stage_stored{buf}"), after=done)

            side = iter(())
            for u in range(6):
                interleave(projections(u), side, 1.15)
                side = attention(u)

            gate_ready = [None] * NT

            def keep_gate(c):
                def consume(i, psum, token):
                    dst = gate[:, i, c * 512:(c + 1) * 512]
                    gate_ready[i] = twice_silu(psum, dst, [token])
                    return gate_ready[i]
                return consume

            gates = chain(*[token_major(w_in, 9 * D + c * 512, 512, tile, keep_gate(c)) for c in range(2)])
            interleave(gates, side, 2.0)
            barrier()

            heads = carve(2, 3, DIL_HEADS * ROW)
            mix, Y = carve(2, D), carve(NT, D)
            heads_free = [None, None]
            mix_free = [None, None]
            yT = xT
            yT_ready = []
            mins, corr, dens = small[:, 16:32], small[:, 32:80], small[:, 80:128]
            stats_free = None
            for n in range(NT):
                b = n % 2
                H = heads[:, b].rearrange("p g (h r) -> p g h r", h=DIL_HEADS)
                landed = pool.dma(G.dma_start, heads[:, b], scratch[:, n * P:(n + 1) * P, :].rearrange("g p c -> p g c"),
                                  counter(f"heads_landed{b}"), after=[heads_free[b]])
                by_g = lambda a: a.rearrange("p (g h) -> p g h", g=3)
                t = dve(V.tensor_reduce, mins, H[:, :, :, ROW - 1].rearrange("p g h -> p h g"), AX.X, ALU.min, after=[landed, stats_free])
                t = dve(V.tensor_tensor, by_g(corr), mins.unsqueeze(1).to_broadcast([P, 3, DIL_HEADS]), H[:, :, :, ROW - 1], ALU.subtract, after=[t])
                t = act(A.activation, corr, corr, ACT.Exp, after=[t])
                t = dve(V.tensor_tensor, by_g(dens), by_g(corr), H[:, :, :, ROW - 2], ALU.mult, after=[t])
                t = dve(V.tensor_reduce, mins, dens.rearrange("p (g h) -> p h g", g=3), AX.X, ALU.add, after=[t])
                t = dve(V.reciprocal, mins, mins, after=[t])
                t = dve(V.tensor_tensor, by_g(corr), by_g(corr), mins.unsqueeze(1).to_broadcast([P, 3, DIL_HEADS]), ALU.mult, after=[t])
                for g in range(3):
                    w = corr[:, g * 16:(g + 1) * 16].unsqueeze(2).to_broadcast([P, DIL_HEADS, HD])
                    t = dve(V.tensor_tensor, H[:, g, :, 0:HD], H[:, g, :, 0:HD], w, ALU.mult, after=[t] if g == 0 else [])
                stats_free = t
                m = mix[:, b, :].rearrange("p (h r) -> p h r", h=DIL_HEADS)
                t = dve(V.tensor_tensor, m, H[:, 0, :, 0:HD], H[:, 1, :, 0:HD], ALU.add, after=[t, mix_free[b]])
                t = dve(V.tensor_tensor, m, m, H[:, 2, :, 0:HD], ALU.add, after=[t])
                heads_free[b] = t
                t = dve(V.scalar_tensor_tensor, mix[:, b, :], mix[:, b, :], 0.5, gate[:, n, :], ALU.mult, ALU.mult, after=[t])
                for c in range(2):
                    pb = 4 + 2 * b + c
                    for k in range(4):
                        t2 = pe(T.transpose, tile(bank[pb], k), tile(mix[:, b, :], 4 * c + k), ident, after=[t, bank_read[pb]], signal=(k == 3))
                    dst = yT[:, 4 * c:4 * c + 4, n * P:(n + 1) * P]
                    bank_read[pb] = act(A.copy, dst, bank[pb][:, :].rearrange("p (a b) -> p a b", a=4), after=[t2])
                    yT_ready.append(bank_read[pb])
                mix_free[b] = t2
            pe.wait(*yT_ready)
            return Y

        def project_out(w, Y):
            Yready = [None] * NT

            def keep(c):
                def consume(i, psum, token):
                    Yready[i] = act(A.copy, Y[:, i, c * 512:(c + 1) * 512], psum, after=[token])
                    return Yready[i]
                return consume
            for c in range(2):
                for _ in token_major(w, c * 512, 512, tile, keep(c)):
                    pass
            return Yready

        def finish_layer(w, Y, row_name):
            row, tmp = carve(D), carve(2, D)
            row_in = load_row(row_name, row)
            Yready = project_out(w, Y)
            dve.wait(row_in)
            add_normed(Y, Yready, row, tmp)
            barrier()

        def differential_layer():
            QT, KT, VV = carve(2, 4, S), carve(2, 4, S), carve(2, NT, 512)
            rope_a, rope_b = carve(2, S), carve(2, S)
            E, PT = carve(2, 2, S), carve(2, S)
            O = carve(NT, D)
            rowv = carve(P + 4 * HD)
            stat = small[:, 192:192 + 16]
            neg_lam, lam2 = small[:, 208:209], small[:, 209:211]
            w_in = I["diff_w_in"]
            rows_in = pool.dma(G.dma_start, rowv, I["rows"][0, ROWS["subln"][0]:ROWS["lk2"][1]].partition_broadcast(P), counter("rows_landed"))
            xT_ready = norm_to_feature_major(x, "norm_pre1", xT, gate, [])
            pe.wait(*xT_ready)
            for m in range(2):
                a = P + 2 * m * HD
                t = dve(V.tensor_tensor, rowv[:, a:a + HD], rowv[:, a:a + HD], rowv[:, a + HD:a + 2 * HD], ALU.mult, after=[rows_in])
                t = dve(V.tensor_reduce, lam2[:, m:m + 1], rowv[:, a:a + HD], AX.X, ALU.add, after=[t])
            t = act(A.activation, lam2, lam2, ACT.Exp, after=[t])
            t = dve(V.tensor_tensor, neg_lam, lam2[:, 1:2], lam2[:, 0:1], ALU.subtract, after=[t])
            t = dve(V.tensor_scalar, neg_lam, neg_lam, -LAMBDA_INIT, None, ALU.add, after=[t])
            t = dve(V.tensor_scalar, rowv[:, 0:P], rowv[:, 0:P], 0.5 * (1.0 - LAMBDA_INIT), None, ALU.mult, after=[t])
            dve.wait(t)

            rope_read, rope_n, heads_read, ready = [None, None], [0], [None, None], {}

            def projections(u):
                buf = u % 2
                ready[u] = []

                def rotate(dst):
                    def consume(j, psum, token):
                        b = rope_n[0] % 2
                        rope_n[0] += 1
                        t1 = dve(V.tensor_tensor, rope_a[:, b, :], psum, const("cos"), ALU.mult, after=[token, rope_read[b]])
                        for quad in range(4):
                            read = act(A.copy, rope_b[32 * quad:32 * quad + 32, b, :], psum[32 * (quad ^ 1):32 * (quad ^ 1) + 32, :],
                                       after=[t1, rope_read[b]], signal=(quad == 3))
                        t = dve(V.tensor_tensor, rope_b[:, b, :], rope_b[:, b, :], const("sin"), ALU.mult, after=[read])
                        t = dve(V.tensor_tensor, dst[:, buf, j, :], rope_a[:, b, :], rope_b[:, b, :], ALU.add, after=[t, heads_read[buf]])
                        rope_read[b] = t
                        ready[u].append(t)
                        return read
                    return consume

                def keep_v(i, psum, token):
                    t = act(A.copy, VV[:, buf, i, :], psum, after=[token, heads_read[buf]])
                    ready[u].append(t)
                    return t

                yield from feature_major(w_in, u * 512, rotate(QT))
                yield from feature_major(w_in, D + u * 512, rotate(KT))
                yield from token_major(w_in, 2 * D + u * 512, 512, tile, keep_v)

            e_read, pt_read = [None, None], [None, None]

            def attention(u):
                buf = u % 2
                jobs = [(hh, i) for hh in range(4) for i in range(NT)]
                made, turned = {}, {}

                def score(n):
                    hh, i = jobs[n]
                    s, nk = n % 2, (i + 1) * P
                    mx, den = stat[:, 4 * s:4 * s + 2], stat[:, 4 * s + 2:4 * s + 4]
                    for c in range(2):
                        off = 64 * c
                        t = pe(T.matmul, bank[4 + c][:, 0:nk], tile(QT[off:off + 64, buf, hh, :], i), KT[off:off + 64, buf, hh, 0:nk],
                               start=True, stop=True, after=[bank_read[4 + c], ready[u]])
                        t = dve(V.scalar_tensor_tensor, E[:, s, c, 0:nk], bank[4 + c][:, 0:nk], HD ** -0.5,
                                const("mask_causal")[:, 384 - i * P:512], ALU.mult, ALU.add, after=[t, e_read[s]])
                        bank_read[4 + c] = t
                    t = dve(V.tensor_reduce, mx, E[:, s, :, 0:nk], AX.X, ALU.max, negate=True, after=[t])
                    for c in range(2):
                        t2 = act(A.activation, E[:, s, c, 0:nk], E[:, s, c, 0:nk], ACT.Exp, bias=mx[:, c:c + 1],
                                 accum_out=den[:, c:c + 1], after=[t])
                    made[n] = t2

                def combine(n):
                    hh, i = jobs[n]
                    s, nk = n % 2, (i + 1) * P
                    den = stat[:, 4 * s + 2:4 * s + 4]
                    t = dve(V.reciprocal, den, den, after=[made[n]])
                    t = dve(V.tensor_scalar, E[:, s, 0, 0:nk], E[:, s, 0, 0:nk], den[:, 0:1], None, ALU.mult, after=[t])
                    t = dve(V.tensor_scalar, den[:, 1:2], den[:, 1:2], neg_lam, None, ALU.mult, after=[t])
                    t = dve(V.scalar_tensor_tensor, E[:, s, 0, 0:nk], E[:, s, 1, 0:nk], den[:, 1:2], E[:, s, 0, 0:nk], ALU.mult, ALU.add, after=[t])
                    for k in range(i + 1):
                        t2 = pe(T.transpose, tile(bank[6], k), tile(E[:, s, 0, :], k), ident, after=[t, bank_read[6]], signal=(k == i))
                    e_read[s] = t2
                    bank_read[6] = act(A.copy, PT[:, s, 0:nk], bank[6][:, 0:nk], after=[t2, pt_read[s]])
                    turned[n] = bank_read[6]

                def values(n):
                    hh, i = jobs[n]
                    s = n % 2
                    for k in range(i + 1):
                        t = pe(T.matmul, tile(bank[7], i), tile(PT[:, s, :], k), VV[:, buf, k, hh * P:(hh + 1) * P],
                               start=(k == 0), stop=(k == i), after=[turned[n], bank_read[7]], signal=(k == i))
                    pt_read[s] = t
                    if i == NT - 1:
                        h = 4 * u + hh
                        bank_read[7] = act(A.copy, O[:, :, h * P:(h + 1) * P], bank[7][:, :].rearrange("p (a b) -> p a b", a=NT), after=[t])
                    return t

                for n in range(len(jobs) + 1):
                    if n < len(jobs):
                        score(n)
                    if n >= 1:
                        combine(n - 1)
                        yield
                        t = values(n - 1)
                    yield
                heads_read[buf] = t

            side = iter(())
            for u in range(2):
                interleave(projections(u), side, 1.5)
                side = attention(u)

            def keep_gate(c):
                def consume(i, psum, token):
                    dst = gate[:, i, c * 512:(c + 1) * 512]
                    return twice_silu(psum, dst, [token])
                return consume

            interleave(chain(*[token_major(w_in, 3 * D + c * 512, 512, tile, keep_gate(c)) for c in range(2)]), side, 2.2)
            barrier()

            carve(3 * 4096 + 2048 + 2048 + 1024)
            O, rowv = carve(NT, D), carve(P + 4 * HD)
            n_used = carved[0]
            carved[0] = 0
            sq, Y = carve(2, D), carve(NT, D)
            sub = rowv[:, 0:P].unsqueeze(1).to_broadcast([P, 8, P])
            for n in range(NT):
                on = O[:, n, :].rearrange("p (h d) -> p h d", h=8)
                ss = small[:, 16 + 8 * n:24 + 8 * n]
                t = act(A.activation, sq[:, n % 2, :], O[:, n, :], ACT.Square)
                t = dve(V.tensor_reduce, ss, sq[:, n % 2, :].rearrange("p (h d) -> p h d", h=8), AX.X, ALU.add, after=[t])
                act.wait(t)
                t = rstd_of(ss, P, ss, [t])
                t = dve(V.tensor_tensor, on, on, ss.unsqueeze(2).to_broadcast([P, 8, P]), ALU.mult, after=[t])
                t = dve(V.tensor_tensor, on, on, sub, ALU.mult, after=[t])
                t = dve(V.tensor_tensor, O[:, n, :], O[:, n, :], gate[:, n, :], ALU.mult, after=[t])
                for c in range(2):
                    pb = 4 + 2 * (n % 2) + c
                    for k in range(4):
                        t2 = pe(T.transpose, tile(bank[pb], k), tile(O[:, n, :], 4 * c + k), ident, after=[t, bank_read[pb]], signal=(k == 3))
                    bank_read[pb] = act(A.copy, xT[:, 4 * c:4 * c + 4, n * P:(n + 1) * P], bank[pb][:, :].rearrange("p (a b) -> p a b", a=4), after=[t2])
                    pe_waits.append(bank_read[pb])
            pe.wait(*pe_waits)
            pe_waits.clear()
            return Y

        pe_waits = []

        def feed_forward(gain, w_in, w_out):
            hidden = carve(FC, S)
            e = carve(2, S)
            normed = carve(NT, D)
            pe.wait(*norm_to_feature_major(x, gain, xT, normed, []))
            hidden_ready = []
            e_ready, e_n = {}, [0]
            e_free = [None, None]

            def view(c, h):
                return weight(w_in, h * KQ, KQ, c * 256, 256), weight(w_in, h * KQ, KQ, FFN + c * 256, 256)

            for c in range(FC // 2):
                def consume(o, psum, token):
                    s = o % 2
                    dst = hidden[:, 2 * c + s, :]
                    if o < 2:
                        e_ready[s] = twice_silu(psum, e[:, s, :], [token, e_free[s]])
                        return e_ready[s]
                    e_free[s] = dve(V.tensor_tensor, dst, e[:, s, :], psum, ALU.mult, after=[token, e_ready[s]])
                    hidden_ready.append(e_free[s])
                    return e_free[s]
                for _ in project([(view(c, h), KQ, 512) for h in range(2)],
                                 lambda piece, k, kk, o: (piece[:, kk, o * P:(o + 1) * P], xT[:, k, :]), range(4), consume):
                    pass
            pe.wait(*hidden_ready)
            for c in range(2):
                def add(i, psum, token):
                    dst = x[:, i, c * 512:(c + 1) * 512]
                    return dve(V.scalar_tensor_tensor, dst, psum, 0.25, dst, ALU.mult, ALU.add, after=[token])
                for _ in token_major(w_out, c * 512, 512, tile, add, src=hidden, K=FC):
                    pass
            barrier()

        def hybrid():
            mem, memn, memT = carve(2, D), carve(2, D), carve(KC, 2 * P)
            normed = carve(NT, D)
            kv = carve(2, 512)
            carved[0] = 24 * 512
            qaT, kaT, kiT, qiT = carve(4, S), carve(S), carve(S), carve(2, S)
            uT, qmT, va = carve(2, S), carve(2, S), carve(NT, HD)
            mkT, mv = carve(2, MEM), carve(2, MEM)
            sel = carve(1280)
            work, PT = carve(1024), carve(1024)
            hank, bias = carve(2, S), carve(2, S)
            X = carve(2, 2, 256 + S)
            tb, BT, CT = carve(2, P), carve(2, P), carve(2, 2, P)
            coef = small[:, 256:640]

            mem_in = pool.dma(G.dma_start, mem, I["mem"].rearrange("(n p) c -> p n c", p=P), counter("mem_landed"))
            act.wait(mem_in)
            dve.wait(mem_in)
            pe.wait(*norm_to_feature_major(mem, "mem_norm", memT, memn, [], tiles=2))
            kv_ready = []

            def keep_kv(i, psum, token):
                kv_ready.append(act(A.copy, kv[:, i, :], psum, after=[token]))
                return kv_ready[-1]
            for _ in project([(weight(I["w_mem_kv"], k, KQ, 0, 512), KQ, 512) for k in (0, KQ)],
                             lambda piece, k, kk, i: (tile(memT[:, k, :], i), piece[:, kk, :]), range(2), keep_kv):
                pass
            pe.wait(*norm_to_feature_major(x, "mix_norm", xT, normed, []))
            norm_stat = small[:, 128:192]

            def norm_heads(a, heads, stat, tmp, after):
                t = dve(V.tensor_tensor, tmp, a, a, ALU.mult, after=after)
                t = dve(V.tensor_reduce, stat, tmp.rearrange("p (h d) -> p h d", h=heads), AX.X, ALU.add, after=[t])
                t = rstd_of(stat, HD, stat, [t])
                a3 = a.rearrange("p (h d) -> p h d", h=heads)
                return dve(V.tensor_tensor, a3, a3, stat.unsqueeze(2).to_broadcast([P, heads, HD]), ALU.mult, after=[t])

            def turn_chunks(sources, dst, b, scale=None, tiles=NT):
                for n in range(tiles):
                    t = pe(T.transpose, tile(bank[b], n), sources(n), ident, after=[bank_read[b]], signal=(n == tiles - 1))
                if scale is None:
                    bank_read[b] = act(A.copy, dst, bank[b][:, 0:tiles * P], after=[t])
                else:
                    bank_read[b] = act(A.activation, dst, bank[b][:, 0:tiles * P], ACT.Copy, scale=scale, after=[t])
                return bank_read[b]

            for i in range(2):
                t = norm_heads(kv[:, i, 0:256], 4, norm_stat[:, 4 * i:4 * i + 4], work[:, 256 * i:256 * i + 256], kv_ready)
                t = pool(G.tensor_copy, mv[:, i, :], kv[:, i, 256:512], after=[t])
            pe.wait(t, (dve.sem, dve.count))
            for j in range(2):
                turn_chunks(lambda n: kv[:, n, j * P:(j + 1) * P], mkT[:, j, :], 4 + j, param("m_k_gain"), tiles=2)
            barrier()

            proj = carve(NT, 1476)
            kdup = carve(NT, 2, P)
            proj_ready = []

            def keep(c0, n):
                def consume(i, psum, token):
                    proj_ready.append(act(A.copy, proj[:, i, c0:c0 + n], psum, after=[token]))
                    return proj_ready[-1]
                return consume
            for c0, n in ((0, 512), (512, 452), (964, 512)):
                for _ in token_major(I["w_in"], c0, n, tile, keep(c0, n)):
                    pass
            for i in range(NT):
                t = norm_heads(proj[:, i, 0:576], 9, norm_stat[:, 0:9], PT[:, 0:576], [proj_ready])
                t = norm_heads(proj[:, i, 1220:1476], 4, norm_stat[:, 16:20], PT[:, 576:832], [t])
                for m, c0 in ((0, 512), (1, 896)):
                    for half in range(2):
                        t = dve(V.tensor_copy, kdup[:, i, m, half * HD:(half + 1) * HD], proj[:, i, c0:c0 + HD], after=[t])
                t = dve(V.tensor_copy, va[:, i, :], proj[:, i, 576:640])
            pe.wait(t)
            cols = lambda c: (lambda n: proj[:, n, c:c + P])
            turn_list = [(cols(j * P), qaT[:, j, :], param("a_q_gain")) for j in range(4)]
            turn_list += [(lambda n: kdup[:, n, 0, :], kaT, param("a_k_gain")), (lambda n: kdup[:, n, 1, :], kiT, None)]
            turn_list += [(cols(640 + j * P), qiT[:, j, :], None) for j in range(2)]
            turn_list += [(cols(964 + j * P), uT[:, j, :], None) for j in range(2)]
            turn_list += [(cols(1220 + j * P), qmT[:, j, :], param("m_q_gain")) for j in range(2)]
            for m, (src, dst, scale) in enumerate(turn_list):
                turn_chunks(src, dst, m % 8, scale)
            w_idx = small[:, 192:208]
            t = dve(V.tensor_scalar, w_idx.rearrange("p (n h) -> p n h", n=NT), proj[:, :, 960:964], HD ** -0.5 * 4 ** -0.5, None, ALU.mult)
            for lo, hi, b in ((0, 512, 4), (512, 640, 5)):
                t = pe(T.matmul, bank[b][0:8, 0:hi - lo], params[0:BUCKETS, PARAMS["rel_bias"][0]:PARAMS["rel_bias"][1]],
                       const("onehot", BUCKETS)[:, lo:hi], start=True, stop=True, after=[bank_read[b]])
                t = act(A.copy, work[0:8, lo:hi], bank[b][0:8, 0:hi - lo], after=[t])
                bank_read[b] = t
            bias_stored = pool.dma(G.dma_start, scratch_bias, work[0:8, 0:640], counter("bias_stored"), after=[t])

            c8 = lambda i: coef[:, 8 * i:8 * i + 8]
            dt, th, mag, cs, sn, tmp1, tmp2, den, fr, fi = [c8(i) for i in range(10)]
            powers = [(c8(10 + 3 * k), c8(11 + 3 * k), c8(12 + 3 * k)) for k in range(9)]
            lr, li = param("lam_re"), param("lam_im")
            last = [None]

            def v(method, *args, **kw):
                last[0] = dve(method, *args, after=[last[0]], **kw)

            last[0] = act(A.activation, dt, param("log_dt"), ACT.Exp)
            v(V.tensor_tensor, th, li, dt, ALU.mult)
            v(V.tensor_tensor, tmp1, lr, dt, ALU.mult)
            last[0] = act(A.activation, mag, tmp1, ACT.Exp, after=[last[0]])
            MAGIC = 1.5 * 2.0 ** 23
            C1 = 6.28125
            C2 = float(np.float32(2 * math.pi - C1))
            C3 = 2 * math.pi - C1 - C2
            for dst, turn_part, shift in ((sn, 0.0, 0.0), (cs, 0.25, math.pi / 2)):
                v(V.tensor_scalar, tmp1, th, 1 / (2 * math.pi), turn_part, ALU.mult, ALU.add)
                v(V.tensor_scalar, tmp1, tmp1, MAGIC, None, ALU.add)
                v(V.tensor_scalar, tmp1, tmp1, -MAGIC, None, ALU.add)
                v(V.scalar_tensor_tensor, tmp2, tmp1, -C1, th, ALU.mult, ALU.add)
                v(V.scalar_tensor_tensor, tmp2, tmp1, -C2, tmp2, ALU.mult, ALU.add)
                v(V.scalar_tensor_tensor, tmp2, tmp1, -C3, tmp2, ALU.mult, ALU.add)
                v(V.tensor_scalar, tmp2, tmp2, shift, None, ALU.add)
                v(V.tensor_scalar, tmp2, tmp2, 3.1415925, -3.1415925, ALU.min, ALU.max)
                last[0] = act(A.activation, dst, tmp2, ACT.Sin, after=[last[0]])
            ar, ai, nai = powers[0]
            v(V.tensor_tensor, ar, mag, cs, ALU.mult)
            v(V.tensor_tensor, ai, mag, sn, ALU.mult)
            v(V.tensor_tensor, den, lr, lr, ALU.mult)
            v(V.tensor_tensor, tmp1, li, li, ALU.mult)
            v(V.tensor_tensor, den, den, tmp1, ALU.add)
            v(V.reciprocal, den, den)
            v(V.tensor_scalar, cs, ar, -1.0, None, ALU.add)
            v(V.tensor_tensor, tmp1, cs, lr, ALU.mult)
            v(V.tensor_tensor, tmp2, ai, li, ALU.mult)
            v(V.tensor_tensor, fr, tmp1, tmp2, ALU.add)
            v(V.tensor_tensor, fr, fr, den, ALU.mult)
            v(V.tensor_tensor, tmp1, ai, lr, ALU.mult)
            v(V.tensor_tensor, tmp2, cs, li, ALU.mult)
            v(V.tensor_tensor, fi, tmp1, tmp2, ALU.subtract)
            v(V.tensor_tensor, fi, fi, den, ALU.mult)
            for k in range(9):
                r, i_, ni = powers[k]
                v(V.tensor_scalar, ni, i_, -1.0, None, ALU.mult)
                if k < 8:
                    r2, i2, _ = powers[k + 1]
                    v(V.tensor_tensor, tmp1, r, r, ALU.mult)
                    v(V.tensor_tensor, tmp2, i_, i_, ALU.mult)
                    v(V.tensor_tensor, r2, tmp1, tmp2, ALU.subtract)
                    v(V.tensor_tensor, tmp1, r, i_, ALU.mult)
                    v(V.tensor_scalar, i2, tmp1, 2.0, None, ALU.mult)
            g16 = lambda a: a.rearrange("p (g c) -> p g c", g=8)
            bcol = lambda a: a.unsqueeze(2).to_broadcast([P, 8, 16])
            br, bi = param("b_re"), param("b_im")
            t1, t2, t3 = work[:, 640:768], work[:, 768:896], work[:, 896:1024]
            v(V.tensor_tensor, g16(t1), g16(br), bcol(fr), ALU.mult)
            v(V.tensor_tensor, g16(t2), g16(bi), bcol(fi), ALU.mult)
            v(V.tensor_tensor, t3, t1, t2, ALU.subtract)
            v(V.tensor_tensor, g16(t1), g16(bi), bcol(fr), ALU.mult)
            v(V.tensor_tensor, g16(t2), g16(br), bcol(fi), ALU.mult)
            v(V.tensor_tensor, bi, t1, t2, ALU.add)
            v(V.tensor_copy, br, t3)
            v(V.tensor_scalar, param("c_im"), param("c_im"), -1.0, None, ALU.mult)
            pool(G.memset, X[:, :, :, 0:256], 0.0)
            barrier()
            if stop_after == "proj":
                return

            gates = carve(24, S)
            gate_done = {}

            def gate_chunk(c):
                def consume(j, psum, token):
                    gate_done[4 * c + j] = tanh_half(psum, gates[:, 4 * c + j, :], [token])
                    return gate_done[4 * c + j]
                return consume

            def memory_attention():
                for h in range(4):
                    j, off = h // 2, 64 * (h % 2)
                    q, k = qmT[off:off + 64, j, :], mkT[off:off + 64, j, :]
                    nm, dn = small[:, 208:212], small[:, 212:216]
                    W = work.rearrange("p (n k) -> p n k", n=NT)
                    for b in range(2):
                        for i in (2 * b, 2 * b + 1):
                            t = pe(T.matmul, bank[4 + b][:, (i % 2) * MEM:(i % 2 + 1) * MEM], tile(q, i), k, start=True, stop=True,
                                   after=[bank_read[4 + b]], signal=(i % 2 == 1))
                        t = act(A.activation, work[:, b * 512:(b + 1) * 512], bank[4 + b][:, :], ACT.Copy, scale=HD ** -0.5, after=[t, mem_free[0]])
                        bank_read[4 + b] = t
                    yield
                    t = dve(V.tensor_reduce, nm, W, AX.X, ALU.max, negate=True, after=[t])
                    for i in range(NT):
                        t2 = act(A.activation, W[:, i, :], W[:, i, :], ACT.Exp, bias=nm[:, i:i + 1], accum_out=dn[:, i:i + 1], after=[t])
                    t = dve(V.reciprocal, dn, dn, after=[t2])
                    t = dve(V.tensor_tensor, W, W, dn.unsqueeze(2).to_broadcast([P, NT, MEM]), ALU.mult, after=[t])
                    yield
                    for kb in range(2):
                        for i in range(NT):
                            t2 = pe(T.transpose, tile(bank[6], i), W[:, i, kb * P:(kb + 1) * P], ident, after=[t, bank_read[6]], signal=(i == NT - 1))
                        t3 = act(A.copy, PT[:, kb * 512:(kb + 1) * 512], bank[6][:, :], after=[t2, mem_free[1]])
                        bank_read[6] = t3
                    mem_free[0] = t2
                    yield
                    for kb in range(2):
                        t = pe(T.matmul, bank[7][off:off + 64, :], mv[:, kb, h * HD:(h + 1) * HD], PT[:, kb * 512:(kb + 1) * 512],
                               start=(kb == 0), stop=(kb == 1), after=[t3, bank_read[7]], signal=(kb == 1))
                    mem_free[1] = t
                    bank_read[7] = act(A.copy, qmT[off:off + 64, j, :], bank[7][off:off + 64, :], after=[t])
                    yield
            mem_free = [None, None]

            sel_at = [0, P, 3 * P, 6 * P]
            sel_ready = {}

            def choose_keys():
                t = pool(G.tensor_copy, sel[:, 0:P], const("mask_limit"))
                sel_ready[0] = t
                best = small[:, 216:224]
                score_free = None
                for b in range(1, NT):
                    nk = (b + 1) * P
                    score = work[:, 0:nk]
                    for h in range(4):
                        j, off = h // 2, 64 * (h % 2)
                        pb = 4 + h % 2
                        rel = PT[:, (h % 2) * 512:(h % 2) * 512 + nk]
                        t = pe(T.matmul, bank[pb][:, 0:nk], tile(qiT[off:off + 64, j, :], b), kiT[off:off + 64, 0:nk],
                               start=True, stop=True, after=[bank_read[pb]])
                        w = w_idx[:, 4 * b + h:4 * b + h + 1]
                        t = dve(V.tensor_scalar, score if h == 0 else rel, bank[pb][:, 0:nk], 0.0, w, ALU.max, ALU.mult,
                                after=[t, mem_free, score_free])
                        bank_read[pb] = t
                        if h:
                            t = dve(V.tensor_tensor, score, score, rel, ALU.add, after=[t])
                        score_free = t
                    t = dve(V.tensor_tensor, score[:, nk - P:nk], score[:, nk - P:nk], const("mask_limit"), ALU.add, after=[t])
                    yield
                    for r in range(TOPK // 8):
                        t = dve(V.max, best, score, after=[t])
                        t = dve(V.match_replace, score, best, score, TAKEN, after=[t])
                        if r % 2:
                            yield
                    t = dve(V.tensor_scalar, sel[:, sel_at[b]:sel_at[b] + nk], score, 0.9 * TAKEN, NEG, ALU.is_gt, ALU.mult, after=[t])
                    score_free = t
                    sel_ready[b] = t

            def sparse_attention():
                hank_free, bias_free = [None, None], [None, None]
                w_free, pt_free = [None, None], [None, None]
                n = 0
                act.wait(*sel_ready.values())
                for h in range(8):
                    j, off = h // 2, 64 * (h % 2)
                    s = h % 2
                    src = bass.AP(scratch_bias.tensor, h * 640, [[1, P], [1, S]])
                    landed = pool.dma(G.dma_start, hank[:, s, :], src, counter(f"bias_landed{s}"), after=[bias_stored, hank_free[s]])
                    t = pe(T.matmul, bank[4][:, :], const("exchange"), hank[:, s, :], start=True, stop=True, after=[landed, bank_read[4]])
                    hank_free[s] = t
                    bank_read[4] = act(A.copy, bias[:, s, :], bank[4][:, :], after=[t, bias_free[s]])
                    bias_ready = bank_read[4]
                    yield
                    for b in range(NT):
                        nk = (b + 1) * P
                        m = n % 2
                        n += 1
                        W, Pt = work[:, m * 512:m * 512 + nk], PT[:, m * 512:m * 512 + nk]
                        nm, dn = small[:, 224 + 2 * m:225 + 2 * m], small[:, 225 + 2 * m:226 + 2 * m]
                        t = pe(T.matmul, bank[5][:, 0:nk], tile(qaT[off:off + 64, j, :], b), kaT[off:off + 64, 0:nk],
                               start=True, stop=True, after=[bank_read[5]])
                        t = dve(V.scalar_tensor_tensor, W, bank[5][:, 0:nk], HD ** -0.5, bias[:, s, 512 - nk:512], ALU.mult, ALU.add,
                                after=[t, bias_ready, w_free[m], list(sel_ready.values())])
                        bank_read[5] = t
                        t = dve(V.tensor_tensor, W, W, sel[:, sel_at[b]:sel_at[b] + nk], ALU.add, after=[t])
                        if b == NT - 1:
                            bias_free[s] = t
                        t = dve(V.tensor_reduce, nm, W, AX.X, ALU.max, negate=True, after=[t])
                        t = act(A.activation, W, W, ACT.Exp, bias=nm, accum_out=dn, after=[t])
                        t = dve(V.reciprocal, dn, dn, after=[t])
                        t = dve(V.tensor_scalar, W, W, dn, None, ALU.mult, after=[t])
                        yield
                        for k in range(b + 1):
                            t2 = pe(T.transpose, tile(bank[6], k), tile(work[:, m * 512:], k), ident, after=[t, bank_read[6]], signal=(k == b))
                        w_free[m] = t2
                        t3 = act(A.copy, Pt, bank[6][:, 0:nk], after=[t2, pt_free[m]])
                        bank_read[6] = t3
                        yield
                        for k in range(b + 1):
                            t = pe(T.matmul, bank[7][off:off + 64, b * P:(b + 1) * P], va[:, k, :], tile(PT[:, m * 512:], k),
                                   start=(k == 0), stop=(k == b), after=[t3, bank_read[7]], signal=(k == b))
                        pt_free[m] = t
                    bank_read[7] = act(A.copy, qaT[off:off + 64, j, :], bank[7][off:off + 64, :], after=[t])
                    yield

            def state_space():
                tb_free = bt_free = None
                x_free = None
                ct_free = [None, None]
                for pair in range(8):
                    half, cc = pair // 4, pair % 4
                    cb = pair % 2
                    t = pool(G.memset, tb[:, :, :], 0.0, after=[tb_free])
                    tc = pool(G.memset, CT[:, cb, :, :], 0.0, after=[ct_free[cb]])
                    for comp in range(2):
                        for g in range(2):
                            rows = slice(64 * g, 64 * g + 64)
                            c0 = 32 * cc + 16 * g
                            bsrc, csrc = param(("b_re", "b_im")[comp]), param(("c_re", "c_im")[comp])
                            pool(G.tensor_copy, tb[rows, comp, c0:c0 + 16], bsrc[rows, 16 * pair:16 * pair + 16], after=[t])
                            t4 = pool(G.tensor_copy, CT[rows, cb, comp, c0:c0 + 16], csrc[rows, 16 * pair:16 * pair + 16], after=[tc])
                    for comp in range(2):
                        tb_free = pe(T.transpose, tile(bank[4], comp), tb[:, comp, :], ident, after=[t4, bank_read[4]])
                    t = act(A.copy, BT.rearrange("p a b -> p (a b)"), bank[4][:, 0:2 * P], after=[tb_free, bt_free])
                    bank_read[4] = t
                    for comp in range(2):
                        bt_free = pe(T.matmul, bank[5 + comp][:, :], BT[:, comp, :], uT[:, half, :], start=True, stop=True, after=[t, bank_read[5 + comp]])
                        bank_read[5 + comp] = act(A.copy, X[:, 0, comp, 256:], bank[5 + comp][:, :], after=[bt_free, x_free])
                    t = bank_read[6]
                    yield
                    for k in range(9):
                        src, dst = X[:, k % 2], X[:, (k + 1) % 2]
                        sh = 1 << k
                        r, i_, ni = [a[:, pair:pair + 1] for a in powers[k]]
                        now, past = slice(256, 256 + S), slice(256 - sh, 256 - sh + S)
                        ta = dve(V.scalar_tensor_tensor, dst[:, 0, now], src[:, 0, past], r, src[:, 0, now], ALU.mult, ALU.add, after=[t, x_free])
                        tb2 = dve(V.scalar_tensor_tensor, dst[:, 1, now], src[:, 1, past], r, src[:, 1, now], ALU.mult, ALU.add, after=[])
                        dve(V.scalar_tensor_tensor, dst[:, 0, now], src[:, 1, past], ni, dst[:, 0, now], ALU.mult, ALU.add, after=[ta])
                        t = dve(V.scalar_tensor_tensor, dst[:, 1, now], src[:, 0, past], i_, dst[:, 1, now], ALU.mult, ALU.add, after=[tb2])
                        if k % 3 == 2:
                            yield
                    for comp in range(2):
                        x_free = pe(T.matmul, bank[7][:, :], CT[:, cb, comp, :], X[:, 1, comp, 256:], start=(cc == 0 and comp == 0),
                                    stop=(cc == 3 and comp == 1), after=[t, bank_read[7]])
                    ct_free[cb] = x_free
                    if cc == 3:
                        u = uT[:, half, :]
                        z = work[:, half * 512:(half + 1) * 512]
                        t = dve(V.scalar_tensor_tensor, u, u, param("ssm_d", half), bank[7][:, :], ALU.mult, ALU.add, after=[x_free, bt_free, ssm_after])
                        bank_read[7] = t
                        t = dve(V.tensor_tensor, z, u, u, ALU.mult, after=[t])
                        t = dve(V.tensor_scalar, z, z, 0.044715, 1.0, ALU.mult, ALU.add, after=[t])
                        t = dve(V.tensor_tensor, z, z, u, ALU.mult, after=[t])
                        t = act(A.activation, z, z, ACT.Tanh, scale=math.sqrt(2 / math.pi), after=[t])
                        t = dve(V.scalar_tensor_tensor, u, z, 1.0, u, ALU.add, ALU.mult, after=[t])
                        pe_waits.append(t)
                    yield

            ssm_after = []

            def side():
                yield from memory_attention()
                yield from choose_keys()
                yield from sparse_attention()
                ssm_after.append((pe.sem, pe.count))
                yield from state_space()

            main = chain(*[feature_major(I["w_in"], 1476 + c * 512, gate_chunk(c)) for c in range(6)])
            interleave(main, side(), 2.2)
            pe.wait(*pe_waits)
            pe_waits.clear()
            barrier()
            carved[0] = 24 * 512 + 6 * 512 * 2

            merged = gates[:, 16:24, :]
            merge_tok = {}

            def merge(branch, chunk, psum, token):
                if branch == 2:
                    t = dve(V.scalar_tensor_tensor, merged[:, chunk, :], merged[:, chunk, :], 1.0, psum, ALU.add, ALU.mult, after=[token])
                    merge_tok[chunk] = t
                    return t
                g = gates[:, 8 * branch + chunk, :]
                read = dve(V.scalar_tensor_tensor, g, g, float(branch == 0), psum, ALU.add, ALU.mult, after=[token])
                t = dve(V.tensor_tensor, merged[:, chunk, :], merged[:, chunk, :], g, ALU.add, after=[read, merge_tok[chunk]])
                merge_tok[chunk] = t
                return read

            def branch_out(w, src, K, branch):
                for c in range(2):
                    for _ in feature_major(w, c * 512, lambda j, psum, token: merge(branch, 4 * c + j, psum, token), src=src, K=K):
                        pass
            branch_out(I["w_o_m"], qmT, 2, 2)
            branch_out(I["w_o_a"], qaT, 4, 0)
            fold = [None]
            for c in range(2):
                def fold_sigmoid(j, psum, token):
                    z = work[:, (j % 2) * 512:(j % 2 + 1) * 512]
                    read = act(A.activation, z, psum, ACT.Tanh, scale=0.25, after=[token, z_free[j % 2]])
                    t = dve(V.tensor_scalar, z, z, 0.25, 0.25, ALU.mult, ALU.add, after=[read])
                    g = gates[:, 8 + 4 * c + j, :]
                    z_free[j % 2] = dve(V.scalar_tensor_tensor, g, g, 1.0, z, ALU.add, ALU.mult, after=[t])
                    return read
                z_free = [(dve.sem, dve.count)] * 2
                for _ in feature_major(I["w_glu"], D + c * 512, fold_sigmoid, src=uT, K=2):
                    pass
            dve.wait((dve.sem, dve.count))
            branch_out(I["w_glu"], uT, 2, 1)
            pe.wait(*merge_tok.values())
            for c in range(2):
                def add(i, psum, token):
                    dst = x[:, i, c * 512:(c + 1) * 512]
                    return dve(V.scalar_tensor_tensor, dst, psum, 0.5, dst, ALU.mult, ALU.add, after=[token])
                for _ in token_major(I["w_out"], c * 512, 512, tile, add, src=merged):
                    pass
            barrier()

        stored = counter("out_stored")

        def store(after):
            for n in range(NT):
                t = act.dma(A.dma_start, out[n * P:(n + 1) * P, :], x[:, n, :], stored, after=after)
            act.wait(t)

        def final_norm():
            row, tmp = carve(D), carve(2, D)
            row_in = load_row("final", row)
            dve.wait(row_in)
            squares = [None] * NT
            for n in range(NT):
                t = act(A.activation, tmp[:, n % 2, :], x[:, n, :], ACT.Square, accum_out=norm_ss[:, n:n + 1],
                        after=[squares[n - 2] if n > 1 else None])
                squares[n] = t
                t = rstd_of(norm_ss[:, n:n + 1], D, norm_rstd[:, n:n + 1], [t])
                t = dve(V.scalar_tensor_tensor, x[:, n, :], x[:, n, :], norm_rstd[:, n:n + 1], row, ALU.mult, ALU.mult, after=[t])
            return [t]

        def layers():
            finish_layer(I["dil_w_out"], dilated_layer(), "post0")
            if stop_after == "dilated":
                return
            finish_layer(I["diff_w_out"], differential_layer(), "post1")
            if stop_after == "diff":
                return
            feed_forward("ffn1_norm", I["ffn1_w_in"], I["ffn1_w_out"])
            if stop_after == "ffn1":
                return
            hybrid()
            if stop_after == "hybrid":
                return
            feed_forward("ffn2_norm", I["ffn2_w_in"], I["ffn2_w_out"])
            barrier()
            final_norm()

        layers()
        store([(dve.sem, dve.count)])

        block = ctx.enter_context(nc.Block())

        @block.sync
        def _(eng):
            sp.run(eng)

        @block.tensor
        def _(eng):
            pe.run(eng)

        @block.vector
        def _(eng):
            dve.run(eng)

        @block.scalar
        def _(eng):
            act.run(eng)

        @block.gpsimd
        def _(eng):
            pool.run(eng)


def shape_constants():
    c = np.zeros((P, N_CONSTS), np.float32)

    def put(name, value):
        a, b = CONSTS[name]
        c[:value.shape[0], a:b] = value

    put("ident", np.eye(P, dtype=np.float32))
    put("exchange", np.eye(P, dtype=np.float32)[::-1])
    freqs = np.float32(10000.0) ** (-np.arange(0, HD, 2, dtype=np.float32) / np.float32(HD))
    ang = np.arange(S, dtype=np.float32)[:, None] * freqs[None, :].astype(np.float32)
    f = np.arange(P) % 32
    put("cos", np.cos(ang).astype(np.float32).T[f])
    sign = np.where(np.arange(P) % HD < 32, -1.0, 1.0).astype(np.float32)
    put("sin", np.sin(ang).astype(np.float32).T[f] * sign[:, None])
    q, k = np.arange(P)[:, None], np.arange(P)[None, :]
    causal = np.where(k <= q, 0.0, NEG).astype(np.float32)
    kj = np.arange(2 * P)[None, :]
    dist = P + q - kj
    band = np.where((dist >= 0) & (dist <= P), 0.0, NEG).astype(np.float32)
    put("mask_first", np.concatenate([causal, band], 1))
    put("mask_band", np.concatenate([band, band], 1))
    put("mask_causal", np.concatenate([np.zeros((P, 384), np.float32), causal], 1))
    put("mask_16", np.where((k <= q) & (k // 32 == q // 32), 0.0, NEG).astype(np.float32))
    put("mask_limit", np.where((q < 64) & (k >= 64), NEG, 0.0).astype(np.float32))
    rel = np.arange(640) - 127 - 384
    half, exact = BUCKETS // 2, BUCKETS // 4
    n = np.abs(rel)
    nf = np.maximum(n, 1).astype(np.float32)
    large = exact + (np.log(nf / np.float32(exact)) / np.float32(math.log(128 / exact)) * np.float32(half - exact)).astype(np.int32)
    large = np.minimum(large, half - 1)
    bucket = np.where(rel > 0, half, 0) + np.where(n < exact, n, large)
    onehot = (np.arange(BUCKETS)[:, None] == bucket[None, :]).astype(np.float32)
    put("onehot", onehot)
    return c


def kernel(stop_after="", **inputs):
    import concourse.bacc as bacc
    from concourse.bass_utils import run_bass_kernel_spmd as run

    a = {k: np.asarray(v) for k, v in inputs.items()}
    params = np.zeros((P, N_PARAMS), np.float32)

    def put(name, value):
        lo, hi = PARAMS[name]
        params[:value.shape[0], lo:hi] = value

    chunks = lambda v: v.reshape(-1, P).T
    put("norm_pre0", chunks(a["norm_pre"][0]))
    put("norm_pre1", chunks(a["norm_pre"][1]))
    for name in ("ffn1_norm", "mix_norm", "ffn2_norm", "mem_norm"):
        put(name, chunks(a[name + "_2"][0]))
    for name in ("a_q_gain", "a_k_gain", "m_q_gain", "m_k_gain"):
        put(name, np.concatenate([a[name + "_2"][0]] * 2)[:, None])
    put("lam_re", chunks(a["ssm_lambda_re_2"][0].reshape(-1)))
    put("lam_im", chunks(a["ssm_lambda_im_2"][0].reshape(-1)))
    put("log_dt", chunks(np.repeat(a["ssm_log_dt_2"][0], HD)))
    put("ssm_d", chunks(a["ssm_d_2"][0]))
    put("rel_bias", a["rel_bias_2"])
    states = lambda v: v.reshape(8, P, 16).transpose(1, 0, 2).reshape(P, P)
    put("b_re", states(a["ssm_b_re_2"][0].reshape(D, 16)))
    put("b_im", states(a["ssm_b_im_2"][0].reshape(D, 16)))
    put("c_re", states(a["ssm_c_re_2"][0].transpose(0, 2, 1).reshape(D, 16)))
    put("c_im", states(a["ssm_c_im_2"][0].transpose(0, 2, 1).reshape(D, 16)))
    rows = np.concatenate([a["norm_post"][0], a["norm_post"][1], a["final_norm_2"][0], a["diff_subln"][0],
                           a["diff_lambda_q1"][0], a["diff_lambda_k1"][0], a["diff_lambda_q2"][0], a["diff_lambda_k2"][0]])[None]
    given = {"x": a["x"][0], "mem": a["mem_2"][0], "consts": shape_constants(), "params": params, "rows": rows,
             "dil_w_in": a["dil_w_in"][0], "dil_w_out": a["dil_w_out"][0],
             "diff_w_in": a["diff_w_in"][0], "diff_w_out": a["diff_w_out"][0]}
    for name in ("ffn1_w_in", "ffn1_w_out", "w_in", "w_o_a", "w_glu", "w_mem_kv", "w_o_m", "w_out", "ffn2_w_in", "ffn2_w_out"):
        given[name] = a[name + "_2"][0]

    nc = bacc.Bacc("TRN2", target_bir_lowering=False, num_devices=1)
    arrays, I = {}, {}
    for name, v in given.items():
        v = np.ascontiguousarray(v)
        arrays["in_" + name] = v
        I[name] = nc.dram_tensor("in_" + name, v.shape, F32, kind="ExternalInput").ap()
    out = nc.dram_tensor("out_0", (S, D), F32, kind="ExternalOutput").ap()
    program(nc, I, out, stop_after)
    result = run(nc, [arrays], core_ids=[0])
    return result.results[0]["out_0"].reshape(1, S, D)
```

```python
import math
from contextlib import ExitStack

import numpy as np

import concourse.bass as bass
from concourse import mybir

P = 128
D = 1024
S = 512
NT = S // P
KC = D // P
KP = 2
PIECE = KP * 512
RAW = 4
SPLIT = 4
HD = 64
EPS = 1e-6
NEG = -1.0e30
TAKEN = -3.0e38
LAMBDA_INIT = 0.8 - 0.6 * math.exp(-0.3 * 1)

DIL = (1, 4, 16)
DIL_HEADS = 16
ROW = HD + 2

FFN = 2816
FC = FFN // P
MEM = 256
W_IN = 4548
TOPK = min(256, S // 4)
BUCKETS = 32

F32 = mybir.dt.float32
F32R = mybir.dt.float32r
ALU = mybir.AluOpType
ACT = mybir.ActivationFunctionType
AX = mybir.AxisListType

CONSTS = {}
_at = 0
for _name, _n in (("ident", P), ("exchange", P), ("cos", S), ("sin", S), ("mask_first", 384), ("mask_band", 512),
                  ("mask_causal", 512), ("mask_16", P), ("mask_limit", P), ("onehot", 640)):
    CONSTS[_name] = (_at, _at + _n)
    _at += _n
N_CONSTS = _at

PARAMS = {}
_at = 0
for _name, _n in (("a_q_gain", 1), ("a_k_gain", 1), ("m_q_gain", 1), ("m_k_gain", 1),
                  ("lam_re", 8), ("lam_im", 8), ("log_dt", 8), ("ssm_d", 2), ("rel_bias", 8),
                  ("b_re", 2 * P), ("b_im", 2 * P), ("c_re", 2 * P), ("c_im", 2 * P)):
    PARAMS[_name] = (_at, _at + _n)
    _at += _n
N_PARAMS = _at

ROWS = {}
_at = 0
for _name, _n in (("pre0", D), ("post0", D), ("pre1", D), ("post1", D), ("ffn1", D), ("memory", D), ("mix", D), ("ffn2", D),
                  ("final", D), ("subln", P), ("lq1", HD), ("lk1", HD), ("lq2", HD), ("lk2", HD)):
    ROWS[_name] = (_at, _at + _n)
    _at += _n
N_ROWS = _at


UNIT_RATIO, GATE_RATIO = 1.15, 1.0


class Queue:

    def __init__(self, sem):
        self.sem, self.count, self.items, self.waited = sem, 0, [], {}

    def wait(self, *tokens):
        for token in tokens:
            if token is None:
                continue
            if isinstance(token, list):
                self.wait(*token)
                continue
            sem, value = token
            if self.waited.get(sem.name, 0) < value:
                self.waited[sem.name] = value
                self.items.append((None, sem, value, None))

    def __call__(self, method, *args, after=(), signal=True, **kwargs):
        self.wait(*after)
        self.items.append((method, args, kwargs, (self.sem, 1) if signal else None))
        if signal:
            self.count += 1
        return self.sem, self.count

    def dma(self, method, out, in_, counter, after=()):
        self.wait(*after)
        counter[1] += 16
        self.items.append((method, (out, in_), {}, (counter[0], 16)))
        return counter[0], counter[1]

    def run(self, eng):
        for method, a, b, inc in self.items:
            if method is None:
                eng.wait_ge(a, b)
            else:
                ins = method(*a, **b)
                if inc:
                    ins.then_inc(*inc)


HYBRID_RATIO = 1.6


def interleave(main, side, ratio=1.0, finish=True):
    owed = 0.0
    for _ in main:
        owed += ratio
        while owed >= 1.0:
            owed -= 1.0
            next(side, None)
    if finish:
        for _ in side:
            pass


def chain(*streams):
    for stream in streams:
        yield from stream


def program(nc, I, out, stop_after):
    T, V, A, G, SP = nc.tensor, nc.vector, nc.scalar, nc.gpsimd, nc.sync
    ctx = ExitStack()
    with ctx:
        def sb(name, shape, dt=F32):
            return ctx.enter_context(nc.sbuf_tensor(name, shape, dt))

        made_sems = {}

        def sem(name):
            if name not in made_sems:
                made_sems[name] = ctx.enter_context(nc.semaphore(name))
            return made_sems[name]

        consts = sb("consts", [P, N_CONSTS])
        params = sb("params", [P, N_PARAMS])
        raw_ring = sb("raw_ring", [P, RAW, PIECE])
        hi_ring = sb("hi_ring", [P, SPLIT, PIECE], F32R)
        lo_ring = sb("lo_ring", [P, SPLIT, PIECE], F32R)
        x = sb("x", [P, NT, D])
        xh = sb("xh", [P, KC, S], F32R)
        xl = sb("xl", [P, KC, S], F32R)
        small = sb("small", [P, 640])
        minus_half = sb("minus_half", [P, 36])
        FH = 12
        with nc.sbuf_tensor("hidden_hi", [P, FH, S], F32R) as hidden_hi, nc.sbuf_tensor("hidden_lo", [P, FH, S], F32R) as hidden_lo:
            pass
        ARENA = 23304
        arena = sb("arena", [P, ARENA])
        bank = [ctx.enter_context(nc.psum_tensor(f"bank{i}", [P, 512], F32)) for i in range(8)]
        scratch = nc.dram_tensor("scratch_heads", (3, S, DIL_HEADS * ROW), F32, kind="Internal").ap()
        scratch_bias = nc.dram_tensor("scratch_bias", (8, 640), F32, kind="Internal").ap()
        scratch_silu = nc.dram_tensor("scratch_silu", (2, S, D), F32, kind="Internal").ap()
        scratch_gates = nc.dram_tensor("scratch_gates", (24, P, S), F32, kind="Internal").ap()

        def emit(plan):
            def const(name, rows=P):
                a, b = CONSTS[name]
                return consts[0:rows, a:b]

            def param(name, i=None):
                a, b = PARAMS[name]
                return params[:, a:b] if i is None else params[:, a + i:a + i + 1]

            ident = const("ident")

            pe, dve, act, pool = Queue(sem("pe_done")), Queue(sem("dve_done")), Queue(sem("act_done")), Queue(sem("pool_done"))
            sp = Queue(sem("sp_done"))
            piece_landed = [[sem(f"piece_landed{i}"), 0] for i in range(RAW)]
            counters = {}

            def counter(name):
                if name not in counters:
                    counters[name] = [sem(name), 0]
                return counters[name]

            pieces_used = []
            pieces = [] if plan is None else plan
            piece_read = [None] * len(pieces)
            split_read = [None] * SPLIT
            piece_landed_at, piece_parts = [], {}
            n_loaded, n_split, n_seen, n_taken = [0], [0], [0], [0]
            low_part_on = ["dve"]
            bank_read = [None] * 8

            def barrier():
                done = [(q.sem, q.count) for q in (pe, dve, act, pool) if q.count] + [tuple(c) for c in counters.values() if c[1]]
                for q in (pe, dve, act, pool):
                    q.wait(*done)
                carved[0] = 0

            carved = [0]

            def carve(*shape):
                n = int(np.prod(shape))
                a = arena[:, carved[0]:carved[0] + n]
                carved[0] += n
                assert carved[0] <= ARENA, carved[0]
                if len(shape) == 1:
                    return a
                if len(shape) == 2:
                    return a.rearrange("p (a b) -> p a b", a=shape[0])
                if len(shape) == 3:
                    return a.rearrange("p (a b c) -> p a b c", a=shape[0], b=shape[1])
                return a.rearrange("p (a b c d) -> p a b c d", a=shape[0], b=shape[1], c=shape[2])

            def load(p):
                (view, kq, n, _), slot = pieces[p], p % RAW
                dst = raw_ring[:, slot, 0:kq * n].rearrange("p (k n) -> p k n", k=kq)
                read = [piece_read[p - RAW]] if p >= RAW else []
                for i, part in enumerate(view):
                    w = n // len(view)
                    landed = sp.dma(SP.dma_start, dst[:, :, i * w:(i + 1) * w], part, piece_landed[slot], after=read)
                piece_landed_at.append(landed)

            def split(p):
                _, kq, n, _ = pieces[p]
                slot = n_split[0] % SPLIT
                n_split[0] += 1
                raw, hi, lo = raw_ring[:, p % RAW, 0:kq * n], hi_ring[:, slot, 0:kq * n], lo_ring[:, slot, 0:kq * n]
                rounded = act(A.copy, hi, raw, after=[piece_landed_at[p], split_read[slot]])
                if low_part_on[0] == "dve":
                    t = dve(V.tensor_tensor, lo, raw, hi.bitcast(F32), ALU.subtract, after=[rounded])
                else:
                    t = pool(G.tensor_tensor, lo, raw, hi.bitcast(F32), ALU.subtract, after=[rounded])
                piece_read[p] = t
                parts = [a.rearrange("p (k n) -> p k n", k=kq) for a in (hi, lo)]
                piece_parts[p] = parts, t, slot

            def run_ahead(last):
                while True:
                    if n_loaded[0] < len(pieces) and (n_loaded[0] < RAW or piece_read[n_loaded[0] - RAW] is not None):
                        load(n_loaded[0])
                        n_loaded[0] += 1
                        continue
                    if n_seen[0] <= min(last, len(pieces) - 1) and n_seen[0] < n_loaded[0]:
                        if pieces[n_seen[0]][3]:
                            split(n_seen[0])
                        n_seen[0] += 1
                        continue
                    break

            def take(entry):
                p = n_taken[0]
                n_taken[0] += 1
                pieces_used.append(entry)
                if plan is None:
                    pieces.append(entry)
                    piece_read.append(None)
                run_ahead(p)
                _, kq, n, parted = entry
                if parted:
                    parts, t, slot = piece_parts[p]
                    return p, slot, parts, t
                return p, None, [raw_ring[:, p % RAW, 0:kq * n].rearrange("p (k n) -> p k n", k=kq)], piece_landed_at[p]

            def weight(w, k0, kq, c0, n):
                return w[k0 * P:(k0 + kq) * P, c0:c0 + n].rearrange("(k p) n -> p k n", p=P)

            def project(entries, terms, outs, consume, out_cols=S):
                k0 = 0
                total = sum(e[1] for e in entries)
                for first in range(0, len(entries), 2):
                    pair = entries[first:first + 2]
                    taken = [take(e) for e in pair]
                    run_ahead(n_taken[0] + 1)
                    size = sum(e[1] for e in pair)
                    for b, o in enumerate(outs):
                        k = k0
                        for (_, kq, _, _), (_, _, parts, ready_) in zip(pair, taken):
                            for kk in range(kq):
                                products = terms(parts, k, kk, o)
                                for m, (lhsT, rhs) in enumerate(products):
                                    last = m == len(products) - 1
                                    done = pe(T.matmul, bank[b][:, 0:out_cols], lhsT, rhs, start=(k == 0 and m == 0),
                                              stop=(k == total - 1 and last),
                                              after=[ready_, bank_read[b] if k == 0 else None],
                                              signal=(last and kk == kq - 1 and k == k0 + size - 1))
                                k += 1
                        if k == total:
                            bank_read[b] = consume(o, bank[b][:, 0:out_cols], done)
                        if b == len(outs) - 1:
                            for (p, slot, _, _) in taken:
                                if slot is None:
                                    piece_read[p] = done
                                else:
                                    split_read[slot] = done
                        yield
                    k0 += size

            def entries_of(w, c0, n, K, parted, k_first=0):
                return [((weight(w, k_first + k, min(KP, K - k), c0, n),), min(KP, K - k), n, parted) for k in range(0, K, KP)]

            def token_major(w, c0, n, tokens, consume, src=None, K=KC, k_first=0):
                sh, sl = (xh, xl) if src is None else src

                def terms(parts, k, kk, i):
                    wh, wl = parts[0][:, kk, :], parts[1][:, kk, :]
                    h, l = tokens(sh[:, k, :], i), tokens(sl[:, k, :], i)
                    return [(h, wh), (h, wl), (l, wh)]
                return project(entries_of(w, c0, n, K, True, k_first), terms, range(NT), consume, out_cols=n)

            def columns_terms(src):
                def terms(parts, k, kk, j):
                    w = [a[:, kk, j * P:(j + 1) * P] for a in parts]
                    if len(src) == 1:
                        return [(w[0], src[0][:, k, :])]
                    return [(w[0], src[0][:, k, :]), (w[0], src[1][:, k, :]), (w[1], src[0][:, k, :])]
                return terms

            def feature_major(w, c0, consume, src=None, K=KC):
                src = (xh, xl) if src is None else src
                return project(entries_of(w, c0, 512, K, len(src) == 2), columns_terms(src), range(4), consume)

            def run(stream):
                for _ in stream:
                    pass

            def tile(a, i):
                return a[:, i * P:(i + 1) * P]

            def rstd_of(sums, n, dst, after):
                width = sums.shape[-1]
                t = dve(V.tensor_scalar, dst, sums, 1.0 / n, EPS, ALU.mult, ALU.add, after=after)
                return pool(G.tensor_tensor, dst, dst, minus_half[:, 0:width], ALU.pow, after=[t])

            norm_ss = small[:, 0:8]
            norm_rstd = small[:, 8:16]

            def put_parts(src, dst_hi, dst_lo, after, free=None):
                t = act(A.copy, dst_hi, src, after=[after, free])
                return dve(V.tensor_tensor, dst_lo, src, dst_hi.bitcast(F32), ALU.subtract, after=[t])

            def turn_tile(tokens_src, n, first_bank, after):
                for c in range(2):
                    b = first_bank + c
                    for k in range(4):
                        t = pe(T.transpose, tile(bank[b], k), tile(tokens_src, 4 * c + k), ident, after=[after, bank_read[b]], signal=(k == 3))
                    cols = slice(n * P, (n + 1) * P)
                    bank_read[b] = put_parts(bank[b][:, :].rearrange("p (a b) -> p a b", a=4), xh[:, 4 * c:4 * c + 4, cols], xl[:, 4 * c:4 * c + 4, cols], t)
                return bank_read[b], t

            def norm_to_parts(name):
                row, tmp = carve(D), carve(2, D)
                row_in = load_row(name, row)
                free = [None, None]
                for n in range(NT):
                    t = act(A.activation, tmp[:, n % 2, :], x[:, n, :], ACT.Square, accum_out=norm_ss[:, n:n + 1], after=[free[n % 2]])
                    t = rstd_of(norm_ss[:, n:n + 1], D, norm_rstd[:, n:n + 1], [t])
                    t = dve(V.scalar_tensor_tensor, tmp[:, n % 2, :], x[:, n, :], norm_rstd[:, n:n + 1], row, ALU.mult, ALU.mult, after=[t, row_in])
                    t, free[n % 2] = turn_tile(tmp[:, n % 2, :], n, 4 + 2 * (n % 2), t)
                    pe_waits.append(t)
                pe_wait_all()

            def pe_wait_all():
                pe.wait(*pe_waits)
                pe_waits.clear()

            pe_waits = []


            def tanh_half(psum, dst, after):
                return act(A.activation, dst, psum, ACT.Tanh, scale=0.5, after=after)

            def twice_silu(psum, dst, after):
                t = tanh_half(psum, dst, after)
                return dve(V.scalar_tensor_tensor, dst, dst, 1.0, psum, ALU.add, ALU.mult, after=[t])

            def add_normed(Y, Yready, row, tmp):
                squares = [None] * NT
                for n in range(NT):
                    t = act(A.activation, tmp[:, n % 2, :], Y[:, n, :], ACT.Square, accum_out=norm_ss[:, n:n + 1],
                            after=[Yready[n], squares[n - 2] if n > 1 else None])
                    squares[n] = t
                    t = rstd_of(norm_ss[:, n:n + 1], D, norm_rstd[:, n:n + 1], [t])
                    t = dve(V.scalar_tensor_tensor, Y[:, n, :], Y[:, n, :], norm_rstd[:, n:n + 1], row, ALU.mult, ALU.mult, after=[t])
                    t = dve(V.tensor_tensor, x[:, n, :], x[:, n, :], Y[:, n, :], ALU.add, after=[t])
                return t

            first = counter("consts_landed")
            consts_in = sp.dma(SP.dma_start, consts[:, :], I["consts"], first)
            consts_in = sp.dma(SP.dma_start, params[:, :], I["params"], first)
            x_in = [act.dma(A.dma_start, x[:, n, :], I["x"][n * P:(n + 1) * P, :], counter("x_landed")) for n in range(NT)][-1]
            minus_half_set = pool(G.memset, minus_half[:, :], -0.5)
            pool.wait(minus_half_set)
            for q in (pe, dve, act, pool):
                q.wait(consts_in, x_in)

            def load_row(name, dst, after=()):
                a, b = ROWS[name]
                src = I["rows"][0, a:b].partition_broadcast(P)
                return pool.dma(G.dma_start, dst, src, counter("rows_landed"), after=after)

            def gate_panels(w_in, c0, layer, temps):
                free = [None, None]
                m = [0]

                def keep(c):
                    def consume(i, psum, token):
                        b = m[0] % 2
                        m[0] += 1
                        t = twice_silu(psum, temps[:, b, :], [token, free[b]])
                        free[b] = pool.dma(G.dma_start, scratch_silu[layer, i * P:(i + 1) * P, c * 512:(c + 1) * 512], temps[:, b, :],
                                           counter(f"silu_stored{b}"), after=[t])
                        return t
                    return consume
                return chain(*[token_major(w_in, c0 + c * 512, 512, tile, keep(c)) for c in range(2)])

            def dilated_layer():
                QT, KT, VV = carve(2, 4, S), carve(2, 4, S), carve(2, NT, 512)
                rope_a, rope_b = carve(2, S), carve(2, S)
                scores_sb, PT = carve(2, 896), carve(2, 7, P)
                stage = carve(2, NT, 8, ROW)
                used = carved[0]
                carved[0] = 0
                norm_to_parts("pre0")
                carved[0] = used
                gate_temp = carve(2, S)
                dve.wait((pe.sem, pe.count))
                act.wait((dve.sem, dve.count), (pe.sem, pe.count))
                w_in = I["dil_w_in"]
                rope_read = [None, None]
                rope_n = [0]

                def rope(dst, psum, token, g, free):
                    b = rope_n[0] % 2
                    rope_n[0] += 1
                    t1 = dve(V.tensor_tensor, rope_a[:, b, :], psum, const("cos"), ALU.mult, after=[token, rope_read[b]])
                    for quad in range(4):
                        t = act(A.copy, rope_b[32 * quad:32 * quad + 32, b, :], psum[32 * (quad ^ 1):32 * (quad ^ 1) + 32, :],
                                after=[t1, rope_read[b]], signal=(quad == 3))
                    read = t
                    t = dve(V.tensor_tensor, rope_b[:, b, :], rope_b[:, b, :], const("sin"), ALU.mult, after=[t])
                    r = DIL[g]
                    if r == 1:
                        o, a, c = dst, rope_a[:, b, :], rope_b[:, b, :]
                    else:
                        o = dst.rearrange("p (r l) -> p l r", r=r)
                        a = rope_a[:, b, :].rearrange("p (l r) -> p l r", r=r)
                        c = rope_b[:, b, :].rearrange("p (l r) -> p l r", r=r)
                    t = dve(V.tensor_tensor, o, a, c, ALU.add, after=[t, free])
                    rope_read[b] = t
                    return read, t

                def group_tokens(g):
                    def pick(a, i):
                        if DIL[g] == 1:
                            return tile(a, i)
                        return a.rearrange("p (l r) -> p r l", r=4)[:, i, :]
                    return pick

                heads_read = [None, None]
                ready = {}

                def projections(u):
                    g, hf, buf = u // 2, u % 2, u % 2
                    ready[u] = []

                    def rotate(dst):
                        def consume(j, psum, token):
                            read, t = rope(dst[:, buf, j, :], psum, token, g, heads_read[buf])
                            ready[u].append(t)
                            return read
                        return consume

                    def keep_v(i, psum, token):
                        t = act(A.copy, VV[:, buf, i, :], psum, after=[token, heads_read[buf]])
                        ready[u].append(t)
                        return t

                    c = g * D + hf * 512
                    yield from feature_major(w_in, c, rotate(QT))
                    yield from feature_major(w_in, 3 * D + c, rotate(KT))
                    if g < 2:
                        yield from token_major(w_in, 6 * D + c, 512, group_tokens(g), keep_v)
                        return
                    later = []

                    def turn_v(j, psum, token):
                        b = j % 2
                        t = act(A.copy, rope_a[:, b, :].rearrange("p (r l) -> p l r", r=16), psum.rearrange("p (l r) -> p l r", r=16),
                                after=[token, rope_read[b]])

                        def turn():
                            for i in range(NT):
                                t2 = pe(T.transpose, tile(bank[6], i), tile(rope_a[:, b, :], i), ident, after=[t, bank_read[6]], signal=(i == NT - 1))
                            rope_read[b] = t2
                            bank_read[6] = act(A.copy, VV[:, buf, :, j * P:(j + 1) * P], bank[6][:, :].rearrange("p (a b) -> p a b", a=NT),
                                               after=[t2, heads_read[buf]])
                            ready[u].append(bank_read[6])
                        later.append(turn)
                        return t
                    for _ in feature_major(w_in, 6 * D + c, turn_v):
                        while len(later) > 1:
                            later.pop(0)()
                        yield
                    later.pop(0)()

                stage_read = [None, None]
                sc_read, pt_read = [None, None], [None, None]
                heads_n = [0]

                def attention(u):
                    g, hf, buf = u // 2, u % 2, u % 2
                    st = stage[:, buf]
                    if g == 0:
                        blocks = [[(0, 0)], [(1, 0), (2, 1)], [(3, 1), (4, 2)], [(5, 2), (6, 3)]]
                        spans = [(0, 128), (128, 256), (384, 256), (640, 256)]
                    else:
                        blocks = [[(i, i)] for i in range(NT)]
                        spans = [(128 * i, 128) for i in range(NT)]
                    nb = 7 if g == 0 else 4
                    exp_done, first_b = {}, {}

                    def score(hh):
                        j, off = hh // 2, 64 * (hh % 2)
                        q, k = QT[off:off + 64, buf, j, :], KT[off:off + 64, buf, j, :]
                        s = heads_n[0] % 2
                        heads_n[0] += 1
                        first_b[hh] = s
                        sc = scores_sb[:, s, :]
                        if g == 0:
                            for b, tiles_ in ((4, (0, 1)), (5, (2, 3))):
                                base = spans[tiles_[0]][0]
                                for i in tiles_:
                                    a, n = spans[i]
                                    k0 = max(0, i - 1) * P
                                    t = pe(T.matmul, bank[b][:, a - base:a - base + n], tile(q, i), k[:, k0:k0 + n], start=True, stop=True,
                                           after=[bank_read[b], ready[u]], signal=(i == tiles_[1]))
                                n = 384 if b == 4 else 512
                                t = dve(V.scalar_tensor_tensor, sc[:, base:base + n], bank[b][:, 0:n], HD ** -0.5,
                                        const("mask_first" if b == 4 else "mask_band"), ALU.mult, ALU.add, after=[t, sc_read[s]])
                                bank_read[b] = t
                            dve(V.tensor_reduce, st[:, 0:1, hh, ROW - 1], sc[:, 0:P], AX.X, ALU.max, negate=True,
                                after=[t, stage_read[buf]], signal=False)
                            t = dve(V.tensor_reduce, st[:, 1:4, hh, ROW - 1], sc[:, P:896].rearrange("p (a b) -> p a b", a=3),
                                    AX.X, ALU.max, negate=True)
                        else:
                            b = 4 + s
                            for i in range(NT):
                                t = pe(T.matmul, tile(bank[b], i), tile(q, i), tile(k, i), start=True, stop=True,
                                       after=[bank_read[b], ready[u]], signal=(i == NT - 1))
                            m = const("mask_causal")[:, 384:512] if g == 1 else const("mask_16")
                            t = dve(V.scalar_tensor_tensor, sc[:, 0:512].rearrange("p (a b) -> p a b", a=NT),
                                    bank[b][:, :].rearrange("p (a b) -> p a b", a=NT), HD ** -0.5,
                                    m.unsqueeze(1).to_broadcast([P, NT, P]), ALU.mult, ALU.add, after=[t, sc_read[s]])
                            bank_read[b] = t
                            t = dve(V.tensor_reduce, st[:, :, hh, ROW - 1], sc[:, 0:512].rearrange("p (a b) -> p a b", a=NT),
                                    AX.X, ALU.max, negate=True, after=[t, stage_read[buf]])
                        for i in range(NT):
                            a, n = spans[i]
                            t2 = act(A.activation, sc[:, a:a + n], sc[:, a:a + n], ACT.Exp, bias=st[:, i, hh, ROW - 1:ROW],
                                     accum_out=st[:, i, hh, ROW - 2:ROW - 1], after=[t])
                        exp_done[hh] = t2

                    pt_done = {}

                    def turn(hh):
                        s = first_b[hh]
                        for r, lo in enumerate(range(0, nb, 4)):
                            hi = min(nb, lo + 4)
                            for blk in range(lo, hi):
                                t = pe(T.transpose, tile(bank[6], blk - lo), tile(scores_sb[:, s, :], blk), ident,
                                       after=[exp_done[hh], bank_read[6]], signal=(blk == hi - 1))
                            n = (hi - lo) * P
                            dst = PT[:, s, lo:hi, :].rearrange("p a b -> p (a b)")
                            if r == 0:
                                t3 = dve(V.tensor_copy, dst, bank[6][:, 0:n], after=[t, pt_read[s]])
                            else:
                                t3 = act(A.copy, dst, bank[6][:, 0:n], after=[t, pt_read[s]])
                            bank_read[6] = t3
                            pt_done[hh, r] = t3
                        sc_read[s] = t

                    def values(hh):
                        s = first_b[hh]
                        for i in range(NT):
                            for m, (blk, kt) in enumerate(blocks[i]):
                                t = pe(T.matmul, bank[7][:, i * HD:(i + 1) * HD], PT[:, s, blk, :], VV[:, buf, kt, hh * HD:(hh + 1) * HD],
                                       start=(m == 0), stop=(m == len(blocks[i]) - 1),
                                       after=[pt_done[hh, 0], pt_done.get((hh, 1)), bank_read[7]], signal=(i == NT - 1 and m == len(blocks[i]) - 1))
                        pt_read[s] = t
                        bank_read[7] = dve(V.tensor_copy, st[:, :, hh, 0:HD], bank[7][:, 0:NT * HD].rearrange("p (a b) -> p a b", a=NT),
                                           after=[t])
                        return t

                    for step in range(8 + 1):
                        if step < 8:
                            score(step)
                        yield
                        if step >= 1:
                            turn(step - 1)
                            yield
                            t = values(step - 1)
                        yield
                    heads_read[buf] = t
                    done = [bank_read[7], exp_done[7], (act.sem, act.count)]
                    for i in range(NT):
                        rows = scratch[g].rearrange("(l r) c -> r l c", r=DIL[g])
                        if DIL[g] == 16:
                            for rr in range(4):
                                stage_read[buf] = pool.dma(G.dma_start, rows[4 * i + rr, :, hf * 8 * ROW:(hf + 1) * 8 * ROW],
                                                           st[32 * rr:32 * rr + 32, i].rearrange("p a b -> p (a b)"), counter(f"stage_stored{buf}"), after=done)
                        else:
                            dst = rows[i] if DIL[g] == 4 else rows[0, i * P:(i + 1) * P]
                            stage_read[buf] = pool.dma(G.dma_start, dst[:, hf * 8 * ROW:(hf + 1) * 8 * ROW],
                                                       st[:, i].rearrange("p a b -> p (a b)"), counter(f"stage_stored{buf}"), after=done)

                side = iter(())
                for u in range(6):
                    interleave(projections(u), side, UNIT_RATIO)
                    side = attention(u)

                interleave(gate_panels(w_in, 9 * D, 0, gate_temp), side, GATE_RATIO)
                barrier()

                heads = carve(2, 3, DIL_HEADS * ROW)
                mix, gate = carve(2, D), carve(2, D)
                heads_free = [None, None]
                mix_free = [None, None]
                mins, corr, dens = small[:, 16:32], small[:, 32:80], small[:, 80:128]
                stats_free = None
                for n in range(NT):
                    b = n % 2
                    H = heads[:, b].rearrange("p g (h r) -> p g h r", h=DIL_HEADS)
                    landed = pool.dma(G.dma_start, heads[:, b], scratch[:, n * P:(n + 1) * P, :].rearrange("g p c -> p g c"),
                                      counter(f"heads_landed{b}"), after=[heads_free[b]])
                    gate_in = pool.dma(G.dma_start, gate[:, b, :], scratch_silu[0, n * P:(n + 1) * P, :], counter(f"gate_landed{b}"), after=[mix_free[b]])
                    by_g = lambda a: a.rearrange("p (g h) -> p g h", g=3)
                    t = dve(V.tensor_reduce, mins, H[:, :, :, ROW - 1].rearrange("p g h -> p h g"), AX.X, ALU.min, after=[landed, stats_free])
                    t = dve(V.tensor_tensor, by_g(corr), mins.unsqueeze(1).to_broadcast([P, 3, DIL_HEADS]), H[:, :, :, ROW - 1], ALU.subtract, after=[t])
                    t = act(A.activation, corr, corr, ACT.Exp, after=[t])
                    t = dve(V.tensor_tensor, by_g(dens), by_g(corr), H[:, :, :, ROW - 2], ALU.mult, after=[t])
                    t = dve(V.tensor_reduce, mins, dens.rearrange("p (g h) -> p h g", g=3), AX.X, ALU.add, after=[t])
                    t = dve(V.reciprocal, mins, mins, after=[t])
                    t = dve(V.tensor_tensor, by_g(corr), by_g(corr), mins.unsqueeze(1).to_broadcast([P, 3, DIL_HEADS]), ALU.mult, after=[t])
                    for g in range(3):
                        w = corr[:, g * 16:(g + 1) * 16].unsqueeze(2).to_broadcast([P, DIL_HEADS, HD])
                        t = dve(V.tensor_tensor, H[:, g, :, 0:HD], H[:, g, :, 0:HD], w, ALU.mult, after=[t] if g == 0 else [])
                    stats_free = t
                    m = mix[:, b, :].rearrange("p (h r) -> p h r", h=DIL_HEADS)
                    t = dve(V.tensor_tensor, m, H[:, 0, :, 0:HD], H[:, 1, :, 0:HD], ALU.add, after=[t, mix_free[b]])
                    t = dve(V.tensor_tensor, m, m, H[:, 2, :, 0:HD], ALU.add, after=[t])
                    heads_free[b] = t
                    t = dve(V.scalar_tensor_tensor, mix[:, b, :], mix[:, b, :], 0.5, gate[:, b, :], ALU.mult, ALU.mult, after=[t, gate_in])
                    t, mix_free[b] = turn_tile(mix[:, b, :], n, 4 + 2 * b, t)
                    pe_waits.append(t)
                pe_wait_all()

            def project_out(w, Y):
                Yready = [None] * NT

                def keep(c):
                    def consume(i, psum, token):
                        Yready[i] = act(A.copy, Y[:, i, c * 512:(c + 1) * 512], psum, after=[token])
                        return Yready[i]
                    return consume
                for c in range(2):
                    for _ in token_major(w, c * 512, 512, tile, keep(c)):
                        pass
                return Yready

            def finish_layer(w, row_name):
                Y, row, tmp = carve(NT, D), carve(D), carve(2, D)
                row_in = load_row(row_name, row)
                Yready = project_out(w, Y)
                dve.wait(row_in)
                add_normed(Y, Yready, row, tmp)
                barrier()

            def differential_layer():
                QT, KT, VV = carve(2, 4, S), carve(2, 4, S), carve(2, NT, 512)
                rope_a, rope_b = carve(2, S), carve(2, S)
                E, PT = carve(2, 2, S), carve(2, S)
                O = carve(NT, D)
                rowv = carve(P + 4 * HD)
                used = carved[0]
                carved[0] = 0
                norm_to_parts("pre1")
                carved[0] = used
                gate_temp = carve(2, S)
                dve.wait((pe.sem, pe.count))
                act.wait((dve.sem, dve.count), (pe.sem, pe.count))
                stat = small[:, 192:192 + 16]
                neg_lam, lam2 = small[:, 208:209], small[:, 209:211]
                w_in = I["diff_w_in"]
                rows_in = pool.dma(G.dma_start, rowv, I["rows"][0, ROWS["subln"][0]:ROWS["lk2"][1]].partition_broadcast(P), counter("rows_landed"))
                for m in range(2):
                    a = P + 2 * m * HD
                    t = dve(V.tensor_tensor, rowv[:, a:a + HD], rowv[:, a:a + HD], rowv[:, a + HD:a + 2 * HD], ALU.mult, after=[rows_in])
                    t = dve(V.tensor_reduce, lam2[:, m:m + 1], rowv[:, a:a + HD], AX.X, ALU.add, after=[t])
                t = act(A.activation, lam2, lam2, ACT.Exp, after=[t])
                t = dve(V.tensor_tensor, neg_lam, lam2[:, 1:2], lam2[:, 0:1], ALU.subtract, after=[t])
                t = dve(V.tensor_scalar, neg_lam, neg_lam, -LAMBDA_INIT, None, ALU.add, after=[t])
                t = dve(V.tensor_scalar, rowv[:, 0:P], rowv[:, 0:P], 0.5 * (1.0 - LAMBDA_INIT), None, ALU.mult, after=[t])
                dve.wait(t)

                rope_read, rope_n, heads_read, ready = [None, None], [0], [None, None], {}

                def projections(u):
                    buf = u % 2
                    ready[u] = []

                    def rotate(dst):
                        def consume(j, psum, token):
                            b = rope_n[0] % 2
                            rope_n[0] += 1
                            t1 = dve(V.tensor_tensor, rope_a[:, b, :], psum, const("cos"), ALU.mult, after=[token, rope_read[b]])
                            for quad in range(4):
                                read = act(A.copy, rope_b[32 * quad:32 * quad + 32, b, :], psum[32 * (quad ^ 1):32 * (quad ^ 1) + 32, :],
                                           after=[t1, rope_read[b]], signal=(quad == 3))
                            t = dve(V.tensor_tensor, rope_b[:, b, :], rope_b[:, b, :], const("sin"), ALU.mult, after=[read])
                            t = dve(V.tensor_tensor, dst[:, buf, j, :], rope_a[:, b, :], rope_b[:, b, :], ALU.add, after=[t, heads_read[buf]])
                            rope_read[b] = t
                            ready[u].append(t)
                            return read
                        return consume

                    def keep_v(i, psum, token):
                        t = act(A.copy, VV[:, buf, i, :], psum, after=[token, heads_read[buf]])
                        ready[u].append(t)
                        return t

                    yield from feature_major(w_in, u * 512, rotate(QT))
                    yield from feature_major(w_in, D + u * 512, rotate(KT))
                    yield from token_major(w_in, 2 * D + u * 512, 512, tile, keep_v)

                e_read, pt_read = [None, None], [None, None]

                def attention(u):
                    buf = u % 2
                    jobs = [(hh, i) for hh in range(4) for i in range(NT)]
                    made, turned = {}, {}

                    def score(n):
                        hh, i = jobs[n]
                        s, nk = n % 2, (i + 1) * P
                        mx, den = stat[:, 4 * s:4 * s + 2], stat[:, 4 * s + 2:4 * s + 4]
                        for c in range(2):
                            off = 64 * c
                            t = pe(T.matmul, bank[4 + c][:, 0:nk], tile(QT[off:off + 64, buf, hh, :], i), KT[off:off + 64, buf, hh, 0:nk],
                                   start=True, stop=True, after=[bank_read[4 + c], ready[u]])
                            t = dve(V.scalar_tensor_tensor, E[:, s, c, 0:nk], bank[4 + c][:, 0:nk], HD ** -0.5,
                                    const("mask_causal")[:, 384 - i * P:512], ALU.mult, ALU.add, after=[t, e_read[s]])
                            bank_read[4 + c] = t
                        t = dve(V.tensor_reduce, mx, E[:, s, :, 0:nk], AX.X, ALU.max, negate=True, after=[t])
                        for c in range(2):
                            t2 = act(A.activation, E[:, s, c, 0:nk], E[:, s, c, 0:nk], ACT.Exp, bias=mx[:, c:c + 1],
                                     accum_out=den[:, c:c + 1], after=[t])
                        made[n] = t2

                    def combine(n):
                        hh, i = jobs[n]
                        s, nk = n % 2, (i + 1) * P
                        den = stat[:, 4 * s + 2:4 * s + 4]
                        t = dve(V.reciprocal, den, den, after=[made[n]])
                        t = dve(V.tensor_scalar, E[:, s, 0, 0:nk], E[:, s, 0, 0:nk], den[:, 0:1], None, ALU.mult, after=[t])
                        t = dve(V.tensor_scalar, den[:, 1:2], den[:, 1:2], neg_lam, None, ALU.mult, after=[t])
                        t = dve(V.scalar_tensor_tensor, E[:, s, 0, 0:nk], E[:, s, 1, 0:nk], den[:, 1:2], E[:, s, 0, 0:nk], ALU.mult, ALU.add, after=[t])
                        for k in range(i + 1):
                            t2 = pe(T.transpose, tile(bank[6], k), tile(E[:, s, 0, :], k), ident, after=[t, bank_read[6]], signal=(k == i))
                        e_read[s] = t2
                        bank_read[6] = act(A.copy, PT[:, s, 0:nk], bank[6][:, 0:nk], after=[t2, pt_read[s]])
                        turned[n] = bank_read[6]

                    def values(n):
                        hh, i = jobs[n]
                        s = n % 2
                        for k in range(i + 1):
                            t = pe(T.matmul, tile(bank[7], i), tile(PT[:, s, :], k), VV[:, buf, k, hh * P:(hh + 1) * P],
                                   start=(k == 0), stop=(k == i), after=[turned[n], bank_read[7]], signal=(k == i))
                        pt_read[s] = t
                        if i == NT - 1:
                            h = 4 * u + hh
                            bank_read[7] = act(A.copy, O[:, :, h * P:(h + 1) * P], bank[7][:, :].rearrange("p (a b) -> p a b", a=NT), after=[t])
                        return t

                    for n in range(len(jobs) + 1):
                        if n < len(jobs):
                            score(n)
                        if n >= 1:
                            combine(n - 1)
                            yield
                            t = values(n - 1)
                        yield
                    heads_read[buf] = t

                side = iter(())
                for u in range(2):
                    interleave(projections(u), side, 1.5)
                    side = attention(u)

                interleave(gate_panels(w_in, 3 * D, 1, gate_temp), side, 2.2)
                barrier()

                carve(3 * 4096 + 2048 + 2048 + 1024)
                O, rowv = carve(NT, D), carve(P + 4 * HD)
                carved[0] = 0
                sq, gate = carve(2, D), carve(NT, D)
                gate_in = pool.dma(G.dma_start, gate, scratch_silu[1].rearrange("(n p) c -> p n c", p=P), counter("gate_landed0"))
                sub = rowv[:, 0:P].unsqueeze(1).to_broadcast([P, 8, P])
                for n in range(NT):
                    on = O[:, n, :].rearrange("p (h d) -> p h d", h=8)
                    ss = small[:, 16 + 8 * n:24 + 8 * n]
                    t = act(A.activation, sq[:, n % 2, :], O[:, n, :], ACT.Square)
                    t = dve(V.tensor_reduce, ss, sq[:, n % 2, :].rearrange("p (h d) -> p h d", h=8), AX.X, ALU.add, after=[t])
                    act.wait(t)
                    t = rstd_of(ss, P, ss, [t])
                    t = dve(V.tensor_tensor, on, on, ss.unsqueeze(2).to_broadcast([P, 8, P]), ALU.mult, after=[t])
                    t = dve(V.tensor_tensor, on, on, sub, ALU.mult, after=[t])
                    t = dve(V.tensor_tensor, O[:, n, :], O[:, n, :], gate[:, n, :], ALU.mult, after=[t, gate_in])
                    t, _ = turn_tile(O[:, n, :], n, 4 + 2 * (n % 2), t)
                    pe_waits.append(t)
                pe_wait_all()

            def feed_forward(name, w_in, w_out, side=iter(())):
                low_part_on[0] = "dve"
                carved[0] = 2 * FH * S
                e, hid = carve(2, S), carve(2, S)
                used = carved[0]
                norm_to_parts(name)
                e_ready, e_free, hid_free = [None, None], [None, None], [None, None]
                for lot, chunks in enumerate((range(0, FH), range(FH, FC))):
                    if lot:
                        act.wait((pe.sem, pe.count))
                        dve.wait((pe.sem, pe.count))
                    for c in range(chunks[0] // 2, chunks[-1] // 2 + 1):
                        def consume(o, psum, token):
                            s = o % 2
                            if o < 2:
                                e_ready[s] = twice_silu(psum, e[:, s, :], [token, e_free[s]])
                                return e_ready[s]
                            t = dve(V.tensor_tensor, hid[:, s, :], e[:, s, :], psum, ALU.mult, after=[token, e_ready[s], hid_free[s]])
                            e_free[s] = t
                            k = 2 * c + s - chunks[0]
                            hid_free[s] = put_parts(hid[:, s, :], hidden_hi[:, k, :], hidden_lo[:, k, :], t)
                            pe_waits.append(hid_free[s])
                            return t
                        entries = [((weight(w_in, k, KP, c * 256, 256), weight(w_in, k, KP, FFN + c * 256, 256)), KP, 512, True)
                                   for k in range(0, KC, KP)]
                        for _ in project(entries, columns_terms((xh, xl)), range(4), consume):
                            next(side, None)
                    pe_wait_all()
                    for c in range(2):
                        def add(i, psum, token):
                            dst = x[:, i, c * 512:(c + 1) * 512]
                            return dve(V.scalar_tensor_tensor, dst, psum, 0.25, dst, ALU.mult, ALU.add, after=[token, (dve.sem, dve.count)])
                        run(token_major(w_out, c * 512, 512, tile, add, src=(hidden_hi, hidden_lo), K=len(chunks), k_first=chunks[0]))
                run(side)
                barrier()

            KEPT = 2 * MEM + 2 * MEM
            kept = arena[:, ARENA - KEPT:ARENA]
            mkT = kept[:, 0:2 * MEM].rearrange("p (a b) -> p a b", a=2)
            mv = kept[:, 2 * MEM:KEPT].rearrange("p (a b) -> p a b", a=2)
            norm_stat = small[:, 128:192]
            coef = small[:, 256:640]
            c8 = lambda i: coef[:, 8 * i:8 * i + 8]
            powers = [(c8(10 + 3 * k), c8(11 + 3 * k), c8(12 + 3 * k)) for k in range(9)]
            bias_stored = [None]

            def norm_heads(a, heads, stat, tmp, after):
                t = dve(V.tensor_tensor, tmp, a, a, ALU.mult, after=after)
                t = dve(V.tensor_reduce, stat, tmp.rearrange("p (h d) -> p h d", h=heads), AX.X, ALU.add, after=[t])
                t = rstd_of(stat, HD, stat, [t])
                a3 = a.rearrange("p (h d) -> p h d", h=heads)
                return dve(V.tensor_tensor, a3, a3, stat.unsqueeze(2).to_broadcast([P, heads, HD]), ALU.mult, after=[t])

            def turn_chunks(sources, dst, b, scale=None, tiles=NT):
                for n in range(tiles):
                    t = pe(T.transpose, tile(bank[b], n), sources(n), ident, after=[bank_read[b]], signal=(n == tiles - 1))
                if scale is None:
                    bank_read[b] = act(A.copy, dst, bank[b][:, 0:tiles * P], after=[t])
                else:
                    bank_read[b] = act(A.activation, dst, bank[b][:, 0:tiles * P], ACT.Copy, scale=scale, after=[t])
                return bank_read[b]

            def memory_keys_values():
                carved[0] = 2 * FH * S + 4 * S
                mem, row, tmp = carve(2, D), carve(D), carve(D)
                memT, kv = carve(KC, MEM), carve(512)
                assert carved[0] <= ARENA - KEPT
                mem_in = pool.dma(G.dma_start, mem, I["mem"].rearrange("(n p) c -> p n c", p=P), counter("mem_landed"), after=[(pe.sem, pe.count)])
                row_in = load_row("memory", row, after=[(pe.sem, pe.count)])
                act.wait((pe.sem, pe.count))
                for n in range(2):
                    stat = small[:, 240 + 2 * n:241 + 2 * n]
                    t = act(A.activation, tmp, mem[:, n, :], ACT.Square, accum_out=stat, after=[mem_in, (act.sem, act.count)])
                    t = rstd_of(stat, D, stat, [t])
                    t = dve(V.scalar_tensor_tensor, mem[:, n, :], mem[:, n, :], stat, row, ALU.mult, ALU.mult, after=[t, row_in])
                    for c in range(2):
                        yield
                        b = 4 + 2 * n + c
                        for k in range(4):
                            t2 = pe(T.transpose, tile(bank[b], k), tile(mem[:, n, :], 4 * c + k), ident, after=[t, bank_read[b]], signal=(k == 3))
                        bank_read[b] = act(A.copy, memT[:, 4 * c:4 * c + 4, n * P:(n + 1) * P], bank[b][:, :].rearrange("p (a b) -> p a b", a=4), after=[t2])
                memT_ready = [bank_read[b] for b in range(4, 8)]
                for first in range(0, KC, KP):
                    p, _, (w,), landed = take(((weight(I["w_mem_kv"], first, KP, 0, 512),), KP, 512, False))
                    for n in range(2):
                        for kk in range(KP):
                            k = first + kk
                            t = pe(T.matmul, bank[4 + n][:, :], tile(memT[:, k, :], n), w[:, kk, :], start=(k == 0), stop=(k == KC - 1),
                                   after=[landed, memT_ready], signal=(kk == KP - 1))
                    piece_read[p] = t
                    yield
                for n in range(2):
                    t = act(A.copy, kv, bank[4 + n][:, :], after=[t, (dve.sem, dve.count), (pe.sem, pe.count)])
                    bank_read[4 + n] = t
                    dve(V.tensor_copy, mv[:, n, :], kv[:, 256:512], after=[t])
                    t = norm_heads(kv[:, 0:256], 4, norm_stat[:, 4 * n:4 * n + 4], tmp[:, 0:256], [t])
                    yield
                    yield
                    for j in range(2):
                        t2 = pe(T.transpose, tile(bank[6], j), tile(kv, j), ident, after=[t, bank_read[6]])
                    bank_read[6] = act(A.activation, mkT[:, :, n * P:(n + 1) * P], bank[6][:, 0:2 * P].rearrange("p (a b) -> p a b", a=2),
                                       ACT.Copy, scale=param("m_k_gain"), after=[t2])
                    yield

            def coefficients():
                carved[0] = 2 * FH * S + 4 * S
                coef_tmp, beta = carve(768), carve(640)
                act.wait((pe.sem, pe.count), (dve.sem, dve.count))
                for lo, hi, b in ((0, 512, 4), (512, 640, 5)):
                    t = pe(T.matmul, bank[b][0:8, 0:hi - lo], params[0:BUCKETS, PARAMS["rel_bias"][0]:PARAMS["rel_bias"][1]],
                           const("onehot", BUCKETS)[:, lo:hi], start=True, stop=True, after=[bank_read[b]])
                    t = act(A.copy, beta[0:8, lo:hi], bank[b][0:8, 0:hi - lo], after=[t])
                    bank_read[b] = t
                bias_stored[0] = pool.dma(G.dma_start, scratch_bias, beta[0:8, 0:640], counter("bias_stored"), after=[t])
                yield
                dt, th, mag, cs, sn, tmp1, tmp2, den, fr, fi = [c8(i) for i in range(10)]
                lr, li = param("lam_re"), param("lam_im")
                last = [None]

                def v(method, *args, **kw):
                    last[0] = dve(method, *args, after=[last[0]], **kw)

                last[0] = act(A.activation, dt, param("log_dt"), ACT.Exp)
                v(V.tensor_tensor, th, li, dt, ALU.mult)
                v(V.tensor_tensor, tmp1, lr, dt, ALU.mult)
                last[0] = act(A.activation, mag, tmp1, ACT.Exp, after=[last[0]])
                MAGIC = 1.5 * 2.0 ** 23
                C1 = 6.28125
                C2 = float(np.float32(2 * math.pi - C1))
                C3 = 2 * math.pi - C1 - C2
                for dst, turn_part, shift in ((sn, 0.0, 0.0), (cs, 0.25, math.pi / 2)):
                    v(V.tensor_scalar, tmp1, th, 1 / (2 * math.pi), turn_part, ALU.mult, ALU.add)
                    v(V.tensor_scalar, tmp1, tmp1, MAGIC, None, ALU.add)
                    v(V.tensor_scalar, tmp1, tmp1, -MAGIC, None, ALU.add)
                    v(V.scalar_tensor_tensor, tmp2, tmp1, -C1, th, ALU.mult, ALU.add)
                    v(V.scalar_tensor_tensor, tmp2, tmp1, -C2, tmp2, ALU.mult, ALU.add)
                    v(V.scalar_tensor_tensor, tmp2, tmp1, -C3, tmp2, ALU.mult, ALU.add)
                    v(V.tensor_scalar, tmp2, tmp2, shift, None, ALU.add)
                    v(V.tensor_scalar, tmp2, tmp2, 3.1415925, -3.1415925, ALU.min, ALU.max)
                    last[0] = act(A.activation, dst, tmp2, ACT.Sin, after=[last[0]])
                ar, ai, nai = powers[0]
                v(V.tensor_tensor, ar, mag, cs, ALU.mult)
                v(V.tensor_tensor, ai, mag, sn, ALU.mult)
                v(V.tensor_tensor, den, lr, lr, ALU.mult)
                v(V.tensor_tensor, tmp1, li, li, ALU.mult)
                v(V.tensor_tensor, den, den, tmp1, ALU.add)
                v(V.reciprocal, den, den)
                v(V.tensor_scalar, cs, ar, -1.0, None, ALU.add)
                v(V.tensor_tensor, tmp1, cs, lr, ALU.mult)
                v(V.tensor_tensor, tmp2, ai, li, ALU.mult)
                v(V.tensor_tensor, fr, tmp1, tmp2, ALU.add)
                v(V.tensor_tensor, fr, fr, den, ALU.mult)
                v(V.tensor_tensor, tmp1, ai, lr, ALU.mult)
                v(V.tensor_tensor, tmp2, cs, li, ALU.mult)
                v(V.tensor_tensor, fi, tmp1, tmp2, ALU.subtract)
                v(V.tensor_tensor, fi, fi, den, ALU.mult)
                for k in range(9):
                    r, i_, ni = powers[k]
                    v(V.tensor_scalar, ni, i_, -1.0, None, ALU.mult)
                    if k < 8:
                        r2, i2, _ = powers[k + 1]
                        v(V.tensor_tensor, tmp1, r, r, ALU.mult)
                        v(V.tensor_tensor, tmp2, i_, i_, ALU.mult)
                        v(V.tensor_tensor, r2, tmp1, tmp2, ALU.subtract)
                        v(V.tensor_tensor, tmp1, r, i_, ALU.mult)
                        v(V.tensor_scalar, i2, tmp1, 2.0, None, ALU.mult)
                by_pair = lambda a: a.rearrange("p (g c) -> p g c", g=8)
                bcol = lambda a: a.unsqueeze(2).to_broadcast([P, 8, 32])
                br, bi = param("b_re"), param("b_im")
                t1, t2, t3 = coef_tmp[:, 0:256], coef_tmp[:, 256:512], coef_tmp[:, 512:768]
                v(V.tensor_tensor, by_pair(t1), by_pair(br), bcol(fr), ALU.mult)
                v(V.tensor_tensor, by_pair(t2), by_pair(bi), bcol(fi), ALU.mult)
                v(V.tensor_tensor, t3, t1, t2, ALU.subtract)
                v(V.tensor_tensor, by_pair(t1), by_pair(bi), bcol(fr), ALU.mult)
                v(V.tensor_tensor, by_pair(t2), by_pair(br), bcol(fi), ALU.mult)
                v(V.tensor_tensor, t1, t1, t2, ALU.add)
                v(V.tensor_scalar, param("c_im"), param("c_im"), -1.0, None, ALU.mult)
                yield
                for comp, fb in ((0, t3), (1, t1)):
                    for half in range(2):
                        t = pe(T.transpose, tile(bank[4 + comp], half), tile(fb, half), ident, after=[last[0], bank_read[4 + comp]])
                    bank_read[4 + comp] = act(A.copy, (br, bi)[comp], bank[4 + comp][:, 0:2 * P], after=[t])
                pe.wait(bank_read[4], bank_read[5])

            def before_hybrid():
                yield from memory_keys_values()
                yield from coefficients()

            def hybrid():
                low_part_on[0] = "pool"
                proj_u, proj_k, proj_q = carve(NT, 512), carve(NT, 452), carve(NT, 512)
                kdup = carve(NT, 2, P)
                gate_temp = carve(2, S)
                qaT, kaT, kiT, qiT = carve(4, S), carve(S), carve(S), carve(2, S)
                uT, qmT = carve(2, S), carve(2, S)
                sel = carve(1280)
                work, PT = carve(1024), carve(1024)
                hank, bias = carve(S), carve(S)
                X = carve(2, 2, 256 + S)
                assert carved[0] <= ARENA - KEPT, carved[0] - ARENA + KEPT
                carved_here = carved[0]
                carved[0] = 0
                norm_to_parts("mix")
                dve.wait((pe.sem, pe.count))
                act.wait((dve.sem, dve.count), (pe.sem, pe.count))
                pool.wait((pe.sem, pe.count))
                pool(G.memset, X[:, :, :, 0:256], 0.0)

                def keep(dst):
                    ready_ = []

                    def consume(i, psum, token):
                        ready_.append(act(A.copy, dst[:, i, :], psum, after=[token]))
                        return ready_[-1]
                    return consume, ready_

                def narrow(c0, n, dst):
                    consume, ready_ = keep(dst)
                    yield from token_major(I["w_in"], c0, n, tile, consume)
                    dve.wait(ready_)
                    pe.wait(ready_)

                w_idx = small[:, 192:208]

                def turn_u():
                    for j in range(2):
                        turn_chunks(lambda n: proj_u[:, n, j * P:(j + 1) * P], uT[:, j, :], 4 + j)
                        yield
                    for i in range(NT):
                        t = norm_heads(proj_u[:, i, 256:512], 4, norm_stat[:, 16 + 4 * (i % 2):20 + 4 * (i % 2)], PT[:, 0:256], [(dve.sem, dve.count)])
                        yield
                    pe.wait(t)
                    for j in range(2):
                        turn_chunks(lambda n: proj_u[:, n, 256 + j * P:256 + (j + 1) * P], qmT[:, j, :], 6 + j, param("m_q_gain"))
                        yield

                def turn_k():
                    for i in range(NT):
                        t = norm_heads(proj_k[:, i, 0:HD], 1, norm_stat[:, 32:33], PT[:, 0:HD], [(dve.sem, dve.count)])
                        for m, c0 in ((0, 0), (1, 384)):
                            for half in range(2):
                                t = dve(V.tensor_copy, kdup[:, i, m, half * HD:(half + 1) * HD], proj_k[:, i, c0:c0 + HD], after=[t])
                        yield
                    t = dve(V.tensor_scalar, w_idx.rearrange("p (n h) -> p n h", n=NT), proj_k[:, :, 448:452], HD ** -0.5 * 4 ** -0.5, None, ALU.mult)
                    pe.wait(t)
                    turn_chunks(lambda n: kdup[:, n, 1, :], kiT, 5)
                    turn_chunks(lambda n: kdup[:, n, 0, :], kaT, 6, param("a_k_gain"))
                    yield
                    for j in range(2):
                        turn_chunks(lambda n: proj_k[:, n, 128 + j * P:128 + (j + 1) * P], qiT[:, j, :], 6 + j)
                        yield

                def turn_q():
                    for i in range(NT):
                        t = norm_heads(proj_q[:, i, :], 8, norm_stat[:, 48:56], PT[:, 0:512], [(dve.sem, dve.count)])
                        yield
                    pe.wait(t)
                    for j in range(4):
                        turn_chunks(lambda n: proj_q[:, n, j * P:(j + 1) * P], qaT[:, j, :], 5 + j % 2, param("a_q_gain"))
                        yield

                gate_free = [None, None]
                gate_n = [0]

                def gate_chunk(c):
                    def consume(j, psum, token):
                        b = gate_n[0] % 2
                        gate_n[0] += 1
                        t = tanh_half(psum, gate_temp[:, b, :], [token, gate_free[b]])
                        gate_free[b] = act.dma(A.dma_start, scratch_gates[4 * c + j], gate_temp[:, b, :], counter(f"gate_stored{b}"), after=[t])
                        return t
                    return consume

                mem_free = [None, None]

                def memory_attention():
                    for h in range(4):
                        j, off = h // 2, 64 * (h % 2)
                        q, k = qmT[off:off + 64, j, :], mkT[off:off + 64, j, :]
                        nm, dn = small[:, 208:212], small[:, 212:216]
                        W = work.rearrange("p (n k) -> p n k", n=NT)
                        for b in range(2):
                            for i in (2 * b, 2 * b + 1):
                                t = pe(T.matmul, bank[5][:, (i % 2) * MEM:(i % 2 + 1) * MEM], tile(q, i), k, start=True, stop=True,
                                       after=[bank_read[5]], signal=(i % 2 == 1))
                            t = act(A.activation, work[:, b * 512:(b + 1) * 512], bank[5][:, :], ACT.Copy, scale=HD ** -0.5, after=[t, mem_free[0]])
                            bank_read[5] = t
                        yield
                        t = dve(V.tensor_reduce, nm, W, AX.X, ALU.max, negate=True, after=[t])
                        for i in range(NT):
                            t2 = act(A.activation, W[:, i, :], W[:, i, :], ACT.Exp, bias=nm[:, i:i + 1], accum_out=dn[:, i:i + 1], after=[t])
                        t = dve(V.reciprocal, dn, dn, after=[t2])
                        t = dve(V.tensor_tensor, W, W, dn.unsqueeze(2).to_broadcast([P, NT, MEM]), ALU.mult, after=[t])
                        yield
                        for kb in range(2):
                            for i in range(NT):
                                t2 = pe(T.transpose, tile(bank[6], i), W[:, i, kb * P:(kb + 1) * P], ident, after=[t, bank_read[6]], signal=(i == NT - 1))
                            t3 = act(A.copy, PT[:, kb * 512:(kb + 1) * 512], bank[6][:, :], after=[t2, mem_free[1]])
                            bank_read[6] = t3
                        mem_free[0] = t2
                        yield
                        for kb in range(2):
                            t = pe(T.matmul, bank[7][off:off + 64, :], mv[:, kb, h * HD:(h + 1) * HD], PT[:, kb * 512:(kb + 1) * 512],
                                   start=(kb == 0), stop=(kb == 1), after=[t3, bank_read[7]], signal=(kb == 1))
                        mem_free[1] = t
                        bank_read[7] = act(A.copy, qmT[off:off + 64, j, :], bank[7][off:off + 64, :], after=[t])
                        yield
                mem_free = [None, None]

                sel_at = [0, P, 3 * P, 6 * P]
                sel_ready = {}

                def choose_keys():
                    t = pool(G.tensor_copy, sel[:, 0:P], const("mask_limit"))
                    sel_ready[0] = t
                    best = small[:, 216:224]
                    score_free = None
                    for b in range(1, NT):
                        nk = (b + 1) * P
                        score = work[:, 0:nk]
                        for h in range(4):
                            j, off = h // 2, 64 * (h % 2)
                            pb = 5 + h % 2
                            rel = PT[:, (h % 2) * 512:(h % 2) * 512 + nk]
                            t = pe(T.matmul, bank[pb][:, 0:nk], tile(qiT[off:off + 64, j, :], b), kiT[off:off + 64, 0:nk],
                                   start=True, stop=True, after=[bank_read[pb]])
                            w = w_idx[:, 4 * b + h:4 * b + h + 1]
                            t = dve(V.tensor_scalar, score if h == 0 else rel, bank[pb][:, 0:nk], 0.0, w, ALU.max, ALU.mult,
                                    after=[t, mem_free, score_free])
                            bank_read[pb] = t
                            if h:
                                t = dve(V.tensor_tensor, score, score, rel, ALU.add, after=[t])
                            score_free = t
                        t = dve(V.tensor_tensor, score[:, nk - P:nk], score[:, nk - P:nk], const("mask_limit"), ALU.add, after=[t])
                        yield
                        for r in range(TOPK // 8):
                            t = dve(V.max, best, score, after=[t])
                            t = dve(V.match_replace, score, best, score, TAKEN, after=[t])
                            if r % 2:
                                yield
                        t = dve(V.tensor_scalar, sel[:, sel_at[b]:sel_at[b] + nk], score, 0.9 * TAKEN, NEG, ALU.is_gt, ALU.mult, after=[t])
                        score_free = t
                        sel_ready[b] = t

                def sparse_attention():
                    hank_free, bias_free = [None, None], [None, None]
                    w_free, pt_free = [None, None], [None, None]
                    n = 0
                    act.wait(*sel_ready.values())
                    for h in range(8):
                        j, off = h // 2, 64 * (h % 2)
                        s = h % 2
                        src = bass.AP(scratch_bias.tensor, h * 640, [[1, P], [1, S]])
                        landed = pool.dma(G.dma_start, hank, src, counter(f"bias_landed{s}"), after=[bias_stored[0], hank_free[0]])
                        t = pe(T.matmul, bank[6][:, :], const("exchange"), hank, start=True, stop=True, after=[landed, bank_read[6]])
                        hank_free[0] = t
                        bank_read[6] = act(A.copy, bias, bank[6][:, :], after=[t, bias_free[0]])
                        bias_ready = bank_read[6]
                        yield
                        for b in range(NT):
                            nk = (b + 1) * P
                            m = n % 2
                            n += 1
                            W, Pt = work[:, m * 512:m * 512 + nk], PT[:, m * 512:m * 512 + nk]
                            nm, dn = small[:, 224 + 2 * m:225 + 2 * m], small[:, 225 + 2 * m:226 + 2 * m]
                            t = pe(T.matmul, bank[5][:, 0:nk], tile(qaT[off:off + 64, j, :], b), kaT[off:off + 64, 0:nk],
                                   start=True, stop=True, after=[bank_read[5]])
                            t = dve(V.scalar_tensor_tensor, W, bank[5][:, 0:nk], HD ** -0.5, bias[:, 512 - nk:512], ALU.mult, ALU.add,
                                    after=[t, bias_ready, w_free[m], list(sel_ready.values())])
                            bank_read[5] = t
                            t = dve(V.tensor_tensor, W, W, sel[:, sel_at[b]:sel_at[b] + nk], ALU.add, after=[t])
                            if b == NT - 1:
                                bias_free[0] = t
                            t = dve(V.tensor_reduce, nm, W, AX.X, ALU.max, negate=True, after=[t])
                            t = act(A.activation, W, W, ACT.Exp, bias=nm, accum_out=dn, after=[t])
                            t = dve(V.reciprocal, dn, dn, after=[t])
                            t = dve(V.tensor_scalar, W, W, dn, None, ALU.mult, after=[t])
                            yield
                            for k in range(b + 1):
                                t2 = pe(T.transpose, tile(bank[6], k), tile(work[:, m * 512:], k), ident, after=[t, bank_read[6]], signal=(k == b))
                            w_free[m] = t2
                            t3 = act(A.copy, Pt, bank[6][:, 0:nk], after=[t2, pt_free[m]])
                            bank_read[6] = t3
                            yield
                            for k in range(b + 1):
                                t = pe(T.matmul, bank[7][off:off + 64, b * P:(b + 1) * P], proj_k[:, k, HD:2 * HD], tile(PT[:, m * 512:], k),
                                       start=(k == 0), stop=(k == b), after=[t3, bank_read[7]], signal=(k == b))
                            pt_free[m] = t
                        bank_read[7] = act(A.copy, qaT[off:off + 64, j, :], bank[7][off:off + 64, :], after=[t])
                        yield

                def state_space():
                    x_free = y_done = None
                    yT = proj_u[:, 0:2, :]
                    for pair in range(8):
                        half, cc = pair // 4, pair % 4
                        rows = slice(32 * cc, 32 * cc + 32)
                        for comp in range(2):
                            b_pair = tile(param(("b_re", "b_im")[comp]), half)[rows, :]
                            t = pe(T.matmul, bank[4][:, :], b_pair, uT[rows, half, :], start=True, stop=True, after=[bank_read[4]])
                            bank_read[4] = act(A.copy, X[:, 0, comp, 256:], bank[4][:, :], after=[t, x_free, y_done])
                            yield
                        t = bank_read[4]
                        yield
                        for k in range(9):
                            src, dst = X[:, k % 2], X[:, (k + 1) % 2]
                            sh = 1 << k
                            r, i_, ni = [a[:, pair:pair + 1] for a in powers[k]]
                            now, past = slice(256, 256 + S), slice(256 - sh, 256 - sh + S)
                            ta = dve(V.scalar_tensor_tensor, dst[:, 0, now], src[:, 0, past], r, src[:, 0, now], ALU.mult, ALU.add, after=[t, x_free])
                            tb2 = dve(V.scalar_tensor_tensor, dst[:, 1, now], src[:, 1, past], r, src[:, 1, now], ALU.mult, ALU.add, after=[])
                            dve(V.scalar_tensor_tensor, dst[:, 0, now], src[:, 1, past], ni, dst[:, 0, now], ALU.mult, ALU.add, after=[ta])
                            t = dve(V.scalar_tensor_tensor, dst[:, 1, now], src[:, 0, past], i_, dst[:, 1, now], ALU.mult, ALU.add, after=[tb2])
                            yield
                        for comp in range(2):
                            c_pair = param(("c_re", "c_im")[comp])[:, 32 * pair:32 * pair + 32]
                            x_free = pe(T.matmul, bank[4][rows, :], c_pair, X[:, 1, comp, 256:], start=(comp == 0), stop=(comp == 1),
                                        after=[t, bank_read[4]])
                        yield
                        d_col = param("ssm_d", half)
                        y_done = dve(V.scalar_tensor_tensor, yT[rows, half, :], uT[rows, half, :], d_col[rows], bank[4][rows, :], ALU.mult, ALU.add, after=[x_free])
                        bank_read[4] = y_done
                        if cc == 3:
                            y, z = yT[:, half, :], X[:, 0, 0, 256:]
                            t = dve(V.tensor_tensor, z, y, y, ALU.mult, after=[y_done])
                            t = dve(V.tensor_scalar, z, z, 0.044715, 1.0, ALU.mult, ALU.add, after=[t])
                            t = dve(V.tensor_tensor, z, z, y, ALU.mult, after=[t])
                            yield
                            t = act(A.activation, z, z, ACT.Tanh, scale=math.sqrt(2 / math.pi), after=[t])
                            t = dve(V.scalar_tensor_tensor, y, z, 1.0, y, ALU.add, ALU.mult, after=[t])
                            y_done = t
                            pe_waits.append(t)
                        yield

                def heads_stream():
                    yield from memory_attention()
                    yield from choose_keys()
                    yield from turn_q()
                    yield from sparse_attention()

                def both(a, b):
                    live = [a, b]
                    while live:
                        for stream in list(live):
                            try:
                                next(stream)
                            except StopIteration:
                                live.remove(stream)
                        yield

                run(narrow(964, 512, proj_u))
                interleave(narrow(512, 452, proj_k), turn_u(), 1.0)
                scan = state_space()
                interleave(narrow(0, 512, proj_q), both(turn_k(), scan), 1.0, finish=False)
                main = chain(*[feature_major(I["w_in"], 1476 + c * 512, gate_chunk(c)) for c in range(6)])
                interleave(main, both(heads_stream(), scan), HYBRID_RATIO)
                pe_wait_all()
                barrier()

                yT = proj_u[:, 0:2, :]
                carved[0] = 2 * NT * 512 + NT * 452 + NT * 2 * P + 2 * S + 8 * S + 4 * S
                tanhs, folded, z2 = carve(8, S), carve(4, S), carve(2, S)
                merged = arena[:, NT * 512:NT * 512 + KC * S].rearrange("p (a b) -> p a b", a=KC)
                merge_tok = {}
                tanh_free = [None] * 8
                tanh_n = [0]

                def fetch(c):
                    got = []
                    for j in range(4):
                        m = tanh_n[0] % 8
                        tanh_n[0] += 1
                        landed = pool.dma(G.dma_start, tanhs[:, m, :], scratch_gates[4 * c + j], counter(f"tanh_landed{m}"), after=[tanh_free[m]])
                        got.append((m, landed))
                    return got

                def branch_out(w, src, K, branch):
                    for c in range(2):
                        got = fetch(2 * branch + c)

                        def merge(j, psum, token):
                            m, landed = got[j]
                            g, chunk = tanhs[:, m, :], 4 * c + j
                            if branch == 2:
                                t = dve(V.scalar_tensor_tensor, merged[:, chunk, :], g, 1.0, psum, ALU.add, ALU.mult, after=[token, landed])
                                merge_tok[chunk] = tanh_free[m] = t
                                return t
                            read = dve(V.scalar_tensor_tensor, g, g, 1.0, psum, ALU.add, ALU.mult, after=[token, landed])
                            t = dve(V.tensor_tensor, merged[:, chunk, :], merged[:, chunk, :], g, ALU.add, after=[read, merge_tok[chunk]])
                            merge_tok[chunk] = tanh_free[m] = t
                            return read
                        run(feature_major(w, c * 512, merge, src=(src,), K=K))
                branch_out(I["w_o_m"], qmT, 2, 2)
                branch_out(I["w_o_a"], qaT, 4, 0)
                for c in range(2):
                    got = fetch(2 + c)
                    fold_done = {}

                    def fold_sigmoid(j, psum, token):
                        m, landed = got[j]
                        z = z2[:, j % 2, :]
                        read = act(A.activation, z, psum, ACT.Tanh, scale=0.25, after=[token, z_free[j % 2]])
                        t = dve(V.tensor_scalar, z, z, 0.25, 0.25, ALU.mult, ALU.add, after=[read])
                        t = dve(V.scalar_tensor_tensor, folded[:, j, :], tanhs[:, m, :], 1.0, z, ALU.add, ALU.mult, after=[t, landed])
                        z_free[j % 2] = tanh_free[m] = fold_done[j] = t
                        return read

                    def merge_glu(j, psum, token):
                        chunk = 4 * c + j
                        read = dve(V.tensor_tensor, folded[:, j, :], folded[:, j, :], psum, ALU.mult, after=[token, fold_done[j]])
                        t = dve(V.tensor_tensor, merged[:, chunk, :], merged[:, chunk, :], folded[:, j, :], ALU.add, after=[read, merge_tok[chunk]])
                        pe_waits.append(put_parts(merged[:, chunk, :], xh[:, chunk, :], xl[:, chunk, :], t))
                        return read
                    z_free = [(dve.sem, dve.count)] * 2
                    run(feature_major(I["w_glu"], D + c * 512, fold_sigmoid, src=(yT,), K=2))
                    run(feature_major(I["w_glu"], c * 512, merge_glu, src=(yT,), K=2))
                pe_wait_all()
                low_part_on[0] = "dve"
                for c in range(2):
                    def add(i, psum, token):
                        dst = x[:, i, c * 512:(c + 1) * 512]
                        return dve(V.scalar_tensor_tensor, dst, psum, 0.5, dst, ALU.mult, ALU.add, after=[token])
                    run(token_major(I["w_out"], c * 512, 512, tile, add))
                barrier()

            stored = counter("out_stored")

            def store(after):
                for n in range(NT):
                    t = act.dma(A.dma_start, out[n * P:(n + 1) * P, :], x[:, n, :], stored, after=after)
                act.wait(t)

            def final_norm():
                row, tmp = carve(D), carve(2, D)
                row_in = load_row("final", row)
                dve.wait(row_in)
                squares = [None] * NT
                for n in range(NT):
                    t = act(A.activation, tmp[:, n % 2, :], x[:, n, :], ACT.Square, accum_out=norm_ss[:, n:n + 1],
                            after=[squares[n - 2] if n > 1 else None])
                    squares[n] = t
                    t = rstd_of(norm_ss[:, n:n + 1], D, norm_rstd[:, n:n + 1], [t])
                    t = dve(V.scalar_tensor_tensor, x[:, n, :], x[:, n, :], norm_rstd[:, n:n + 1], row, ALU.mult, ALU.mult, after=[t])
                return [t]

            def layers():
                dilated_layer()
                finish_layer(I["dil_w_out"], "post0")
                if stop_after == "dilated":
                    return
                differential_layer()
                finish_layer(I["diff_w_out"], "post1")
                if stop_after == "diff":
                    return
                feed_forward("ffn1", I["ffn1_w_in"], I["ffn1_w_out"], before_hybrid())
                if stop_after == "ffn1":
                    return
                hybrid()
                if stop_after == "hybrid":
                    return
                feed_forward("ffn2", I["ffn2_w_in"], I["ffn2_w_out"])
                barrier()
                final_norm()

            layers()
            store([(dve.sem, dve.count)])
            return pieces_used if plan is None else (pe, dve, act, pool, sp)

        plan = emit(None)
        queues = emit(plan)

        block = ctx.enter_context(nc.Block())

        @block.sync
        def _(eng):
            queues[4].run(eng)

        @block.tensor
        def _(eng):
            queues[0].run(eng)

        @block.vector
        def _(eng):
            queues[1].run(eng)

        @block.scalar
        def _(eng):
            queues[2].run(eng)

        @block.gpsimd
        def _(eng):
            queues[3].run(eng)


def shape_constants():
    c = np.zeros((P, N_CONSTS), np.float32)

    def put(name, value):
        a, b = CONSTS[name]
        c[:value.shape[0], a:b] = value

    put("ident", np.eye(P, dtype=np.float32))
    put("exchange", np.eye(P, dtype=np.float32)[::-1])
    freqs = np.float32(10000.0) ** (-np.arange(0, HD, 2, dtype=np.float32) / np.float32(HD))
    ang = np.arange(S, dtype=np.float32)[:, None] * freqs[None, :].astype(np.float32)
    f = np.arange(P) % 32
    put("cos", np.cos(ang).astype(np.float32).T[f])
    sign = np.where(np.arange(P) % HD < 32, -1.0, 1.0).astype(np.float32)
    put("sin", np.sin(ang).astype(np.float32).T[f] * sign[:, None])
    q, k = np.arange(P)[:, None], np.arange(P)[None, :]
    causal = np.where(k <= q, 0.0, NEG).astype(np.float32)
    kj = np.arange(2 * P)[None, :]
    dist = P + q - kj
    band = np.where((dist >= 0) & (dist <= P), 0.0, NEG).astype(np.float32)
    put("mask_first", np.concatenate([causal, band], 1))
    put("mask_band", np.concatenate([band, band], 1))
    put("mask_causal", np.concatenate([np.zeros((P, 384), np.float32), causal], 1))
    put("mask_16", np.where((k <= q) & (k // 32 == q // 32), 0.0, NEG).astype(np.float32))
    put("mask_limit", np.where((q < 64) & (k >= 64), NEG, 0.0).astype(np.float32))
    rel = np.arange(640) - 127 - 384
    half, exact = BUCKETS // 2, BUCKETS // 4
    n = np.abs(rel)
    nf = np.maximum(n, 1).astype(np.float32)
    large = exact + (np.log(nf / np.float32(exact)) / np.float32(math.log(128 / exact)) * np.float32(half - exact)).astype(np.int32)
    large = np.minimum(large, half - 1)
    bucket = np.where(rel > 0, half, 0) + np.where(n < exact, n, large)
    onehot = (np.arange(BUCKETS)[:, None] == bucket[None, :]).astype(np.float32)
    put("onehot", onehot)
    return c


def kernel(stop_after="", **inputs):
    import concourse.bacc as bacc
    from concourse.bass_utils import run_bass_kernel_spmd as run

    a = {k: np.asarray(v) for k, v in inputs.items()}
    params = np.zeros((P, N_PARAMS), np.float32)

    def put(name, value):
        lo, hi = PARAMS[name]
        params[:value.shape[0], lo:hi] = value

    chunks = lambda v: v.reshape(-1, P).T
    for name in ("a_q_gain", "a_k_gain", "m_q_gain", "m_k_gain"):
        put(name, np.concatenate([a[name + "_2"][0]] * 2)[:, None])
    put("lam_re", chunks(a["ssm_lambda_re_2"][0].reshape(-1)))
    put("lam_im", chunks(a["ssm_lambda_im_2"][0].reshape(-1)))
    put("log_dt", chunks(np.repeat(a["ssm_log_dt_2"][0], HD)))
    put("ssm_d", chunks(a["ssm_d_2"][0]))
    put("rel_bias", a["rel_bias_2"])

    def states(v):
        w = np.zeros((2, HD, 8, 2, 16), np.float32)
        for g in range(2):
            w[g, :, :, g, :] = v.reshape(8, 2, HD, 16)[:, g].transpose(1, 0, 2)
        return w.reshape(P, 256)
    put("b_re", states(a["ssm_b_re_2"][0].reshape(D, 16)))
    put("b_im", states(a["ssm_b_im_2"][0].reshape(D, 16)))
    put("c_re", states(a["ssm_c_re_2"][0].transpose(0, 2, 1).reshape(D, 16)))
    put("c_im", states(a["ssm_c_im_2"][0].transpose(0, 2, 1).reshape(D, 16)))
    rows = np.concatenate([a["norm_pre"][0], a["norm_post"][0], a["norm_pre"][1], a["norm_post"][1], a["ffn1_norm_2"][0],
                           a["mem_norm_2"][0], a["mix_norm_2"][0], a["ffn2_norm_2"][0], a["final_norm_2"][0], a["diff_subln"][0],
                           a["diff_lambda_q1"][0], a["diff_lambda_k1"][0], a["diff_lambda_q2"][0], a["diff_lambda_k2"][0]])[None]
    given = {"x": a["x"][0], "mem": a["mem_2"][0], "consts": shape_constants(), "params": params, "rows": rows,
             "dil_w_in": a["dil_w_in"][0], "dil_w_out": a["dil_w_out"][0],
             "diff_w_in": a["diff_w_in"][0], "diff_w_out": a["diff_w_out"][0]}
    for name in ("ffn1_w_in", "ffn1_w_out", "w_in", "w_o_a", "w_glu", "w_mem_kv", "w_o_m", "w_out", "ffn2_w_in", "ffn2_w_out"):
        given[name] = a[name + "_2"][0]

    nc = bacc.Bacc("TRN2", target_bir_lowering=False, num_devices=1)
    arrays, I = {}, {}
    for name, v in given.items():
        v = np.ascontiguousarray(v)
        arrays["in_" + name] = v
        I[name] = nc.dram_tensor("in_" + name, v.shape, F32, kind="ExternalInput").ap()
    out = nc.dram_tensor("out_0", (S, D), F32, kind="ExternalOutput").ap()
    program(nc, I, out, stop_after)
    result = run(nc, [arrays], core_ids=[0])
    return result.results[0]["out_0"].reshape(1, S, D)
```

```python
import math
from contextlib import ExitStack

import numpy as np

import concourse.bass as bass
from concourse import mybir

P = 128
D = 1024
S = 512
NT = S // P
KC = D // P
KP = 2
PIECE = KP * 512
RAW = 4
SPLIT = 4
HD = 64
EPS = 1e-6
NEG = -1.0e30
TAKEN = -3.0e38
LAMBDA_INIT = 0.8 - 0.6 * math.exp(-0.3 * 1)

DIL = (1, 4, 16)
DIL_HEADS = 16
ROW = HD + 2

FFN = 2816
FC = FFN // P
MEM = 256
W_IN = 4548
TOPK = min(256, S // 4)
BUCKETS = 32

F32 = mybir.dt.float32
F32R = mybir.dt.float32r
ALU = mybir.AluOpType
ACT = mybir.ActivationFunctionType
AX = mybir.AxisListType

CONSTS = {}
_at = 0
for _name, _n in (("ident", P), ("exchange", P), ("cos", S), ("sin", S), ("mask_first", 384), ("mask_band", 512),
                  ("mask_causal", 512), ("mask_16", P), ("mask_limit", P), ("onehot", 640)):
    CONSTS[_name] = (_at, _at + _n)
    _at += _n
N_CONSTS = _at

PARAMS = {}
_at = 0
for _name, _n in (("a_q_gain", 1), ("a_k_gain", 1), ("m_q_gain", 1), ("m_k_gain", 1),
                  ("lam_re", 8), ("lam_im", 8), ("log_dt", 8), ("ssm_d", 2), ("rel_bias", 8),
                  ("b_re", 2 * P), ("b_im", 2 * P), ("c_re", 2 * P), ("c_im", 2 * P)):
    PARAMS[_name] = (_at, _at + _n)
    _at += _n
N_PARAMS = _at

ROWS = {}
_at = 0
for _name, _n in (("pre0", D), ("post0", D), ("pre1", D), ("post1", D), ("ffn1", D), ("memory", D), ("mix", D), ("ffn2", D),
                  ("final", D), ("subln", P), ("lq1", HD), ("lk1", HD), ("lq2", HD), ("lk2", HD)):
    ROWS[_name] = (_at, _at + _n)
    _at += _n
N_ROWS = _at


UNIT_RATIO, GATE_RATIO, HYBRID_RATIO = 0.85, 1.6, 1.25


class Queue:

    def __init__(self, sem):
        self.sem, self.count, self.items, self.waited = sem, 0, [], {}

    def wait(self, *tokens):
        for token in tokens:
            if token is None:
                continue
            if isinstance(token, list):
                self.wait(*token)
                continue
            sem, value = token
            if self.waited.get(sem.name, 0) < value:
                self.waited[sem.name] = value
                self.items.append((None, sem, value, None))

    def __call__(self, method, *args, after=(), signal=True, **kwargs):
        self.wait(*after)
        self.items.append((method, args, kwargs, (self.sem, 1) if signal else None))
        if signal:
            self.count += 1
        return self.sem, self.count

    def dma(self, method, out, in_, counter, after=()):
        self.wait(*after)
        counter[1] += 16
        self.items.append((method, (out, in_), {}, (counter[0], 16)))
        return counter[0], counter[1]

    def run(self, eng):
        for method, a, b, inc in self.items:
            if method is None:
                eng.wait_ge(a, b)
            else:
                ins = method(*a, **b)
                if inc:
                    ins.then_inc(*inc)


def interleave(main, side, ratio=1.0, finish=True):
    owed = 0.0
    for _ in main:
        owed += ratio
        while owed >= 1.0:
            owed -= 1.0
            next(side, None)
    if finish:
        for _ in side:
            pass


def chain(*streams):
    for stream in streams:
        yield from stream


def program(nc, I, out, stop_after):
    T, V, A, G, SP = nc.tensor, nc.vector, nc.scalar, nc.gpsimd, nc.sync
    ctx = ExitStack()
    with ctx:
        def sb(name, shape, dt=F32):
            return ctx.enter_context(nc.sbuf_tensor(name, shape, dt))

        made_sems = {}

        def sem(name):
            if name not in made_sems:
                made_sems[name] = ctx.enter_context(nc.semaphore(name))
            return made_sems[name]

        consts = sb("consts", [P, N_CONSTS])
        params = sb("params", [P, N_PARAMS])
        raw_ring = sb("raw_ring", [P, RAW, PIECE])
        hi_ring = sb("hi_ring", [P, SPLIT, PIECE], F32R)
        lo_ring = sb("lo_ring", [P, SPLIT, PIECE], F32R)
        x = sb("x", [P, NT, D])
        xh = sb("xh", [P, KC, S], F32R)
        xl = sb("xl", [P, KC, S], F32R)
        small = sb("small", [P, 640])
        minus_half = sb("minus_half", [P, 36])
        gain_row = sb("gain_row", [P, D])
        FH = 12
        with nc.sbuf_tensor("hidden_hi", [P, FH, S], F32R) as hidden_hi, nc.sbuf_tensor("hidden_lo", [P, FH, S], F32R) as hidden_lo:
            pass
        ARENA = 22280
        KEPT = 2 * MEM + 2 * MEM
        arena = sb("arena", [P, ARENA])
        bank = [ctx.enter_context(nc.psum_tensor(f"bank{i}", [P, 512], F32)) for i in range(8)]
        scratch = nc.dram_tensor("scratch_heads", (3, S, DIL_HEADS * ROW), F32, kind="Internal").ap()
        scratch_bias = nc.dram_tensor("scratch_bias", (8, 640), F32, kind="Internal").ap()
        scratch_silu = nc.dram_tensor("scratch_silu", (2, S, D), F32, kind="Internal").ap()
        scratch_gates = nc.dram_tensor("scratch_gates", (24, P, S), F32, kind="Internal").ap()

        def emit(plan):
            def const(name, rows=P):
                a, b = CONSTS[name]
                return consts[0:rows, a:b]

            def param(name, i=None):
                a, b = PARAMS[name]
                return params[:, a:b] if i is None else params[:, a + i:a + i + 1]

            ident = const("ident")

            pe, dve, act, pool = Queue(sem("pe_done")), Queue(sem("dve_done")), Queue(sem("act_done")), Queue(sem("pool_done"))
            sp = Queue(sem("sp_done"))
            piece_landed = [[sem(f"piece_landed{i}"), 0] for i in range(RAW)]
            counters = {}

            def counter(name):
                if name not in counters:
                    counters[name] = [sem(name), 0]
                return counters[name]

            pieces_used = []
            pieces = [] if plan is None else plan
            piece_read = [None] * len(pieces)
            split_read = [None] * SPLIT
            piece_landed_at, piece_parts = [], {}
            n_loaded, n_split, n_seen, n_taken = [0], [0], [0], [0]
            low_part_on = ["pool"]
            bank_read = [None] * 8

            def barrier():
                done = [(q.sem, q.count) for q in (pe, dve, act, pool) if q.count] + [tuple(c) for c in counters.values() if c[1]]
                for q in (pe, dve, act, pool):
                    q.wait(*done)
                carved[0] = 0

            carved = [0]

            def carve(*shape):
                n = int(np.prod(shape))
                a = arena[:, carved[0]:carved[0] + n]
                carved[0] += n
                assert carved[0] <= ARENA, carved[0]
                if len(shape) == 1:
                    return a
                if len(shape) == 2:
                    return a.rearrange("p (a b) -> p a b", a=shape[0])
                if len(shape) == 3:
                    return a.rearrange("p (a b c) -> p a b c", a=shape[0], b=shape[1])
                return a.rearrange("p (a b c d) -> p a b c d", a=shape[0], b=shape[1], c=shape[2])

            def load(p):
                (view, kq, n, _), slot = pieces[p], p % RAW
                dst = raw_ring[:, slot, 0:kq * n].rearrange("p (k n) -> p k n", k=kq)
                read = [piece_read[p - RAW]] if p >= RAW else []
                for i, part in enumerate(view):
                    w = n // len(view)
                    landed = sp.dma(SP.dma_start, dst[:, :, i * w:(i + 1) * w], part, piece_landed[slot], after=read)
                piece_landed_at.append(landed)

            def split(p):
                _, kq, n, _ = pieces[p]
                slot = n_split[0] % SPLIT
                n_split[0] += 1
                raw, hi, lo = raw_ring[:, p % RAW, 0:kq * n], hi_ring[:, slot, 0:kq * n], lo_ring[:, slot, 0:kq * n]
                rounded = act(A.copy, hi, raw, after=[piece_landed_at[p], split_read[slot]])
                if low_part_on[0] == "dve":
                    t = dve(V.tensor_tensor, lo, raw, hi.bitcast(F32), ALU.subtract, after=[rounded])
                else:
                    t = pool(G.tensor_tensor, lo, raw, hi.bitcast(F32), ALU.subtract, after=[rounded])
                piece_read[p] = t
                parts = [a.rearrange("p (k n) -> p k n", k=kq) for a in (hi, lo)]
                piece_parts[p] = parts, t, slot

            def run_ahead(last):
                while True:
                    if n_loaded[0] < len(pieces) and (n_loaded[0] < RAW or piece_read[n_loaded[0] - RAW] is not None):
                        load(n_loaded[0])
                        n_loaded[0] += 1
                        continue
                    if n_seen[0] <= min(last, len(pieces) - 1) and n_seen[0] < n_loaded[0]:
                        if pieces[n_seen[0]][3]:
                            split(n_seen[0])
                        n_seen[0] += 1
                        continue
                    break

            def take(entry):
                p = n_taken[0]
                n_taken[0] += 1
                pieces_used.append(entry)
                if plan is None:
                    pieces.append(entry)
                    piece_read.append(None)
                run_ahead(p)
                _, kq, n, parted = entry
                if parted:
                    parts, t, slot = piece_parts[p]
                    return p, slot, parts, t
                return p, None, [raw_ring[:, p % RAW, 0:kq * n].rearrange("p (k n) -> p k n", k=kq)], piece_landed_at[p]

            def weight(w, k0, kq, c0, n):
                return w[k0 * P:(k0 + kq) * P, c0:c0 + n].rearrange("(k p) n -> p k n", p=P)

            def project(entries, terms, outs, consume, needs, out_cols=S):
                k0 = 0
                total = sum(e[1] for e in entries)
                for first in range(0, len(entries), 2):
                    pair = entries[first:first + 2]
                    taken = [take(e) for e in pair]
                    run_ahead(n_taken[0] + 1)
                    size = sum(e[1] for e in pair)
                    for b, o in enumerate(outs):
                        k = k0
                        for (_, kq, _, _), (_, _, parts, ready_) in zip(pair, taken):
                            for kk in range(kq):
                                products = terms(parts, k, kk, o)
                                for m, (lhsT, rhs) in enumerate(products):
                                    last = m == len(products) - 1
                                    done = pe(T.matmul, bank[b][:, 0:out_cols], lhsT, rhs, start=(k == 0 and m == 0),
                                              stop=(k == total - 1 and last),
                                              after=[ready_, bank_read[b], needs(o)] if k == 0 and m == 0 else [ready_],
                                              signal=(last and kk == kq - 1 and k == k0 + size - 1))
                                k += 1
                        if k == total:
                            bank_read[b] = consume(o, bank[b][:, 0:out_cols], done)
                        if b == len(outs) - 1:
                            for (p, slot, _, _) in taken:
                                if slot is None:
                                    piece_read[p] = done
                                else:
                                    split_read[slot] = done
                        yield
                    k0 += size

            def entries_of(w, c0, n, K, parted, k_first=0):
                return [((weight(w, k_first + k, min(KP, K - k), c0, n),), min(KP, K - k), n, parted) for k in range(0, K, KP)]

            def token_major(w, c0, n, tokens, consume, src=None, K=KC, k_first=0):
                sh, sl = (xh, xl) if src is None else src

                def terms(parts, k, kk, i):
                    wh, wl = parts[0][:, kk, :], parts[1][:, kk, :]
                    h, l = tokens(sh[:, k, :], i), tokens(sl[:, k, :], i)
                    return [(h, wh), (h, wl), (l, wh)]
                return project(entries_of(w, c0, n, K, True, k_first), terms, range(NT), consume, (lambda i: parts_ready[i]) if src is None else (lambda i: None), out_cols=n)

            def columns_terms(src):
                def terms(parts, k, kk, j):
                    w = [a[:, kk, j * P:(j + 1) * P] for a in parts]
                    if len(src) == 1:
                        return [(w[0], src[0][:, k, :])]
                    return [(w[0], src[0][:, k, :]), (w[0], src[1][:, k, :]), (w[1], src[0][:, k, :])]
                return terms

            def feature_major(w, c0, consume, src=None, K=KC):
                needs = (lambda j: list(parts_ready)) if src is None else (lambda j: None)
                src = (xh, xl) if src is None else src
                return project(entries_of(w, c0, 512, K, len(src) == 2), columns_terms(src), range(4), consume, needs)

            def run(stream):
                for _ in stream:
                    pass

            def tile(a, i):
                return a[:, i * P:(i + 1) * P]

            def rstd_of(sums, n, dst, after):
                width = sums.shape[-1]
                t = dve(V.tensor_scalar, dst, sums, 1.0 / n, EPS, ALU.mult, ALU.add, after=after)
                return pool(G.tensor_tensor, dst, dst, minus_half[:, 0:width], ALU.pow, after=[t])

            norm_ss = small[:, 0:8]
            norm_rstd = small[:, 8:16]

            def put_parts(src, dst_hi, dst_lo, after, free=None):
                t = act(A.copy, dst_hi, src, after=[after, free])
                return dve(V.tensor_tensor, dst_lo, src, dst_hi.bitcast(F32), ALU.subtract, after=[t])

            parts_ready = [None] * NT

            def turn_tile(tokens_src, n, after):
                for c in range(2):
                    b = 4 + 2 * (n % 2) + c
                    for k in range(4):
                        t = pe(T.transpose, tile(bank[b], k), tile(tokens_src, 4 * c + k), ident, after=[after, bank_read[b]], signal=(k == 3))
                    cols = slice(n * P, (n + 1) * P)
                    bank_read[b] = put_parts(bank[b][:, :].rearrange("p (a b) -> p a b", a=4), xh[:, 4 * c:4 * c + 4, cols], xl[:, 4 * c:4 * c + 4, cols], t)
                parts_ready[n] = bank_read[b]
                return t

            def hand_over():
                stored_all = [tuple(c) for name, c in counters.items() if "_stored" in name]
                for q in (dve, act, pool):
                    q.wait(*[(o.sem, o.count) for o in (pe, dve, act, pool) if o.count], *stored_all)
                carved[0] = 0

            gain_row_in = [None]

            def load_gain(name, after=()):
                gain_row_in[0] = load_row(name, gain_row[:, :], after)

            norm_tmp = arena[:, ARENA - KEPT - 2 * D:ARENA - KEPT].rearrange("p (a b) -> p a b", a=2)
            norm_tmp_free = [None, None]

            def norm_scale(n, after):
                ss, rstd = norm_ss[:, 4 + n:5 + n], norm_rstd[:, 4 + n:5 + n]
                t = act(A.activation, norm_tmp[:, n % 2, :], x[:, n, :], ACT.Square, accum_out=ss, after=[norm_tmp_free[n % 2], after])
                return rstd_of(ss, D, rstd, [t])

            def norm_tile(n, after):
                t = dve(V.scalar_tensor_tensor, norm_tmp[:, n % 2, :], x[:, n, :], norm_rstd[:, 4 + n:5 + n], gain_row[:, :],
                        ALU.mult, ALU.mult, after=[after, gain_row_in[0]])
                norm_tmp_free[n % 2] = turn_tile(norm_tmp[:, n % 2, :], n, t)
                return t

            def norm_to_parts(next_name, x_ready):
                scale = {}
                for n in range(NT + 1):
                    if n < NT:
                        scale[n] = norm_scale(n, x_ready[n])
                    if n:
                        t = norm_tile(n - 1, scale[n - 1])
                load_gain(next_name, [t])
                hand_over()

            def pe_wait_all():
                pe.wait(*pe_waits)
                pe_waits.clear()

            pe_waits = []


            def tanh_half(psum, dst, after):
                return act(A.activation, dst, psum, ACT.Tanh, scale=0.5, after=after)

            def twice_silu(psum, dst, after):
                t = tanh_half(psum, dst, after)
                return dve(V.scalar_tensor_tensor, dst, dst, 1.0, psum, ALU.add, ALU.mult, after=[t])

            def add_normed(Y, Yready, row, row_in, tmp, next_name):
                squares, y_scale, x_scale = [None] * NT, {}, {}

                def scale_y(n):
                    t = act(A.activation, tmp[:, n % 2, :], Y[:, n, :], ACT.Square, accum_out=norm_ss[:, n:n + 1],
                            after=[Yready[n], squares[n - 2] if n > 1 else None])
                    squares[n] = t
                    y_scale[n] = rstd_of(norm_ss[:, n:n + 1], D, norm_rstd[:, n:n + 1], [t])
                scale_y(0)
                for n in range(NT + 1):
                    if n < NT:
                        if n + 1 < NT:
                            scale_y(n + 1)
                        t = dve(V.scalar_tensor_tensor, Y[:, n, :], Y[:, n, :], norm_rstd[:, n:n + 1], row, ALU.mult, ALU.mult, after=[y_scale[n], row_in])
                        t = dve(V.tensor_tensor, x[:, n, :], x[:, n, :], Y[:, n, :], ALU.add, after=[t])
                        x_scale[n] = norm_scale(n, t)
                    if n:
                        t = norm_tile(n - 1, x_scale[n - 1])
                load_gain(next_name, [t])
                hand_over()

            first = counter("consts_landed")
            consts_in = sp.dma(SP.dma_start, consts[:, :], I["consts"], first)
            consts_in = sp.dma(SP.dma_start, params[:, :], I["params"], first)
            x_in = [act.dma(A.dma_start, x[:, n, :], I["x"][n * P:(n + 1) * P, :], counter("x_landed")) for n in range(NT)][-1]
            minus_half_set = pool(G.memset, minus_half[:, :], -0.5)
            pool.wait(minus_half_set)
            for q in (pe, dve, act, pool):
                q.wait(consts_in, x_in)

            def load_row(name, dst, after=()):
                a, b = ROWS[name]
                src = I["rows"][0, a:b].partition_broadcast(P)
                return pool.dma(G.dma_start, dst, src, counter("rows_landed"), after=after)

            load_gain("pre0")

            def gate_panels(w_in, c0, layer, temps, temps_read):
                free = list(temps_read)
                m = [0]

                def keep(c):
                    def consume(i, psum, token):
                        b = m[0] % 2
                        m[0] += 1
                        t = twice_silu(psum, temps[:, b, :], [token, free[b]])
                        free[b] = pool.dma(G.dma_start, scratch_silu[layer, i * P:(i + 1) * P, c * 512:(c + 1) * 512], temps[:, b, :],
                                           counter(f"silu_stored{b}"), after=[t])
                        return t
                    return consume
                return chain(*[token_major(w_in, c0 + c * 512, 512, tile, keep(c)) for c in range(2)])

            def dilated_layer():
                QT, KT, VV = carve(2, 4, S), carve(2, 4, S), carve(2, NT, 512)
                rope_a, rope_b = carve(2, S), carve(2, S)
                scores_sb, PT = carve(2, 896), carve(2, 7, P)
                stage = carve(2, NT, 8, ROW)
                w_in = I["dil_w_in"]
                rope_read = [None, None]
                rope_n = [0]

                def rope(dst, psum, token, g, free, rotated):
                    b = rope_n[0] % 2
                    rope_n[0] += 1
                    t1 = dve(V.tensor_tensor, rope_a[:, b, :], psum, const("cos"), ALU.mult, after=[token, rope_read[b]])
                    for quad in range(4):
                        t = act(A.copy, rope_b[32 * quad:32 * quad + 32, b, :], psum[32 * (quad ^ 1):32 * (quad ^ 1) + 32, :],
                                after=[t1, rope_read[b]], signal=(quad == 3))
                    read = t
                    finish_rope()

                    def rest():
                        t = dve(V.tensor_tensor, rope_b[:, b, :], rope_b[:, b, :], const("sin"), ALU.mult, after=[read])
                        r = DIL[g]
                        if r == 1:
                            o, a, c = dst, rope_a[:, b, :], rope_b[:, b, :]
                        else:
                            o = dst.rearrange("p (r l) -> p l r", r=r)
                            a = rope_a[:, b, :].rearrange("p (l r) -> p l r", r=r)
                            c = rope_b[:, b, :].rearrange("p (l r) -> p l r", r=r)
                        rope_read[b] = dve(V.tensor_tensor, o, a, c, ALU.add, after=[t, free])
                        rotated.append(rope_read[b])
                    rope_rest.append(rest)
                    return read

                rope_rest = []

                def finish_rope():
                    while rope_rest:
                        rope_rest.pop()()

                def group_tokens(g):
                    def pick(a, i):
                        if DIL[g] == 1:
                            return tile(a, i)
                        return a.rearrange("p (l r) -> p r l", r=4)[:, i, :]
                    return pick

                heads_read = [None, None]
                ready = {}

                def projections(u):
                    g, hf, buf = u // 2, u % 2, u % 2
                    ready[u] = []

                    def rotate(dst):
                        def consume(j, psum, token):
                            return rope(dst[:, buf, j, :], psum, token, g, heads_read[buf], ready[u])
                        return consume

                    def keep_v(i, psum, token):
                        t = act(A.copy, VV[:, buf, i, :], psum, after=[token, heads_read[buf]])
                        ready[u].append(t)
                        return t

                    c = g * D + hf * 512
                    if g < 2:
                        yield from token_major(w_in, 6 * D + c, 512, group_tokens(g), keep_v)
                    yield from feature_major(w_in, c, rotate(QT))
                    yield from feature_major(w_in, 3 * D + c, rotate(KT))
                    finish_rope()
                    if g < 2:
                        return
                    later = []

                    def turn_v(j, psum, token):
                        b = j % 2
                        t = act(A.copy, rope_a[:, b, :].rearrange("p (r l) -> p l r", r=16), psum.rearrange("p (l r) -> p l r", r=16),
                                after=[token, rope_read[b]])

                        def turn():
                            for i in range(NT):
                                t2 = pe(T.transpose, tile(bank[6], i), tile(rope_a[:, b, :], i), ident, after=[t, bank_read[6]], signal=(i == NT - 1))
                            rope_read[b] = t2
                            bank_read[6] = act(A.copy, VV[:, buf, :, j * P:(j + 1) * P], bank[6][:, :].rearrange("p (a b) -> p a b", a=NT),
                                               after=[t2, heads_read[buf]])
                            ready[u].append(bank_read[6])
                        later.append(turn)
                        return t
                    for _ in feature_major(w_in, 6 * D + c, turn_v):
                        while len(later) > 1:
                            later.pop(0)()
                        yield
                    later.pop(0)()

                stage_read = [None, None]
                sc_read, pt_read = [None, None], [None, None]
                heads_n = [0]

                def attention(u):
                    g, hf, buf = u // 2, u % 2, u % 2
                    st = stage[:, buf]
                    if g == 0:
                        blocks = [[(0, 0)], [(1, 0), (2, 1)], [(3, 1), (4, 2)], [(5, 2), (6, 3)]]
                        spans = [(0, 128), (128, 256), (384, 256), (640, 256)]
                    else:
                        blocks = [[(i, i)] for i in range(NT)]
                        spans = [(128 * i, 128) for i in range(NT)]
                    nb = 7 if g == 0 else 4
                    exp_done, first_b = {}, {}

                    def score(hh):
                        j, off = hh // 2, 64 * (hh % 2)
                        q, k = QT[off:off + 64, buf, j, :], KT[off:off + 64, buf, j, :]
                        s = heads_n[0] % 2
                        heads_n[0] += 1
                        first_b[hh] = s
                        sc = scores_sb[:, s, :]
                        if g == 0:
                            for b, tiles_ in ((4, (0, 1)), (5, (2, 3))):
                                base = spans[tiles_[0]][0]
                                for i in tiles_:
                                    a, n = spans[i]
                                    k0 = max(0, i - 1) * P
                                    t = pe(T.matmul, bank[b][:, a - base:a - base + n], tile(q, i), k[:, k0:k0 + n], start=True, stop=True,
                                           after=[bank_read[b], ready[u]], signal=(i == tiles_[1]))
                                n = 384 if b == 4 else 512
                                t = dve(V.scalar_tensor_tensor, sc[:, base:base + n], bank[b][:, 0:n], HD ** -0.5,
                                        const("mask_first" if b == 4 else "mask_band"), ALU.mult, ALU.add, after=[t, sc_read[s]])
                                bank_read[b] = t
                            dve(V.tensor_reduce, st[:, 0:1, hh, ROW - 1], sc[:, 0:P], AX.X, ALU.max, negate=True,
                                after=[t, stage_read[buf]], signal=False)
                            t = dve(V.tensor_reduce, st[:, 1:4, hh, ROW - 1], sc[:, P:896].rearrange("p (a b) -> p a b", a=3),
                                    AX.X, ALU.max, negate=True)
                        else:
                            b = 4 + s
                            for i in range(NT):
                                t = pe(T.matmul, tile(bank[b], i), tile(q, i), tile(k, i), start=True, stop=True,
                                       after=[bank_read[b], ready[u]], signal=(i == NT - 1))
                            m = const("mask_causal")[:, 384:512] if g == 1 else const("mask_16")
                            t = dve(V.scalar_tensor_tensor, sc[:, 0:512].rearrange("p (a b) -> p a b", a=NT),
                                    bank[b][:, :].rearrange("p (a b) -> p a b", a=NT), HD ** -0.5,
                                    m.unsqueeze(1).to_broadcast([P, NT, P]), ALU.mult, ALU.add, after=[t, sc_read[s]])
                            bank_read[b] = t
                            t = dve(V.tensor_reduce, st[:, :, hh, ROW - 1], sc[:, 0:512].rearrange("p (a b) -> p a b", a=NT),
                                    AX.X, ALU.max, negate=True, after=[t, stage_read[buf]])
                        for i in range(NT):
                            a, n = spans[i]
                            t2 = act(A.activation, sc[:, a:a + n], sc[:, a:a + n], ACT.Exp, bias=st[:, i, hh, ROW - 1:ROW],
                                     accum_out=st[:, i, hh, ROW - 2:ROW - 1], after=[t])
                        exp_done[hh] = t2

                    pt_done = {}

                    def turn(hh):
                        s = first_b[hh]
                        for r, lo in enumerate(range(0, nb, 4)):
                            hi = min(nb, lo + 4)
                            for blk in range(lo, hi):
                                t = pe(T.transpose, tile(bank[6], blk - lo), tile(scores_sb[:, s, :], blk), ident,
                                       after=[exp_done[hh], bank_read[6]], signal=(blk == hi - 1))
                            n = (hi - lo) * P
                            dst = PT[:, s, lo:hi, :].rearrange("p a b -> p (a b)")
                            if r == 0:
                                t3 = dve(V.tensor_copy, dst, bank[6][:, 0:n], after=[t, pt_read[s]])
                            else:
                                t3 = act(A.copy, dst, bank[6][:, 0:n], after=[t, pt_read[s]])
                            bank_read[6] = t3
                            pt_done[hh, r] = t3
                        sc_read[s] = t

                    def values(hh):
                        s = first_b[hh]
                        for i in range(NT):
                            for m, (blk, kt) in enumerate(blocks[i]):
                                t = pe(T.matmul, bank[7][:, i * HD:(i + 1) * HD], PT[:, s, blk, :], VV[:, buf, kt, hh * HD:(hh + 1) * HD],
                                       start=(m == 0), stop=(m == len(blocks[i]) - 1),
                                       after=[pt_done[hh, 0], pt_done.get((hh, 1)), bank_read[7]], signal=(i == NT - 1 and m == len(blocks[i]) - 1))
                        pt_read[s] = t
                        bank_read[7] = dve(V.tensor_copy, st[:, :, hh, 0:HD], bank[7][:, 0:NT * HD].rearrange("p (a b) -> p a b", a=NT),
                                           after=[t])
                        return t

                    for step in range(8 + 2):
                        if step < 8:
                            score(step)
                        yield
                        if 1 <= step < 9:
                            turn(step - 1)
                        if step >= 2:
                            t = values(step - 2)
                        yield
                    heads_read[buf] = t
                    done = [bank_read[7], exp_done[7], (act.sem, act.count)]
                    for i in range(NT):
                        rows = scratch[g].rearrange("(l r) c -> r l c", r=DIL[g])
                        if DIL[g] == 16:
                            for rr in range(4):
                                stage_read[buf] = pool.dma(G.dma_start, rows[4 * i + rr, :, hf * 8 * ROW:(hf + 1) * 8 * ROW],
                                                           st[32 * rr:32 * rr + 32, i].rearrange("p a b -> p (a b)"), counter(f"stage_stored{buf}"), after=done)
                        else:
                            dst = rows[i] if DIL[g] == 4 else rows[0, i * P:(i + 1) * P]
                            stage_read[buf] = pool.dma(G.dma_start, dst[:, hf * 8 * ROW:(hf + 1) * 8 * ROW],
                                                       st[:, i].rearrange("p a b -> p (a b)"), counter(f"stage_stored{buf}"), after=done)

                side = iter(())
                for u in range(6):
                    interleave(projections(u), side, UNIT_RATIO)
                    side = attention(u)

                interleave(gate_panels(w_in, 9 * D, 0, rope_a, rope_read), side, GATE_RATIO)
                barrier()

                heads = carve(2, 3, DIL_HEADS * ROW)
                mix, gate = carve(2, D), carve(2, D)
                heads_free = [None, None]
                mix_free = [None, None]
                mins, corr, dens = small[:, 16:32], small[:, 32:80], small[:, 80:128]
                stats_free = None
                for n in range(NT):
                    b = n % 2
                    H = heads[:, b].rearrange("p g (h r) -> p g h r", h=DIL_HEADS)
                    landed = pool.dma(G.dma_start, heads[:, b], scratch[:, n * P:(n + 1) * P, :].rearrange("g p c -> p g c"),
                                      counter(f"heads_landed{b}"), after=[heads_free[b]])
                    gate_in = pool.dma(G.dma_start, gate[:, b, :], scratch_silu[0, n * P:(n + 1) * P, :], counter(f"gate_landed{b}"), after=[mix_free[b]])
                    by_g = lambda a: a.rearrange("p (g h) -> p g h", g=3)
                    t = dve(V.tensor_reduce, mins, H[:, :, :, ROW - 1].rearrange("p g h -> p h g"), AX.X, ALU.min, after=[landed, stats_free])
                    t = dve(V.tensor_tensor, by_g(corr), mins.unsqueeze(1).to_broadcast([P, 3, DIL_HEADS]), H[:, :, :, ROW - 1], ALU.subtract, after=[t])
                    t = act(A.activation, corr, corr, ACT.Exp, after=[t])
                    t = dve(V.tensor_tensor, by_g(dens), by_g(corr), H[:, :, :, ROW - 2], ALU.mult, after=[t])
                    t = dve(V.tensor_reduce, mins, dens.rearrange("p (g h) -> p h g", g=3), AX.X, ALU.add, after=[t])
                    t = dve(V.reciprocal, mins, mins, after=[t])
                    t = dve(V.tensor_tensor, by_g(corr), by_g(corr), mins.unsqueeze(1).to_broadcast([P, 3, DIL_HEADS]), ALU.mult, after=[t])
                    weights = t
                    for g in (2, 0, 1):
                        w = corr[:, g * 16:(g + 1) * 16].unsqueeze(2).to_broadcast([P, DIL_HEADS, HD])
                        on, tt = (pool, G.tensor_tensor) if g == 2 else (dve, V.tensor_tensor)
                        t = on(tt, H[:, g, :, 0:HD], H[:, g, :, 0:HD], w, ALU.mult, after=[weights])
                        if g == 2:
                            third = t
                    stats_free = [t, third]
                    m = mix[:, b, :].rearrange("p (h r) -> p h r", h=DIL_HEADS)
                    t = dve(V.tensor_tensor, m, H[:, 0, :, 0:HD], H[:, 1, :, 0:HD], ALU.add, after=[t, mix_free[b]])
                    t = dve(V.tensor_tensor, m, m, H[:, 2, :, 0:HD], ALU.add, after=[t, third])
                    heads_free[b] = t
                    t = dve(V.scalar_tensor_tensor, mix[:, b, :], mix[:, b, :], 0.5, gate[:, b, :], ALU.mult, ALU.mult, after=[t, gate_in])
                    mix_free[b] = turn_tile(mix[:, b, :], n, t)

            def project_out(w, Y):
                Yready = [None] * NT

                def keep(c):
                    def consume(i, psum, token):
                        Yready[i] = act(A.copy, Y[:, i, c * 512:(c + 1) * 512], psum, after=[token])
                        return Yready[i]
                    return consume
                for c in range(2):
                    for _ in token_major(w, c * 512, 512, tile, keep(c)):
                        pass
                return Yready

            def finish_layer(w, row_name, next_name):
                hand_over()
                Y, row, tmp = carve(NT, D), carve(D), carve(2, D)
                row_in = load_row(row_name, row)
                Yready = project_out(w, Y)
                add_normed(Y, Yready, row, row_in, tmp, next_name)

            def differential_layer():
                QT, KT, VV = carve(2, 4, S), carve(2, 4, S), carve(2, NT, 512)
                rope_a, rope_b = carve(2, S), carve(2, S)
                E, PT = carve(2, 2, S), carve(2, S)
                O = carve(NT, D)
                rowv = carve(P + 4 * HD)
                stat = small[:, 192:192 + 16]
                neg_lam, lam2 = small[:, 208:209], small[:, 209:211]
                inv_den = small[:, 216:224]
                inv_read = [None, None]
                w_in = I["diff_w_in"]
                rows_in = pool.dma(G.dma_start, rowv, I["rows"][0, ROWS["subln"][0]:ROWS["lk2"][1]].partition_broadcast(P), counter("rows_landed"))
                for m in range(2):
                    a = P + 2 * m * HD
                    t = dve(V.tensor_tensor, rowv[:, a:a + HD], rowv[:, a:a + HD], rowv[:, a + HD:a + 2 * HD], ALU.mult, after=[rows_in])
                    t = dve(V.tensor_reduce, lam2[:, m:m + 1], rowv[:, a:a + HD], AX.X, ALU.add, after=[t])
                t = act(A.activation, lam2, lam2, ACT.Exp, after=[t])
                t = dve(V.tensor_tensor, neg_lam, lam2[:, 1:2], lam2[:, 0:1], ALU.subtract, after=[t])
                t = dve(V.tensor_scalar, neg_lam, neg_lam, -LAMBDA_INIT, None, ALU.add, after=[t])
                t = dve(V.tensor_scalar, rowv[:, 0:P], rowv[:, 0:P], 0.5 * (1.0 - LAMBDA_INIT), None, ALU.mult, after=[t])
                dve.wait(t)

                rope_read, rope_n, heads_read, ready = [None, None], [0], [None, None], {}
                rope_rest = []

                def finish_rope():
                    while rope_rest:
                        rope_rest.pop()()

                def projections(u):
                    buf = u % 2
                    ready[u] = []

                    def rotate(dst):
                        def consume(j, psum, token):
                            b = rope_n[0] % 2
                            rope_n[0] += 1
                            t1 = dve(V.tensor_tensor, rope_a[:, b, :], psum, const("cos"), ALU.mult, after=[token, rope_read[b]])
                            for quad in range(4):
                                read = act(A.copy, rope_b[32 * quad:32 * quad + 32, b, :], psum[32 * (quad ^ 1):32 * (quad ^ 1) + 32, :],
                                           after=[t1, rope_read[b]], signal=(quad == 3))
                            finish_rope()

                            def rest():
                                t = dve(V.tensor_tensor, rope_b[:, b, :], rope_b[:, b, :], const("sin"), ALU.mult, after=[read])
                                t = dve(V.tensor_tensor, dst[:, buf, j, :], rope_a[:, b, :], rope_b[:, b, :], ALU.add, after=[t, heads_read[buf]])
                                rope_read[b] = t
                                ready[u].append(t)
                            rope_rest.append(rest)
                            return read
                        return consume

                    def keep_v(i, psum, token):
                        t = act(A.copy, VV[:, buf, i, :], psum, after=[token, heads_read[buf]])
                        ready[u].append(t)
                        return t

                    yield from token_major(w_in, 2 * D + u * 512, 512, tile, keep_v)
                    yield from feature_major(w_in, u * 512, rotate(QT))
                    yield from feature_major(w_in, D + u * 512, rotate(KT))
                    finish_rope()

                e_read, pt_read = [None, None], [None, None]

                def attention(u):
                    buf = u % 2
                    jobs = [(hh, i) for hh in range(4) for i in range(NT)]
                    made, combined, turned = {}, {}, {}

                    def score(n):
                        hh, i = jobs[n]
                        s, nk = n % 2, (i + 1) * P
                        mx, den = stat[:, 4 * s:4 * s + 2], stat[:, 4 * s + 2:4 * s + 4]
                        for c in range(2):
                            off = 64 * c
                            t = pe(T.matmul, bank[4 + c][:, 0:nk], tile(QT[off:off + 64, buf, hh, :], i), KT[off:off + 64, buf, hh, 0:nk],
                                   start=True, stop=True, after=[bank_read[4 + c], ready[u]])
                            t = dve(V.scalar_tensor_tensor, E[:, s, c, 0:nk], bank[4 + c][:, 0:nk], HD ** -0.5,
                                    const("mask_causal")[:, 384 - i * P:512], ALU.mult, ALU.add, after=[t, e_read[s]])
                            bank_read[4 + c] = t
                        t = dve(V.tensor_reduce, mx, E[:, s, :, 0:nk], AX.X, ALU.max, negate=True, after=[t])
                        for c in range(2):
                            t2 = act(A.activation, E[:, s, c, 0:nk], E[:, s, c, 0:nk], ACT.Exp, bias=mx[:, c:c + 1],
                                     accum_out=den[:, c:c + 1], after=[t])
                        made[n] = t2

                    def combine(n):
                        hh, i = jobs[n]
                        s, nk = n % 2, (i + 1) * P
                        den = stat[:, 4 * s + 2:4 * s + 4]
                        keep_den = inv_den[:, 4 * (hh % 2) + i:4 * (hh % 2) + i + 1]
                        t = dve(V.reciprocal, keep_den, den[:, 0:1], after=[made[n], inv_read[hh % 2]])
                        t = dve(V.reciprocal, den[:, 1:2], den[:, 1:2], after=[])
                        t = dve(V.tensor_scalar, den[:, 1:2], den[:, 1:2], den[:, 0:1], neg_lam, ALU.mult, ALU.mult, after=[t])
                        combined[n] = dve(V.scalar_tensor_tensor, E[:, s, 0, 0:nk], E[:, s, 1, 0:nk], den[:, 1:2], E[:, s, 0, 0:nk],
                                          ALU.mult, ALU.add, after=[t])

                    def turn(n):
                        i = jobs[n][1]
                        s, nk = n % 2, (i + 1) * P
                        for k in range(i + 1):
                            t2 = pe(T.transpose, tile(bank[6], k), tile(E[:, s, 0, :], k), ident, after=[combined[n], bank_read[6]], signal=(k == i))
                        e_read[s] = t2
                        bank_read[6] = act(A.copy, PT[:, s, 0:nk], bank[6][:, 0:nk], after=[t2, pt_read[s]])
                        turned[n] = bank_read[6]

                    def values(n):
                        hh, i = jobs[n]
                        s = n % 2
                        for k in range(i + 1):
                            t = pe(T.matmul, tile(bank[7], i), tile(PT[:, s, :], k), VV[:, buf, k, hh * P:(hh + 1) * P],
                                   start=(k == 0), stop=(k == i), after=[turned[n], bank_read[7]], signal=(k == i))
                        pt_read[s] = t
                        if i == NT - 1:
                            h = 4 * u + hh
                            inv = inv_den[:, 4 * (hh % 2):4 * (hh % 2) + 4].unsqueeze(2).to_broadcast([P, NT, P])
                            bank_read[7] = dve(V.tensor_tensor, O[:, :, h * P:(h + 1) * P], bank[7][:, :].rearrange("p (a b) -> p a b", a=NT), inv,
                                               ALU.mult, after=[t])
                            inv_read[hh % 2] = bank_read[7]
                        return t

                    N = len(jobs)
                    for n in range(N + 2):
                        if 1 <= n <= N:
                            combine(n - 1)
                        if n < N:
                            score(n)
                        yield
                        if 1 <= n <= N:
                            turn(n - 1)
                        if n >= 2:
                            t = values(n - 2)
                        yield
                    heads_read[buf] = t

                side = iter(())
                for u in range(2):
                    interleave(projections(u), side, 1.5)
                    side = attention(u)

                interleave(gate_panels(w_in, 3 * D, 1, rope_a, rope_read), side, 2.2)
                barrier()

                carve(3 * 4096 + 2048 + 2048 + 1024)
                O, rowv = carve(NT, D), carve(P + 4 * HD)
                carved[0] = 0
                sq, gate = carve(NT, D), carve(NT, D)
                gate_in = pool.dma(G.dma_start, gate, scratch_silu[1].rearrange("(n p) c -> p n c", p=P), counter("gate_landed0"))
                sub = rowv[:, 0:P].unsqueeze(1).to_broadcast([P, 8, P])
                scales, gates_ready = [], []
                for n in range(NT):
                    t = act(A.activation, sq[:, n, :], O[:, n, :], ACT.Square)
                    ss = small[:, 16 + 8 * n:24 + 8 * n]
                    t = dve(V.tensor_reduce, ss, sq[:, n, :].rearrange("p (h d) -> p h d", h=8), AX.X, ALU.add, after=[t])
                    scales.append(rstd_of(ss, P, ss, [t]))
                    by_head = gate[:, n, :].rearrange("p (h d) -> p h d", h=8)
                    gates_ready.append(pool(G.tensor_tensor, by_head, by_head, sub, ALU.mult, after=[gate_in]))
                for n in range(NT):
                    on = O[:, n, :].rearrange("p (h d) -> p h d", h=8)
                    ss = small[:, 16 + 8 * n:24 + 8 * n]
                    t = dve(V.tensor_tensor, on, on, ss.unsqueeze(2).to_broadcast([P, 8, P]), ALU.mult, after=[scales[n]])
                    t = dve(V.tensor_tensor, O[:, n, :], O[:, n, :], gate[:, n, :], ALU.mult, after=[t, gates_ready[n]])
                    turn_tile(O[:, n, :], n, t)

            def feed_forward(w_in, w_out, side=iter(())):
                low_part_on[0] = "pool"
                carved[0] = 2 * FH * S
                e, hid = carve(2, S), carve(2, S)
                x_ready = [None] * NT
                e_ready, e_free, hid_free = [None, None], [None, None], [None, None]
                for lot, chunks in enumerate((range(0, FH), range(FH, FC))):
                    if lot:
                        act.wait((pe.sem, pe.count))
                        dve.wait((pe.sem, pe.count))
                    for c in range(chunks[0] // 2, chunks[-1] // 2 + 1):
                        def consume(o, psum, token):
                            s = o % 2
                            if o < 2:
                                e_ready[s] = twice_silu(psum, e[:, s, :], [token, e_free[s]])
                                return e_ready[s]
                            t = dve(V.tensor_tensor, hid[:, s, :], e[:, s, :], psum, ALU.mult, after=[token, e_ready[s], hid_free[s]])
                            e_free[s] = t
                            k = 2 * c + s - chunks[0]
                            hid_free[s] = put_parts(hid[:, s, :], hidden_hi[:, k, :], hidden_lo[:, k, :], t)
                            pe_waits.append(hid_free[s])
                            return t
                        entries = [((weight(w_in, k, KP, c * 256, 256), weight(w_in, k, KP, FFN + c * 256, 256)), KP, 512, True)
                                   for k in range(0, KC, KP)]
                        for _ in project(entries, columns_terms((xh, xl)), range(4), consume, lambda o: list(parts_ready)):
                            next(side, None)
                    pe_wait_all()
                    for c in range(2):
                        def add(i, psum, token):
                            dst = x[:, i, c * 512:(c + 1) * 512]
                            x_ready[i] = dve(V.scalar_tensor_tensor, dst, psum, 0.25, dst, ALU.mult, ALU.add, after=[token, (dve.sem, dve.count)])
                            return x_ready[i]
                        run(token_major(w_out, c * 512, 512, tile, add, src=(hidden_hi, hidden_lo), K=len(chunks), k_first=chunks[0]))
                run(side)
                return x_ready

            kept = arena[:, ARENA - KEPT:ARENA]
            mkT = kept[:, 0:2 * MEM].rearrange("p (a b) -> p a b", a=2)
            mv = kept[:, 2 * MEM:KEPT].rearrange("p (a b) -> p a b", a=2)
            norm_stat = small[:, 128:192]
            coef = small[:, 256:640]
            c8 = lambda i: coef[:, 8 * i:8 * i + 8]
            powers = [(c8(10 + 3 * k), c8(11 + 3 * k), c8(12 + 3 * k)) for k in range(9)]
            bias_stored = [None]

            def norm_heads(a, heads, stat, tmp, after):
                t = dve(V.tensor_tensor, tmp, a, a, ALU.mult, after=after)
                t = dve(V.tensor_reduce, stat, tmp.rearrange("p (h d) -> p h d", h=heads), AX.X, ALU.add, after=[t])
                t = rstd_of(stat, HD, stat, [t])
                a3 = a.rearrange("p (h d) -> p h d", h=heads)
                return dve(V.tensor_tensor, a3, a3, stat.unsqueeze(2).to_broadcast([P, heads, HD]), ALU.mult, after=[t])

            def turn_chunks(sources, dst, b, scale=None, tiles=NT):
                for n in range(tiles):
                    t = pe(T.transpose, tile(bank[b], n), sources(n), ident, after=[bank_read[b]], signal=(n == tiles - 1))
                if scale is None:
                    bank_read[b] = act(A.copy, dst, bank[b][:, 0:tiles * P], after=[t])
                else:
                    bank_read[b] = act(A.activation, dst, bank[b][:, 0:tiles * P], ACT.Copy, scale=scale, after=[t])
                return bank_read[b]

            def memory_keys_values():
                carved[0] = 2 * FH * S + 4 * S
                mem, row, tmp = carve(2, D), carve(D), carve(D)
                memT, kv = carve(KC, MEM), carve(512)
                assert carved[0] <= ARENA - KEPT
                mem_in = pool.dma(G.dma_start, mem, I["mem"].rearrange("(n p) c -> p n c", p=P), counter("mem_landed"), after=[(pe.sem, pe.count)])
                row_in = load_row("memory", row, after=[(pe.sem, pe.count)])
                act.wait((pe.sem, pe.count))
                for n in range(2):
                    stat = small[:, 240 + 2 * n:241 + 2 * n]
                    t = act(A.activation, tmp, mem[:, n, :], ACT.Square, accum_out=stat, after=[mem_in, (act.sem, act.count)])
                    t = rstd_of(stat, D, stat, [t])
                    t = dve(V.scalar_tensor_tensor, mem[:, n, :], mem[:, n, :], stat, row, ALU.mult, ALU.mult, after=[t, row_in])
                    yield
                    for c in range(2):
                        yield
                        b = 4 + 2 * n + c
                        for k in range(4):
                            t2 = pe(T.transpose, tile(bank[b], k), tile(mem[:, n, :], 4 * c + k), ident, after=[t, bank_read[b]], signal=(k == 3))
                        bank_read[b] = act(A.copy, memT[:, 4 * c:4 * c + 4, n * P:(n + 1) * P], bank[b][:, :].rearrange("p (a b) -> p a b", a=4), after=[t2])
                memT_ready = [bank_read[b] for b in range(4, 8)]
                for first in range(0, KC, KP):
                    p, _, (w,), landed = take(((weight(I["w_mem_kv"], first, KP, 0, 512),), KP, 512, False))
                    for n in range(2):
                        for kk in range(KP):
                            k = first + kk
                            t = pe(T.matmul, bank[4 + n][:, :], tile(memT[:, k, :], n), w[:, kk, :], start=(k == 0), stop=(k == KC - 1),
                                   after=[landed, memT_ready], signal=(kk == KP - 1))
                    piece_read[p] = t
                    yield
                for n in range(2):
                    t = act(A.copy, kv, bank[4 + n][:, :], after=[t, (dve.sem, dve.count), (pe.sem, pe.count)])
                    bank_read[4 + n] = t
                    dve(V.tensor_copy, mv[:, n, :], kv[:, 256:512], after=[t])
                    t = norm_heads(kv[:, 0:256], 4, norm_stat[:, 4 * n:4 * n + 4], tmp[:, 0:256], [t])
                    yield
                    yield
                    for j in range(2):
                        t2 = pe(T.transpose, tile(bank[6], j), tile(kv, j), ident, after=[t, bank_read[6]])
                    bank_read[6] = act(A.activation, mkT[:, :, n * P:(n + 1) * P], bank[6][:, 0:2 * P].rearrange("p (a b) -> p a b", a=2),
                                       ACT.Copy, scale=param("m_k_gain"), after=[t2])
                    yield

            def coefficients():
                carved[0] = 2 * FH * S + 4 * S
                coef_tmp, beta = carve(768), carve(640)
                act.wait((pe.sem, pe.count), (dve.sem, dve.count))
                for lo, hi, b in ((0, 512, 4), (512, 640, 5)):
                    t = pe(T.matmul, bank[b][0:8, 0:hi - lo], params[0:BUCKETS, PARAMS["rel_bias"][0]:PARAMS["rel_bias"][1]],
                           const("onehot", BUCKETS)[:, lo:hi], start=True, stop=True, after=[bank_read[b]])
                    t = act(A.copy, beta[0:8, lo:hi], bank[b][0:8, 0:hi - lo], after=[t])
                    bank_read[b] = t
                bias_stored[0] = pool.dma(G.dma_start, scratch_bias, beta[0:8, 0:640], counter("bias_stored"), after=[t])
                yield
                dt, th, mag, cs, sn, tmp1, tmp2, den, fr, fi = [c8(i) for i in range(10)]
                lr, li = param("lam_re"), param("lam_im")
                last = [None]

                def v(method, *args, **kw):
                    last[0] = dve(method, *args, after=[last[0]], **kw)

                last[0] = act(A.activation, dt, param("log_dt"), ACT.Exp)
                v(V.tensor_tensor, th, li, dt, ALU.mult)
                v(V.tensor_tensor, tmp1, lr, dt, ALU.mult)
                last[0] = act(A.activation, mag, tmp1, ACT.Exp, after=[last[0]])
                MAGIC = 1.5 * 2.0 ** 23
                C1 = 6.28125
                C2 = float(np.float32(2 * math.pi - C1))
                C3 = 2 * math.pi - C1 - C2
                for dst, turn_part, shift in ((sn, 0.0, 0.0), (cs, 0.25, math.pi / 2)):
                    v(V.tensor_scalar, tmp1, th, 1 / (2 * math.pi), turn_part, ALU.mult, ALU.add)
                    v(V.tensor_scalar, tmp1, tmp1, MAGIC, None, ALU.add)
                    v(V.tensor_scalar, tmp1, tmp1, -MAGIC, None, ALU.add)
                    v(V.scalar_tensor_tensor, tmp2, tmp1, -C1, th, ALU.mult, ALU.add)
                    v(V.scalar_tensor_tensor, tmp2, tmp1, -C2, tmp2, ALU.mult, ALU.add)
                    v(V.scalar_tensor_tensor, tmp2, tmp1, -C3, tmp2, ALU.mult, ALU.add)
                    v(V.tensor_scalar, tmp2, tmp2, shift, None, ALU.add)
                    v(V.tensor_scalar, tmp2, tmp2, 3.1415925, -3.1415925, ALU.min, ALU.max)
                    last[0] = act(A.activation, dst, tmp2, ACT.Sin, after=[last[0]])
                ar, ai, nai = powers[0]
                v(V.tensor_tensor, ar, mag, cs, ALU.mult)
                v(V.tensor_tensor, ai, mag, sn, ALU.mult)
                v(V.tensor_tensor, den, lr, lr, ALU.mult)
                v(V.tensor_tensor, tmp1, li, li, ALU.mult)
                v(V.tensor_tensor, den, den, tmp1, ALU.add)
                v(V.reciprocal, den, den)
                v(V.tensor_scalar, cs, ar, -1.0, None, ALU.add)
                v(V.tensor_tensor, tmp1, cs, lr, ALU.mult)
                v(V.tensor_tensor, tmp2, ai, li, ALU.mult)
                v(V.tensor_tensor, fr, tmp1, tmp2, ALU.add)
                v(V.tensor_tensor, fr, fr, den, ALU.mult)
                v(V.tensor_tensor, tmp1, ai, lr, ALU.mult)
                v(V.tensor_tensor, tmp2, cs, li, ALU.mult)
                v(V.tensor_tensor, fi, tmp1, tmp2, ALU.subtract)
                v(V.tensor_tensor, fi, fi, den, ALU.mult)
                for k in range(9):
                    r, i_, ni = powers[k]
                    v(V.tensor_scalar, ni, i_, -1.0, None, ALU.mult)
                    if k < 8:
                        r2, i2, _ = powers[k + 1]
                        v(V.tensor_tensor, tmp1, r, r, ALU.mult)
                        v(V.tensor_tensor, tmp2, i_, i_, ALU.mult)
                        v(V.tensor_tensor, r2, tmp1, tmp2, ALU.subtract)
                        v(V.tensor_tensor, tmp1, r, i_, ALU.mult)
                        v(V.tensor_scalar, i2, tmp1, 2.0, None, ALU.mult)
                by_pair = lambda a: a.rearrange("p (g c) -> p g c", g=8)
                bcol = lambda a: a.unsqueeze(2).to_broadcast([P, 8, 32])
                br, bi = param("b_re"), param("b_im")
                t1, t2, t3 = coef_tmp[:, 0:256], coef_tmp[:, 256:512], coef_tmp[:, 512:768]
                v(V.tensor_tensor, by_pair(t1), by_pair(br), bcol(fr), ALU.mult)
                v(V.tensor_tensor, by_pair(t2), by_pair(bi), bcol(fi), ALU.mult)
                v(V.tensor_tensor, t3, t1, t2, ALU.subtract)
                v(V.tensor_tensor, by_pair(t1), by_pair(bi), bcol(fr), ALU.mult)
                v(V.tensor_tensor, by_pair(t2), by_pair(br), bcol(fi), ALU.mult)
                v(V.tensor_tensor, t1, t1, t2, ALU.add)
                v(V.tensor_scalar, param("c_im"), param("c_im"), -1.0, None, ALU.mult)
                for _ in range(12):
                    yield
                for comp, fb in ((0, t3), (1, t1)):
                    for half in range(2):
                        t = pe(T.transpose, tile(bank[4 + comp], half), tile(fb, half), ident, after=[last[0], bank_read[4 + comp]])
                    bank_read[4 + comp] = act(A.copy, (br, bi)[comp], bank[4 + comp][:, 0:2 * P], after=[t])
                pe.wait(bank_read[4], bank_read[5])

            def before_hybrid():
                yield from memory_keys_values()
                yield from coefficients()

            def hybrid():
                low_part_on[0] = "pool"
                proj_u, proj_k, proj_q = carve(NT, 512), carve(NT, 452), carve(NT, 512)
                gate_temp = carve(2, S)
                qaT, kaT, kiT, qiT = carve(4, S), carve(S), carve(S), carve(2, S)
                uT, qmT = carve(2, S), carve(2, S)
                sel = carve(1280)
                work, PT = carve(1024), carve(1024)
                kdup = work.rearrange("p (a b c) -> p a b c", a=NT, b=2)
                bias_sel = qiT
                hank, bias = carve(S), carve(S)
                X = carve(2, 2, 256 + S)
                assert carved[0] <= ARENA - KEPT, carved[0] - ARENA + KEPT
                pool(G.memset, X[:, :, :, 0:256], 0.0)

                def keep(dst):
                    ready_ = []

                    def consume(i, psum, token):
                        ready_.append(act(A.copy, dst[:, i, :], psum, after=[token]))
                        return ready_[-1]
                    return consume, ready_

                def narrow(c0, n, dst):
                    consume, ready_ = keep(dst)
                    yield from token_major(I["w_in"], c0, n, tile, consume)
                    dve.wait(ready_)
                    pe.wait(ready_)

                w_idx = small[:, 192:208]

                def turn_u():
                    for j in range(2):
                        turn_chunks(lambda n: proj_u[:, n, j * P:(j + 1) * P], uT[:, j, :], 4 + j)
                        yield
                    for i in range(NT):
                        t = norm_heads(proj_u[:, i, 256:512], 4, norm_stat[:, 16 + 4 * (i % 2):20 + 4 * (i % 2)], PT[:, 0:256], [(dve.sem, dve.count)])
                        yield
                    pe.wait(t)
                    for j in range(2):
                        turn_chunks(lambda n: proj_u[:, n, 256 + j * P:256 + (j + 1) * P], qmT[:, j, :], 6 + j, param("m_q_gain"))
                        yield

                def turn_k():
                    for i in range(NT):
                        t = norm_heads(proj_k[:, i, 0:HD], 1, norm_stat[:, 32:33], PT[:, 0:HD], [(dve.sem, dve.count)])
                        for m, c0 in ((0, 0), (1, 384)):
                            for half in range(2):
                                t = dve(V.tensor_copy, kdup[:, i, m, half * HD:(half + 1) * HD], proj_k[:, i, c0:c0 + HD], after=[t])
                        yield
                    t = dve(V.tensor_scalar, w_idx.rearrange("p (n h) -> p n h", n=NT), proj_k[:, :, 448:452], HD ** -0.5 * 4 ** -0.5, None, ALU.mult)
                    pe.wait(t)
                    turn_chunks(lambda n: kdup[:, n, 1, :], kiT, 5)
                    turn_chunks(lambda n: kdup[:, n, 0, :], kaT, 6, param("a_k_gain"))
                    yield
                    for j in range(2):
                        turn_chunks(lambda n: proj_k[:, n, 128 + j * P:128 + (j + 1) * P], qiT[:, j, :], 6 + j)
                        yield

                def turn_q():
                    for i in range(NT):
                        t = norm_heads(proj_q[:, i, :], 8, norm_stat[:, 48:56], PT[:, 0:512], [(dve.sem, dve.count)])
                        yield
                    pe.wait(t)
                    for j in range(4):
                        turn_chunks(lambda n: proj_q[:, n, j * P:(j + 1) * P], qaT[:, j, :], 5 + j % 2, param("a_q_gain"))
                        yield

                gate_free = [None, None]
                gate_n = [0]

                def gate_chunk(c):
                    def consume(j, psum, token):
                        b = gate_n[0] % 2
                        gate_n[0] += 1
                        t = tanh_half(psum, gate_temp[:, b, :], [token, gate_free[b]])
                        gate_free[b] = act.dma(A.dma_start, scratch_gates[4 * c + j], gate_temp[:, b, :], counter(f"gate_stored{b}"), after=[t])
                        return t
                    return consume

                mem_free = [None, None]

                def memory_attention():
                    for h in range(4):
                        j, off = h // 2, 64 * (h % 2)
                        q, k = qmT[off:off + 64, j, :], mkT[off:off + 64, j, :]
                        nm, dn = small[:, 208:212], small[:, 212:216]
                        W = work.rearrange("p (n k) -> p n k", n=NT)
                        for b in range(2):
                            for i in (2 * b, 2 * b + 1):
                                t = pe(T.matmul, bank[5][:, (i % 2) * MEM:(i % 2 + 1) * MEM], tile(q, i), k, start=True, stop=True,
                                       after=[bank_read[5]], signal=(i % 2 == 1))
                            t = act(A.activation, work[:, b * 512:(b + 1) * 512], bank[5][:, :], ACT.Copy, scale=HD ** -0.5, after=[t, mem_free[0]])
                            bank_read[5] = t
                        yield
                        t = dve(V.tensor_reduce, nm, W, AX.X, ALU.max, negate=True, after=[t])
                        for i in range(NT):
                            t2 = act(A.activation, W[:, i, :], W[:, i, :], ACT.Exp, bias=nm[:, i:i + 1], accum_out=dn[:, i:i + 1], after=[t])
                        t = dve(V.reciprocal, dn, dn, after=[t2])
                        for i in range(NT):
                            t2 = act(A.activation, W[:, i, :], W[:, i, :], ACT.Copy, scale=dn[:, i:i + 1], after=[t])
                        t = t2
                        yield
                        for kb in range(2):
                            for i in range(NT):
                                t2 = pe(T.transpose, tile(bank[6], i), W[:, i, kb * P:(kb + 1) * P], ident, after=[t, bank_read[6]], signal=(i == NT - 1))
                            t3 = act(A.copy, PT[:, kb * 512:(kb + 1) * 512], bank[6][:, :], after=[t2, mem_free[1]])
                            bank_read[6] = t3
                        mem_free[0] = t2
                        yield
                        for kb in range(2):
                            t = pe(T.matmul, bank[7][off:off + 64, :], mv[:, kb, h * HD:(h + 1) * HD], PT[:, kb * 512:(kb + 1) * 512],
                                   start=(kb == 0), stop=(kb == 1), after=[t3, bank_read[7]], signal=(kb == 1))
                        mem_free[1] = t
                        bank_read[7] = act(A.copy, qmT[off:off + 64, j, :], bank[7][off:off + 64, :], after=[t])
                        yield
                mem_free = [None, None]

                sel_at = [0, P, 3 * P, 6 * P]
                sel_ready = {}

                def choose_keys():
                    t = pool(G.tensor_copy, sel[:, 0:P], const("mask_limit"))
                    sel_ready[0] = t
                    best = small[:, 216:224]
                    score_free = None
                    for b in range(1, NT):
                        nk = (b + 1) * P
                        score = work[:, 0:nk]
                        for h in range(4):
                            j, off = h // 2, 64 * (h % 2)
                            pb = 5 + h % 2
                            rel = PT[:, (h % 2) * 512:(h % 2) * 512 + nk]
                            t = pe(T.matmul, bank[pb][:, 0:nk], tile(qiT[off:off + 64, j, :], b), kiT[off:off + 64, 0:nk],
                                   start=True, stop=True, after=[bank_read[pb]])
                            w = w_idx[:, 4 * b + h:4 * b + h + 1]
                            t = dve(V.tensor_scalar, score if h == 0 else rel, bank[pb][:, 0:nk], 0.0, w, ALU.max, ALU.mult,
                                    after=[t, mem_free, score_free])
                            bank_read[pb] = t
                            if h:
                                t = dve(V.tensor_tensor, score, score, rel, ALU.add, after=[t])
                            score_free = t
                        t = dve(V.tensor_tensor, score[:, nk - P:nk], score[:, nk - P:nk], const("mask_limit"), ALU.add, after=[t])
                        yield
                        for r in range(TOPK // 8):
                            t = dve(V.max, best, score, after=[t])
                            t = dve(V.match_replace, score, best, score, TAKEN, after=[t])
                            if r % 2:
                                yield
                        t = dve(V.tensor_scalar, sel[:, sel_at[b]:sel_at[b] + nk], score, 0.9 * TAKEN, NEG, ALU.is_gt, ALU.mult, after=[t])
                        score_free = t
                        sel_ready[b] = t

                def sparse_attention():
                    hank_free = bias_free = bias_ready = None
                    sum_free, w_free, pt_free = [None, None], [None, None], [None, None]
                    scaled, turned, with_bias = {}, {}, {}
                    jobs = [(h, b) for h in range(8) for b in range(NT)]

                    def head_bias(h):
                        nonlocal hank_free, bias_ready
                        src = bass.AP(scratch_bias.tensor, h * 640, [[1, P], [1, S]])
                        landed = pool.dma(G.dma_start, hank, src, counter(f"bias_landed{h % 2}"), after=[bias_stored[0], hank_free])
                        t = hank_free = pe(T.matmul, bank[6][:, :], const("exchange"), hank, start=True, stop=True, after=[landed, bank_read[6]])
                        bias_ready = bank_read[6] = act(A.copy, bias, bank[6][:, :], after=[t, bias_free])

                    def bias_with_mask(n):
                        nonlocal bias_free
                        h, b = jobs[n]
                        nk = (b + 1) * P
                        bias_free = pool(G.tensor_tensor, bias_sel[:, n % 2, 0:nk], bias[:, 512 - nk:512], sel[:, sel_at[b]:sel_at[b] + nk], ALU.add,
                                         after=[bias_ready, sum_free[n % 2], sel_ready[b]])
                        with_bias[n] = bias_free

                    def score(n):
                        h, b = jobs[n]
                        m, nk, off = n % 2, (b + 1) * P, 64 * (h % 2)
                        W = work[:, m * 512:m * 512 + nk]
                        nm, dn = small[:, 224 + 2 * m:225 + 2 * m], small[:, 225 + 2 * m:226 + 2 * m]
                        t = pe(T.matmul, bank[5][:, 0:nk], tile(qaT[off:off + 64, h // 2, :], b), kaT[off:off + 64, 0:nk],
                               start=True, stop=True, after=[bank_read[5]])
                        t = dve(V.scalar_tensor_tensor, W, bank[5][:, 0:nk], HD ** -0.5, bias_sel[:, m, 0:nk], ALU.mult, ALU.add,
                                after=[t, with_bias[n], w_free[m]])
                        bank_read[5] = sum_free[m] = t
                        t = dve(V.tensor_reduce, nm, W, AX.X, ALU.max, negate=True, after=[t])
                        scaled[n] = act(A.activation, W, W, ACT.Exp, bias=nm, accum_out=dn, after=[t])

                    def scale(n):
                        m, nk = n % 2, (jobs[n][1] + 1) * P
                        W, dn = work[:, m * 512:m * 512 + nk], small[:, 225 + 2 * m:226 + 2 * m]
                        t = dve(V.reciprocal, dn, dn, after=[scaled[n]])
                        scaled[n] = act(A.activation, W, W, ACT.Copy, scale=dn, after=[t])

                    def turn(n):
                        b, m = jobs[n][1], n % 2
                        for k in range(b + 1):
                            t = pe(T.transpose, tile(bank[6], k), tile(work[:, m * 512:], k), ident, after=[scaled[n], bank_read[6]], signal=(k == b))
                        w_free[m] = t
                        turned[n] = bank_read[6] = act(A.copy, PT[:, m * 512:m * 512 + (b + 1) * P], bank[6][:, 0:(b + 1) * P], after=[t, pt_free[m]])

                    def values(n):
                        h, b = jobs[n]
                        m, off = n % 2, 64 * (h % 2)
                        for k in range(b + 1):
                            t = pe(T.matmul, bank[7][off:off + 64, b * P:(b + 1) * P], proj_k[:, k, HD:2 * HD], tile(PT[:, m * 512:], k),
                                   start=(k == 0), stop=(k == b), after=[turned[n], bank_read[7]], signal=(k == b))
                        pt_free[m] = t
                        if b == NT - 1:
                            bank_read[7] = act(A.copy, qaT[off:off + 64, h // 2, :], bank[7][off:off + 64, :], after=[t])

                    N = len(jobs)
                    head_bias(0)
                    bias_with_mask(0)
                    yield
                    for n in range(N + 2):
                        if 1 <= n <= N:
                            scale(n - 1)
                        if n < N:
                            score(n)
                        if n + 1 < N:
                            if jobs[n + 1][1] == 0:
                                head_bias(jobs[n + 1][0])
                            bias_with_mask(n + 1)
                        yield
                        if 1 <= n <= N:
                            turn(n - 1)
                        if n >= 2:
                            values(n - 2)
                        yield

                def state_space():
                    x_free = y_done = None
                    yT = proj_u[:, 0:2, :]
                    for pair in range(8):
                        half, cc = pair // 4, pair % 4
                        rows = slice(32 * cc, 32 * cc + 32)
                        for comp in range(2):
                            b_pair = tile(param(("b_re", "b_im")[comp]), half)[rows, :]
                            t = pe(T.matmul, bank[4][:, :], b_pair, uT[rows, half, :], start=True, stop=True, after=[bank_read[4]])
                            bank_read[4] = act(A.copy, X[:, 0, comp, 256:], bank[4][:, :], after=[t, x_free, y_done])
                            yield
                        t = bank_read[4]
                        yield
                        for k in range(9):
                            src, dst = X[:, k % 2], X[:, (k + 1) % 2]
                            sh = 1 << k
                            r, i_, ni = [a[:, pair:pair + 1] for a in powers[k]]
                            now, past = slice(256, 256 + S), slice(256 - sh, 256 - sh + S)
                            ta = dve(V.scalar_tensor_tensor, dst[:, 0, now], src[:, 0, past], r, src[:, 0, now], ALU.mult, ALU.add, after=[t, x_free])
                            tb2 = dve(V.scalar_tensor_tensor, dst[:, 1, now], src[:, 1, past], r, src[:, 1, now], ALU.mult, ALU.add, after=[])
                            dve(V.scalar_tensor_tensor, dst[:, 0, now], src[:, 1, past], ni, dst[:, 0, now], ALU.mult, ALU.add, after=[ta])
                            t = dve(V.scalar_tensor_tensor, dst[:, 1, now], src[:, 0, past], i_, dst[:, 1, now], ALU.mult, ALU.add, after=[tb2])
                            yield
                        for comp in range(2):
                            c_pair = param(("c_re", "c_im")[comp])[:, 32 * pair:32 * pair + 32]
                            x_free = pe(T.matmul, bank[4][rows, :], c_pair, X[:, 1, comp, 256:], start=(comp == 0), stop=(comp == 1),
                                        after=[t, bank_read[4]])
                        yield
                        d_col = param("ssm_d", half)
                        y_done = dve(V.scalar_tensor_tensor, yT[rows, half, :], uT[rows, half, :], d_col[rows], bank[4][rows, :], ALU.mult, ALU.add, after=[x_free])
                        bank_read[4] = y_done
                        if cc == 3:
                            y, z = yT[:, half, :], X[:, 0, 0, 256:]
                            t = dve(V.tensor_tensor, z, y, y, ALU.mult, after=[y_done])
                            t = dve(V.tensor_scalar, z, z, 0.044715, 1.0, ALU.mult, ALU.add, after=[t])
                            t = dve(V.tensor_tensor, z, z, y, ALU.mult, after=[t])
                            yield
                            t = act(A.activation, z, z, ACT.Tanh, scale=math.sqrt(2 / math.pi), after=[t])
                            t = dve(V.scalar_tensor_tensor, y, z, 1.0, y, ALU.add, ALU.mult, after=[t])
                            y_done = t
                            pe_waits.append(t)
                        yield

                def heads_stream():
                    yield from memory_attention()
                    yield from choose_keys()
                    yield from turn_q()
                    yield from sparse_attention()

                def both(a, b):
                    live = [a, b]
                    while live:
                        for stream in list(live):
                            try:
                                next(stream)
                            except StopIteration:
                                live.remove(stream)
                        yield

                run(narrow(964, 512, proj_u))
                scan, u_turns = state_space(), turn_u()

                def turn_then_scan():
                    for _ in range(2):
                        next(u_turns)
                        yield
                    yield from both(u_turns, scan)
                interleave(narrow(512, 452, proj_k), turn_then_scan(), 1.5, finish=False)
                run(u_turns)
                interleave(narrow(0, 512, proj_q), both(turn_k(), scan), 1.0, finish=False)
                main = chain(*[feature_major(I["w_in"], 1476 + c * 512, gate_chunk(c)) for c in range(6)])
                interleave(main, both(heads_stream(), scan), HYBRID_RATIO)
                pe_wait_all()
                barrier()

                yT = proj_u[:, 0:2, :]
                carved[0] = 2 * NT * 512 + NT * 452 + 2 * S + 8 * S + 4 * S
                tanhs, folded, z2 = carve(8, S), carve(4, S), carve(2, S)
                merged = arena[:, NT * 512:NT * 512 + KC * S].rearrange("p (a b) -> p a b", a=KC)
                merge_tok = {}
                tanh_free = [None] * 8
                tanh_n = [0]

                def fetch(c):
                    got = []
                    for j in range(4):
                        m = tanh_n[0] % 8
                        tanh_n[0] += 1
                        landed = pool.dma(G.dma_start, tanhs[:, m, :], scratch_gates[4 * c + j], counter(f"tanh_landed{m}"), after=[tanh_free[m]])
                        got.append((m, landed))
                    return got

                def branch_out(w, src, K, branch):
                    for c in range(2):
                        got = fetch(2 * branch + c)

                        def merge(j, psum, token):
                            m, landed = got[j]
                            g, chunk = tanhs[:, m, :], 4 * c + j
                            if branch == 2:
                                t = dve(V.scalar_tensor_tensor, merged[:, chunk, :], g, 1.0, psum, ALU.add, ALU.mult, after=[token, landed])
                                merge_tok[chunk] = tanh_free[m] = t
                                return t
                            read = dve(V.scalar_tensor_tensor, g, g, 1.0, psum, ALU.add, ALU.mult, after=[token, landed])
                            t = dve(V.tensor_tensor, merged[:, chunk, :], merged[:, chunk, :], g, ALU.add, after=[read, merge_tok[chunk]])
                            merge_tok[chunk] = tanh_free[m] = t
                            return read
                        run(feature_major(w, c * 512, merge, src=(src,), K=K))
                branch_out(I["w_o_m"], qmT, 2, 2)
                branch_out(I["w_o_a"], qaT, 4, 0)
                for c in range(2):
                    got = fetch(2 + c)
                    fold_done = {}

                    def fold_sigmoid(j, psum, token):
                        m, landed = got[j]
                        z = z2[:, j % 2, :]
                        read = act(A.activation, z, psum, ACT.Tanh, scale=0.25, after=[token, z_free[j % 2]])
                        t = dve(V.tensor_scalar, z, z, 0.25, 0.25, ALU.mult, ALU.add, after=[read])
                        t = dve(V.scalar_tensor_tensor, folded[:, j, :], tanhs[:, m, :], 1.0, z, ALU.add, ALU.mult, after=[t, landed])
                        z_free[j % 2] = tanh_free[m] = fold_done[j] = t
                        return read

                    def merge_glu(j, psum, token):
                        chunk = 4 * c + j
                        read = dve(V.tensor_tensor, folded[:, j, :], folded[:, j, :], psum, ALU.mult, after=[token, fold_done[j]])
                        t = dve(V.tensor_tensor, merged[:, chunk, :], merged[:, chunk, :], folded[:, j, :], ALU.add, after=[read, merge_tok[chunk]])
                        pe_waits.append(put_parts(merged[:, chunk, :], xh[:, chunk, :], xl[:, chunk, :], t))
                        return read
                    z_free = [(dve.sem, dve.count)] * 2
                    run(feature_major(I["w_glu"], D + c * 512, fold_sigmoid, src=(yT,), K=2))
                    run(feature_major(I["w_glu"], c * 512, merge_glu, src=(yT,), K=2))
                pe_wait_all()
                low_part_on[0] = "pool"
                parts_ready[:] = [None] * NT
                x_ready = [None] * NT
                for c in range(2):
                    def add(i, psum, token):
                        dst = x[:, i, c * 512:(c + 1) * 512]
                        x_ready[i] = dve(V.scalar_tensor_tensor, dst, psum, 0.5, dst, ALU.mult, ALU.add, after=[token])
                        return x_ready[i]
                    run(token_major(I["w_out"], c * 512, 512, tile, add))
                return x_ready

            stored = counter("out_stored")

            def store(n, after):
                return act.dma(A.dma_start, out[n * P:(n + 1) * P, :], x[:, n, :], stored, after=after)

            def final_norm(x_ready):
                scale = [norm_scale(n, [x_ready[n], (act.sem, act.count)]) for n in range(NT)]
                for n in range(NT):
                    t = dve(V.scalar_tensor_tensor, x[:, n, :], x[:, n, :], norm_rstd[:, 4 + n:5 + n], gain_row[:, :], ALU.mult, ALU.mult,
                            after=[scale[n], gain_row_in[0]])
                    last = store(n, [t])
                act.wait(last)

            def store_all():
                act.wait([store(n, [(dve.sem, dve.count)]) for n in range(NT)][-1])

            def layers():
                norm_to_parts("pre1", [None] * NT)
                dilated_layer()
                finish_layer(I["dil_w_out"], "post0", "ffn1")
                if stop_after == "dilated":
                    return store_all()
                differential_layer()
                finish_layer(I["diff_w_out"], "post1", "mix")
                if stop_after == "diff":
                    return store_all()
                x_ready = feed_forward(I["ffn1_w_in"], I["ffn1_w_out"], before_hybrid())
                if stop_after == "ffn1":
                    return store_all()
                norm_to_parts("ffn2", x_ready)
                x_ready = hybrid()
                if stop_after == "hybrid":
                    return store_all()
                norm_to_parts("final", x_ready)
                final_norm(feed_forward(I["ffn2_w_in"], I["ffn2_w_out"]))

            layers()
            return pieces_used if plan is None else (pe, dve, act, pool, sp)

        plan = emit(None)
        queues = emit(plan)

        block = ctx.enter_context(nc.Block())

        @block.sync
        def _(eng):
            queues[4].run(eng)

        @block.tensor
        def _(eng):
            queues[0].run(eng)

        @block.vector
        def _(eng):
            queues[1].run(eng)

        @block.scalar
        def _(eng):
            queues[2].run(eng)

        @block.gpsimd
        def _(eng):
            queues[3].run(eng)


def shape_constants():
    c = np.zeros((P, N_CONSTS), np.float32)

    def put(name, value):
        a, b = CONSTS[name]
        c[:value.shape[0], a:b] = value

    put("ident", np.eye(P, dtype=np.float32))
    put("exchange", np.eye(P, dtype=np.float32)[::-1])
    freqs = np.float32(10000.0) ** (-np.arange(0, HD, 2, dtype=np.float32) / np.float32(HD))
    ang = np.arange(S, dtype=np.float32)[:, None] * freqs[None, :].astype(np.float32)
    f = np.arange(P) % 32
    put("cos", np.cos(ang).astype(np.float32).T[f])
    sign = np.where(np.arange(P) % HD < 32, -1.0, 1.0).astype(np.float32)
    put("sin", np.sin(ang).astype(np.float32).T[f] * sign[:, None])
    q, k = np.arange(P)[:, None], np.arange(P)[None, :]
    causal = np.where(k <= q, 0.0, NEG).astype(np.float32)
    kj = np.arange(2 * P)[None, :]
    dist = P + q - kj
    band = np.where((dist >= 0) & (dist <= P), 0.0, NEG).astype(np.float32)
    put("mask_first", np.concatenate([causal, band], 1))
    put("mask_band", np.concatenate([band, band], 1))
    put("mask_causal", np.concatenate([np.zeros((P, 384), np.float32), causal], 1))
    put("mask_16", np.where((k <= q) & (k // 32 == q // 32), 0.0, NEG).astype(np.float32))
    put("mask_limit", np.where((q < 64) & (k >= 64), NEG, 0.0).astype(np.float32))
    rel = np.arange(640) - 127 - 384
    half, exact = BUCKETS // 2, BUCKETS // 4
    n = np.abs(rel)
    nf = np.maximum(n, 1).astype(np.float32)
    large = exact + (np.log(nf / np.float32(exact)) / np.float32(math.log(128 / exact)) * np.float32(half - exact)).astype(np.int32)
    large = np.minimum(large, half - 1)
    bucket = np.where(rel > 0, half, 0) + np.where(n < exact, n, large)
    onehot = (np.arange(BUCKETS)[:, None] == bucket[None, :]).astype(np.float32)
    put("onehot", onehot)
    return c


def kernel(stop_after="", **inputs):
    import concourse.bacc as bacc
    from concourse.bass_utils import run_bass_kernel_spmd as run

    a = {k: np.asarray(v) for k, v in inputs.items()}
    params = np.zeros((P, N_PARAMS), np.float32)

    def put(name, value):
        lo, hi = PARAMS[name]
        params[:value.shape[0], lo:hi] = value

    chunks = lambda v: v.reshape(-1, P).T
    for name in ("a_q_gain", "a_k_gain", "m_q_gain", "m_k_gain"):
        put(name, np.concatenate([a[name + "_2"][0]] * 2)[:, None])
    put("lam_re", chunks(a["ssm_lambda_re_2"][0].reshape(-1)))
    put("lam_im", chunks(a["ssm_lambda_im_2"][0].reshape(-1)))
    put("log_dt", chunks(np.repeat(a["ssm_log_dt_2"][0], HD)))
    put("ssm_d", chunks(a["ssm_d_2"][0]))
    put("rel_bias", a["rel_bias_2"])

    def states(v):
        w = np.zeros((2, HD, 8, 2, 16), np.float32)
        for g in range(2):
            w[g, :, :, g, :] = v.reshape(8, 2, HD, 16)[:, g].transpose(1, 0, 2)
        return w.reshape(P, 256)
    put("b_re", states(a["ssm_b_re_2"][0].reshape(D, 16)))
    put("b_im", states(a["ssm_b_im_2"][0].reshape(D, 16)))
    put("c_re", states(a["ssm_c_re_2"][0].transpose(0, 2, 1).reshape(D, 16)))
    put("c_im", states(a["ssm_c_im_2"][0].transpose(0, 2, 1).reshape(D, 16)))
    rows = np.concatenate([a["norm_pre"][0], a["norm_post"][0], a["norm_pre"][1], a["norm_post"][1], a["ffn1_norm_2"][0],
                           a["mem_norm_2"][0], a["mix_norm_2"][0], a["ffn2_norm_2"][0], a["final_norm_2"][0], a["diff_subln"][0],
                           a["diff_lambda_q1"][0], a["diff_lambda_k1"][0], a["diff_lambda_q2"][0], a["diff_lambda_k2"][0]])[None]
    given = {"x": a["x"][0], "mem": a["mem_2"][0], "consts": shape_constants(), "params": params, "rows": rows,
             "dil_w_in": a["dil_w_in"][0], "dil_w_out": a["dil_w_out"][0],
             "diff_w_in": a["diff_w_in"][0], "diff_w_out": a["diff_w_out"][0]}
    for name in ("ffn1_w_in", "ffn1_w_out", "w_in", "w_o_a", "w_glu", "w_mem_kv", "w_o_m", "w_out", "ffn2_w_in", "ffn2_w_out"):
        given[name] = a[name + "_2"][0]

    nc = bacc.Bacc("TRN2", target_bir_lowering=False, num_devices=1)
    arrays, I = {}, {}
    for name, v in given.items():
        v = np.ascontiguousarray(v)
        arrays["in_" + name] = v
        I[name] = nc.dram_tensor("in_" + name, v.shape, F32, kind="ExternalInput").ap()
    out = nc.dram_tensor("out_0", (S, D), F32, kind="ExternalOutput").ap()
    program(nc, I, out, stop_after)
    result = run(nc, [arrays], core_ids=[0])
    return result.results[0]["out_0"].reshape(1, S, D)
```
